# Optimizing a Trainium2 kernel written in Bass

```python
import jax, jax.numpy as jnp
from jax import lax
import numpy as np

D_MODEL = 1024
BATCH = 1
SEQ = 512
DEPTH = 1

GRID_W = 64
CTX_LEN = 256
HG_HEADS = 4
HG_DK = 128
HG_DV = 128
HG_KEY = HG_HEADS * HG_DK
HG_VAL = HG_HEADS * HG_DV
HG_CHUNK = 64
ATT_HEADS = 8
ATT_KV_HEADS = 2
ATT_HEAD_DIM = 64
ATT_GROUPS = ATT_HEADS // ATT_KV_HEADS
ATT_Q = ATT_HEADS * ATT_HEAD_DIM
ATT_KV = ATT_KV_HEADS * ATT_HEAD_DIM
Q_BLOCK = 128
ROPE_AXIS_DIM = ATT_HEAD_DIM // 2
ROPE_THETA = 10000.0
N_EXPERTS = 16
EC_CAPACITY_FACTOR = 2
EXPERT_FF = 1024
IN_SPLITS = (HG_KEY, HG_KEY, HG_KEY, HG_VAL, HG_VAL, ATT_Q, ATT_KV, ATT_KV, D_MODEL, D_MODEL)
IN_COLS = 3 * HG_KEY + 2 * HG_VAL + ATT_Q + 2 * ATT_KV + 2 * D_MODEL
N_MOD = 6
NORM_EPS = 1e-6


def rms_norm(x, g):
    xf = x.astype(jnp.float32)
    y = xf * lax.rsqrt(jnp.mean(xf * xf, axis=-1, keepdims=True) + NORM_EPS)
    return (y * g.astype(jnp.float32)).astype(x.dtype)

def modulate(h, shift, scale):
    return h * (1 + scale) + shift

def adaln_params(cond, w_mod, b_mod):
    m = jax.nn.silu(cond) @ w_mod + b_mod
    return jnp.split(m[..., None, :], N_MOD, axis=-1)

def axial_rope_tables(length):
    rows = length // GRID_W
    row = jnp.repeat(jnp.arange(rows, dtype=jnp.float32), GRID_W)
    col = jnp.tile(jnp.arange(GRID_W, dtype=jnp.float32), rows)
    inv_freq = ROPE_THETA ** (-jnp.arange(0, ROPE_AXIS_DIM, 2, dtype=jnp.float32) / ROPE_AXIS_DIM)
    ang = jnp.concatenate([row[:, None] * inv_freq, col[:, None] * inv_freq], axis=-1)
    return jnp.cos(ang), jnp.sin(ang)

def apply_axial_rope(x, cos, sin):
    b_, length, h_, d = x.shape
    half = ROPE_AXIS_DIM // 2
    xs = x.astype(jnp.float32).reshape(b_, length, h_, 2, ROPE_AXIS_DIM)
    x1, x2 = xs[..., :half], xs[..., half:]
    c = cos.reshape(length, 1, 2, half)
    s = sin.reshape(length, 1, 2, half)
    out = jnp.concatenate([x1 * c - x2 * s, x2 * c + x1 * s], axis=-1)
    return out.reshape(b_, length, h_, d).astype(x.dtype)

def heads(a, n):
    return a.reshape(a.shape[0], a.shape[1], n, -1)

def hgrn_gates(f_pre, lb):
    f_pre = heads(f_pre.astype(jnp.float32), HG_HEADS)
    lb = lb.reshape(HG_HEADS, HG_DK)
    log_f = jnp.log(lb + (1 - lb) * jax.nn.sigmoid(f_pre))
    key = (1 - lb) * jax.nn.sigmoid(-f_pre)
    return key, log_f

def hgrn_chunk_scan(q, k, v, log_f, s0):
    b_, length, h_, _ = q.shape
    dv = v.shape[-1]
    n_chunks = length // HG_CHUNK

    def chunks(a):
        return a.astype(jnp.float32).reshape(b_, n_chunks, HG_CHUNK, h_, a.shape[-1]).transpose(1, 0, 3, 2, 4)

    incl = jnp.tril(jnp.ones((HG_CHUNK, HG_CHUNK), dtype=bool))[:, :, None]

    def step(state, inp):
        qc, kc, vc, fc = inp
        cum = jnp.cumsum(fc, axis=2)
        rel = jnp.where(incl, cum[:, :, :, None, :] - cum[:, :, None, :, :], -jnp.inf)
        scores = jnp.einsum("bhtk,bhsk,bhtsk->bhts", qc, kc, jnp.exp(rel))
        o = (jnp.einsum("bhts,bhsv->bhtv", scores, vc)
             + jnp.einsum("bhtk,bhkv->bhtv", qc * jnp.exp(cum), state))
        last = cum[:, :, -1:, :]
        new_state = (jnp.exp(last[:, :, 0, :, None]) * state
                     + jnp.einsum("bhsk,bhsv->bhkv", kc * jnp.exp(last - cum), vc))
        return new_state, o

    s_fin, o = lax.scan(step, s0.astype(jnp.float32), tuple(chunks(a) for a in (q, k, v, log_f)))
    o = o.transpose(1, 0, 3, 2, 4).reshape(b_, length, h_, dv)
    return o.astype(v.dtype), s_fin

def hgrn_bidir(q, i, k_f, lf_f, k_b, lf_b, s_f0, s_b0):
    o_f, s_f = hgrn_chunk_scan(q, k_f, i, lf_f, s_f0)
    flip = lambda a: a[:, ::-1]
    o_b, s_b = hgrn_chunk_scan(flip(q), flip(k_b), flip(i), flip(lf_b), s_b0)
    return o_f + flip(o_b), s_f, s_b

def attend_blocks(q, k, v):
    b_, lq = q.shape[:2]
    nb = lq // Q_BLOCK
    qb = q.reshape(b_, nb, Q_BLOCK, ATT_KV_HEADS, ATT_GROUPS, ATT_HEAD_DIM).transpose(1, 0, 2, 3, 4, 5)
    scale = ATT_HEAD_DIM ** -0.5

    def one_block(qi):
        s = jnp.einsum("bqhgd,bkhd->bhgqk", qi, k, preferred_element_type=jnp.float32) * scale
        p = jax.nn.softmax(s, axis=-1)
        return jnp.einsum("bhgqk,bkhd->bqhgd", p.astype(v.dtype), v)

    o = lax.map(one_block, qb)
    return o.transpose(1, 0, 2, 3, 4, 5).reshape(b_, lq, ATT_Q)

def token_mix(hx, hc, w_in, lb_f, lb_b, hg_norm_g, q_norm_g, k_norm_g,
              w_branch_a, w_branch_b, w_out, cos, sin, ctx_out):
    split_at = np.cumsum(IN_SPLITS)[:-1].tolist()

    def project(h):
        return jnp.split(h @ w_in, split_at, axis=-1)

    def qk_norm(aq, ak):
        return rms_norm(heads(aq, ATT_HEADS), q_norm_g), rms_norm(heads(ak, ATT_KV_HEADS), k_norm_g)

    def merge(o_hg, g_hg, o_att, ga, gb):
        b_, length = g_hg.shape[:2]
        a = (rms_norm(o_hg, hg_norm_g.reshape(HG_HEADS, HG_DV)).reshape(b_, length, HG_VAL)
             * jax.nn.silu(g_hg)) @ w_branch_a
        bb = o_att @ w_branch_b
        return (jax.nn.sigmoid(ga) * a + jax.nn.sigmoid(gb) * bb) @ w_out

    cq, cff, cfb, ci, cg, caq, cak, cav, cga, cgb = project(hc)
    ckf, clf = hgrn_gates(cff, lb_f)
    ckb, clb = hgrn_gates(cfb, lb_b)
    zeros = jnp.zeros((hc.shape[0], HG_HEADS, HG_DK, HG_DV), jnp.float32)
    co, cs_f, cs_b = hgrn_bidir(heads(cq, HG_HEADS), heads(ci, HG_HEADS), ckf, clf, ckb, clb, zeros, zeros)
    cqa, cka = qk_norm(caq, cak)
    cva = heads(cav, ATT_KV_HEADS)

    xq, xff, xfb, xi, xg, xaq, xak, xav, xga, xgb = project(hx)
    xkf, xlf = hgrn_gates(xff, lb_f)
    xkb, xlb = hgrn_gates(xfb, lb_b)
    xo, _, _ = hgrn_bidir(heads(xq, HG_HEADS), heads(xi, HG_HEADS), xkf, xlf, xkb, xlb, cs_f, cs_b)
    xqa, xka = qk_norm(xaq, xak)
    xqa = apply_axial_rope(xqa, cos, sin)
    xka = apply_axial_rope(xka, cos, sin)
    keys = jnp.concatenate([cka, xka], axis=1)
    vals = jnp.concatenate([cva, heads(xav, ATT_KV_HEADS)], axis=1)
    y_x = merge(xo, xg, attend_blocks(xqa, keys, vals), xga, xgb)
    if not ctx_out:
        return y_x, None
    y_c = merge(co, cg, attend_blocks(cqa, cka, cva), cga, cgb)
    return y_x, y_c

def expert_choice_moe(h, w_router, w_gate, w_up, w_down):
    b_, length, _ = h.shape
    cap = EC_CAPACITY_FACTOR * length // N_EXPERTS
    aff = jax.nn.softmax((h @ w_router).astype(jnp.float32), axis=-1)
    gate, idx = lax.top_k(jnp.swapaxes(aff, 1, 2), cap)
    bidx = jnp.arange(b_)[:, None, None]
    xe = h[bidx, idx]
    hid = jax.nn.silu(jnp.einsum("becd,edf->becf", xe, w_gate)) * jnp.einsum("becd,edf->becf", xe, w_up)
    ye = jnp.einsum("becf,efd->becd", hid, w_down) * gate[..., None].astype(h.dtype)
    return jnp.zeros_like(h).at[bidx, idx].add(ye)

def first_inputs(seed: int = 0) -> dict:
    key = jax.random.key(seed)
    ks = jax.random.split(key, 24)
    n = jax.random.normal
    f32 = jnp.float32
    d = D_MODEL
    return {
        "x": n(ks[0], (BATCH, SEQ, d), f32),
        "c": n(ks[1], (BATCH, d), f32),
        "ctx": n(ks[2], (BATCH, CTX_LEN, d), f32),
        "c_ctx": n(ks[3], (d,), f32),
        "w_mod": n(ks[4], (DEPTH, d, N_MOD * d), f32) * (0.5 * d ** -0.5),
        "b_mod": n(ks[5], (DEPTH, N_MOD * d), f32) * 0.02,
        "norm1_g": 1.0 + 0.1 * n(ks[6], (DEPTH, d), f32),
        "norm2_g": 1.0 + 0.1 * n(ks[7], (DEPTH, d), f32),
        "w_in": n(ks[8], (DEPTH, d, IN_COLS), f32) * d ** -0.5,
        "hg_lb_logits": 0.5 * n(ks[9], (2, DEPTH + 1, HG_KEY), f32),
        "hg_norm_g": 1.0 + 0.1 * n(ks[10], (DEPTH, HG_VAL), f32),
        "q_norm_g": 1.0 + 0.1 * n(ks[11], (DEPTH, ATT_HEAD_DIM), f32),
        "k_norm_g": 1.0 + 0.1 * n(ks[12], (DEPTH, ATT_HEAD_DIM), f32),
        "w_branch_a": n(ks[13], (DEPTH, HG_VAL, d), f32) * HG_VAL ** -0.5,
        "w_branch_b": n(ks[14], (DEPTH, ATT_Q, d), f32) * ATT_Q ** -0.5,
        "w_out": n(ks[15], (DEPTH, d, d), f32) * d ** -0.5,
        "w_router": n(ks[16], (DEPTH, d, N_EXPERTS), f32) * d ** -0.5,
        "w_exp_gate": n(ks[17], (DEPTH, N_EXPERTS, d, EXPERT_FF), f32) * d ** -0.5,
        "w_exp_up": n(ks[18], (DEPTH, N_EXPERTS, d, EXPERT_FF), f32) * d ** -0.5,
        "w_exp_down": n(ks[19], (DEPTH, N_EXPERTS, EXPERT_FF, d), f32) * EXPERT_FF ** -0.5,
        "final_norm_g": 1.0 + 0.1 * n(ks[20], (d,), f32),
    }

def first_block(x, c, ctx, c_ctx, w_mod, b_mod, norm1_g, norm2_g, w_in, hg_lb_logits, hg_norm_g,
              q_norm_g, k_norm_g, w_branch_a, w_branch_b, w_out, w_router, w_exp_gate, w_exp_up,
              w_exp_down, final_norm_g):
    cos, sin = axial_rope_tables(x.shape[1])
    lb_all = jnp.cumsum(jax.nn.softmax(hg_lb_logits.astype(jnp.float32), axis=1), axis=1)
    for l in range(DEPTH):
        last = l == DEPTH - 1
        sh1, sc1, g1, sh2, sc2, g2 = adaln_params(c, w_mod[l], b_mod[l])
        csh1, csc1, cg1, csh2, csc2, cg2 = adaln_params(c_ctx, w_mod[l], b_mod[l])
        hx = modulate(rms_norm(x, norm1_g[l]), sh1, sc1)
        hc = modulate(rms_norm(ctx, norm1_g[l]), csh1, csc1)
        y_x, y_c = token_mix(hx, hc, w_in[l], lb_all[0, l], lb_all[1, l], hg_norm_g[l], q_norm_g[l],
                             k_norm_g[l], w_branch_a[l], w_branch_b[l], w_out[l], cos, sin, not last)
        x = x + g1 * y_x
        x = x + g2 * expert_choice_moe(modulate(rms_norm(x, norm2_g[l]), sh2, sc2),
                                       w_router[l], w_exp_gate[l], w_exp_up[l], w_exp_down[l])
        if not last:
            ctx = ctx + cg1 * y_c
            ctx = ctx + cg2 * expert_choice_moe(modulate(rms_norm(ctx, norm2_g[l]), csh2, csc2),
                                                w_router[l], w_exp_gate[l], w_exp_up[l], w_exp_down[l])
    return rms_norm(x, final_norm_g)


HEAD_DIM = 64
N_ATTN_HEADS = 8
N_KV_GROUPS = 2
HEADS_PER_GROUP = N_ATTN_HEADS // N_KV_GROUPS
ATTN_WIDTH = N_ATTN_HEADS * HEAD_DIM
CONV_WIDTH = D_MODEL - ATTN_WIDTH
KV_WIDTH = N_KV_GROUPS * HEAD_DIM
N_BRANCH = 3
CMP_BLOCK = 32
CMP_STRIDE = 16
CMP_HIDDEN = 4 * HEAD_DIM
SEL_BLOCK = 64
SEL_TOPK = 16
WINDOW = 512
CONV_K = 3
D_FF = 4 * D_MODEL
IN_WIDTH = ATTN_WIDTH + 6 * KV_WIDTH + N_BRANCH * N_ATTN_HEADS + 3 * CONV_WIDTH
EPS = 1e-6
NEG = -1e30
FORCE_BONUS = 1e4


def rms_norm_2(x, g):
    xf = x.astype(jnp.float32)
    y = xf * lax.rsqrt(jnp.mean(xf * xf, axis=-1, keepdims=True) + EPS)
    return (y * g.astype(jnp.float32)).astype(x.dtype)

def alibi_slopes():
    h = np.arange(1, N_ATTN_HEADS + 1, dtype=np.float32)
    s = np.power(np.float32(2.0), -8.0 * h / N_ATTN_HEADS).astype(np.float32)
    return jnp.asarray(s, dtype=jnp.float32).reshape(N_KV_GROUPS, HEADS_PER_GROUP)

def masked_softmax(s, mask):
    s = jnp.where(mask, s, NEG)
    m = jnp.max(s, axis=-1, keepdims=True)
    p = jnp.where(mask, jnp.exp(s - m), 0.0)
    return p / jnp.maximum(jnp.sum(p, axis=-1, keepdims=True), 1e-30)

def cmp_to_sel_matrix(n_cmp, n_sel):
    s0 = jnp.arange(n_cmp)[:, None] * CMP_STRIDE
    s1 = jnp.arange(n_sel)[None, :] * SEL_BLOCK
    shared = jnp.clip(jnp.minimum(s0 + CMP_BLOCK, s1 + SEL_BLOCK) - jnp.maximum(s0, s1), 0, None)
    return shared.astype(jnp.float32) / CMP_BLOCK

def compress(k_raw, pe, w1, b1, w2, b2):
    B, T = k_raw.shape[0], k_raw.shape[1]
    ch = k_raw.reshape(B, T // CMP_STRIDE, CMP_STRIDE, N_KV_GROUPS, HEAD_DIM)
    blk = jnp.concatenate([ch[:, :-1], ch[:, 1:]], axis=2)
    blk = blk + pe[None, None, :, None, :]
    blk = blk.transpose(0, 3, 1, 2, 4).reshape(B, N_KV_GROUPS, -1, CMP_BLOCK * HEAD_DIM)
    hdn = jax.nn.gelu(blk @ w1 + b1)
    return hdn @ w2 + b2

def nsa_attention(q, k_cmp, v_cmp, k_slc, v_slc, k_win, v_win, gates):
    B, T = q.shape[0], q.shape[1]
    G, R, hd = N_KV_GROUPS, HEADS_PER_GROUP, HEAD_DIM
    f32 = jnp.float32
    n_cmp = k_cmp.shape[2]
    n_sel = T // SEL_BLOCK
    n_top = min(SEL_TOPK, n_sel)
    n_qb = T // Q_BLOCK
    slopes = alibi_slopes()[None, :, :, None, None]
    sel_map = cmp_to_sel_matrix(n_cmp, n_sel)
    cmp_end = jnp.arange(n_cmp, dtype=jnp.int32) * CMP_STRIDE + (CMP_BLOCK - 1)
    sel_id = jnp.arange(n_sel, dtype=jnp.int32)
    sel_off = jnp.arange(SEL_BLOCK, dtype=jnp.int32)
    win_off = jnp.arange(Q_BLOCK + WINDOW, dtype=jnp.int32) - WINDOW
    ks_blk = k_slc.reshape(B, n_sel, SEL_BLOCK, G, hd).transpose(0, 3, 1, 2, 4)
    vs_blk = v_slc.reshape(B, n_sel, SEL_BLOCK, G, hd).transpose(0, 3, 1, 2, 4)
    kw_pad = jnp.pad(k_win, ((0, 0), (WINDOW, 0), (0, 0), (0, 0)))
    vw_pad = jnp.pad(v_win, ((0, 0), (WINDOW, 0), (0, 0), (0, 0)))
    q_blocks = (q * (hd ** -0.5)).reshape(B, n_qb, Q_BLOCK, G, R, hd).transpose(1, 0, 3, 4, 2, 5)
    g_blocks = gates.reshape(B, n_qb, Q_BLOCK, G, R, N_BRANCH).transpose(1, 0, 3, 4, 2, 5)
    b_ix = jnp.arange(B)[:, None, None, None]
    g_ix = jnp.arange(G)[None, :, None, None]

    def one_block(args):
        c, qb, gb = args
        q0 = c * Q_BLOCK
        t = q0 + jnp.arange(Q_BLOCK, dtype=jnp.int32)
        s = jnp.einsum('bgrqd,bgid->bgrqi', qb, k_cmp).astype(f32)
        dist = (t[:, None] - cmp_end[None, :]).astype(f32)
        p_cmp = masked_softmax(s - slopes * dist, dist >= 0)
        o_cmp = jnp.einsum('bgrqi,bgid->bgrqd', p_cmp.astype(v_cmp.dtype), v_cmp)
        imp = jnp.einsum('bgrqi,ij->bgqj', p_cmp, sel_map)
        jt = (t // SEL_BLOCK)[:, None]
        forced = (sel_id == 0) | (sel_id == jt) | (sel_id == jt - 1)
        valid = sel_id * SEL_BLOCK <= t[:, None]
        imp = jnp.where(valid, jnp.where(forced, imp + FORCE_BONUS, imp), NEG)
        _, idx = lax.top_k(imp, n_top)
        kg = ks_blk[b_ix, g_ix, idx].reshape(B, G, Q_BLOCK, n_top * SEL_BLOCK, hd)
        vg = vs_blk[b_ix, g_ix, idx].reshape(B, G, Q_BLOCK, n_top * SEL_BLOCK, hd)
        pos = (idx[..., None] * SEL_BLOCK + sel_off).reshape(B, G, Q_BLOCK, n_top * SEL_BLOCK)
        dist = (t[None, None, :, None] - pos).astype(f32)[:, :, None]
        s = jnp.einsum('bgrqd,bgqmd->bgrqm', qb, kg).astype(f32)
        p_slc = masked_softmax(s - slopes * dist, dist >= 0)
        o_slc = jnp.einsum('bgrqm,bgqmd->bgrqd', p_slc.astype(vg.dtype), vg)
        kw = lax.dynamic_slice_in_dim(kw_pad, q0, Q_BLOCK + WINDOW, axis=1)
        vw = lax.dynamic_slice_in_dim(vw_pad, q0, Q_BLOCK + WINDOW, axis=1)
        spos = q0 + win_off
        dist_i = t[:, None] - spos[None, :]
        mask = (spos[None, :] >= 0) & (dist_i >= 0) & (dist_i < WINDOW)
        s = jnp.einsum('bgrqd,bsgd->bgrqs', qb, kw).astype(f32)
        p_win = masked_softmax(s - slopes * dist_i.astype(f32), mask)
        o_win = jnp.einsum('bgrqs,bsgd->bgrqd', p_win.astype(vw.dtype), vw)
        o = gb[..., 0:1] * o_cmp + gb[..., 1:2] * o_slc + gb[..., 2:3] * o_win
        return o.astype(q.dtype)

    out = lax.map(one_block, (jnp.arange(n_qb, dtype=jnp.int32), q_blocks, g_blocks))
    return out.transpose(1, 0, 4, 2, 3, 5).reshape(B, T, N_ATTN_HEADS * hd)

def short_conv_mixer(h, c_gate, b_gate, conv_w):
    u = c_gate * h
    v = lax.conv_general_dilated(u, conv_w[:, None, :], window_strides=(1,),
                                 padding=((CONV_K - 1, 0),),
                                 dimension_numbers=('NWC', 'WIO', 'NWC'),
                                 feature_group_count=CONV_WIDTH)
    return b_gate * v

def second_inputs(seed: int = 0) -> dict:
    key = jax.random.key(seed)
    ks = jax.random.split(key, 16)
    f32 = jnp.float32

    def nrm(k, shape, scale):
        return jax.random.normal(k, shape, f32) * scale

    return {
        'x': nrm(ks[0], (BATCH, SEQ, D_MODEL), 1.0),
        'g_mix_norm': 1.0 + nrm(ks[1], (DEPTH, D_MODEL), 0.02),
        'w_in': nrm(ks[2], (DEPTH, D_MODEL, IN_WIDTH), D_MODEL ** -0.5),
        'g_q': 1.0 + nrm(ks[3], (DEPTH, HEAD_DIM), 0.02),
        'g_k': 1.0 + nrm(ks[4], (DEPTH, N_BRANCH, HEAD_DIM), 0.02),
        'pe_cmp': nrm(ks[5], (DEPTH, 2, CMP_BLOCK, HEAD_DIM), 0.1),
        'w_cmp1': nrm(ks[6], (DEPTH, 2, CMP_BLOCK * HEAD_DIM, CMP_HIDDEN), (CMP_BLOCK * HEAD_DIM) ** -0.5),
        'b_cmp1': nrm(ks[7], (DEPTH, 2, CMP_HIDDEN), 0.01),
        'w_cmp2': nrm(ks[8], (DEPTH, 2, CMP_HIDDEN, HEAD_DIM), CMP_HIDDEN ** -0.5),
        'b_cmp2': nrm(ks[9], (DEPTH, 2, HEAD_DIM), 0.01),
        'conv_w': nrm(ks[10], (DEPTH, CONV_K, CONV_WIDTH), CONV_K ** -0.5),
        'g_out': 1.0 + nrm(ks[11], (DEPTH, D_MODEL), 0.02),
        'w_o': nrm(ks[12], (DEPTH, D_MODEL, D_MODEL), (2 * DEPTH * D_MODEL) ** -0.5),
        'g_ffn_norm': 1.0 + nrm(ks[13], (DEPTH, D_MODEL), 0.02),
        'w_up': nrm(ks[14], (DEPTH, D_MODEL, D_FF), D_MODEL ** -0.5),
        'w_down': nrm(ks[15], (DEPTH, D_FF, D_MODEL), (2 * DEPTH * D_FF) ** -0.5),
    }

def second_block(x, g_mix_norm, w_in, g_q, g_k, pe_cmp, w_cmp1, b_cmp1, w_cmp2, b_cmp2,
              conv_w, g_out, w_o, g_ffn_norm, w_up, w_down):
    B, T = x.shape[0], x.shape[1]
    sizes = [ATTN_WIDTH] + [KV_WIDTH] * 6 + [N_BRANCH * N_ATTN_HEADS] + [CONV_WIDTH] * 3
    offs = [int(o) for o in np.cumsum(sizes)[:-1]]
    kv_shape = (B, T, N_KV_GROUPS, HEAD_DIM)
    for l in range(DEPTH):
        h = rms_norm_2(x, g_mix_norm[l])
        z = h @ w_in[l]
        q, kc, vc, ks_, vs_, kw_, vw_, gl, hc, cg, bg = jnp.split(z, offs, axis=-1)
        q = rms_norm_2(q.reshape(B, T, N_ATTN_HEADS, HEAD_DIM), g_q[l])
        k_cmp = rms_norm_2(compress(kc.reshape(kv_shape), pe_cmp[l, 0], w_cmp1[l, 0], b_cmp1[l, 0],
                                  w_cmp2[l, 0], b_cmp2[l, 0]), g_k[l, 0])
        v_cmp = compress(vc.reshape(kv_shape), pe_cmp[l, 1], w_cmp1[l, 1], b_cmp1[l, 1],
                         w_cmp2[l, 1], b_cmp2[l, 1])
        k_slc = rms_norm_2(ks_.reshape(kv_shape), g_k[l, 1])
        k_win = rms_norm_2(kw_.reshape(kv_shape), g_k[l, 2])
        gates = jax.nn.sigmoid(gl).reshape(B, T, N_ATTN_HEADS, N_BRANCH)
        attn_out = nsa_attention(q, k_cmp, v_cmp, k_slc, vs_.reshape(kv_shape),
                                 k_win, vw_.reshape(kv_shape), gates)
        conv_out = short_conv_mixer(hc, cg, bg, conv_w[l])
        mixed = jnp.concatenate([rms_norm_2(attn_out, g_out[l, :ATTN_WIDTH]),
                                 rms_norm_2(conv_out, g_out[l, ATTN_WIDTH:])], axis=-1)
        x = x + mixed @ w_o[l]
        h = rms_norm_2(x, g_ffn_norm[l])
        x = x + jnp.square(jax.nn.relu(h @ w_up[l])) @ w_down[l]
    return x


def setup_inputs(seed=0):
    out = dict(first_inputs(seed))
    for name, value in second_inputs(seed + 1).items():
        if name != "x":
            out[name + "_2"] = value
    return out


def reference(
    x, c, ctx, c_ctx, w_mod, b_mod, norm1_g, norm2_g, w_in, hg_lb_logits, hg_norm_g, q_norm_g,
    k_norm_g, w_branch_a, w_branch_b, w_out, w_router, w_exp_gate, w_exp_up, w_exp_down,
    final_norm_g, g_mix_norm_2, w_in_2, g_q_2, g_k_2, pe_cmp_2, w_cmp1_2, b_cmp1_2, w_cmp2_2,
    b_cmp2_2, conv_w_2, g_out_2, w_o_2, g_ffn_norm_2, w_up_2, w_down_2,
):
    x = first_block(
        x, c, ctx, c_ctx, w_mod, b_mod, norm1_g, norm2_g, w_in, hg_lb_logits, hg_norm_g,
        q_norm_g, k_norm_g, w_branch_a, w_branch_b, w_out, w_router, w_exp_gate, w_exp_up,
        w_exp_down, final_norm_g,
    )
    return second_block(
        x, g_mix_norm_2, w_in_2, g_q_2, g_k_2, pe_cmp_2, w_cmp1_2, b_cmp1_2, w_cmp2_2, b_cmp2_2,
        conv_w_2, g_out_2, w_o_2, g_ffn_norm_2, w_up_2, w_down_2,
    )


_drawn_inputs = setup_inputs


def setup_inputs(seed=0):
    import zlib

    import numpy as np

    out = dict(_drawn_inputs(seed))
    spreads = {}
    factors = {'ctx': 4.917,
     'b_mod': 3.23,
     'hg_norm_g': 3.653,
     'q_norm_g': 8.0,
     'k_norm_g': 8.0,
     'g_mix_norm_2': 3.026,
     'g_q_2': 8.0,
     'g_k_2': 8.0,
     'b_cmp1_2': 8.0,
     'b_cmp2_2': 30.916,
     'g_out_2': 4.507,
     'g_ffn_norm_2': 4.195}
    for name, (base, spread) in spreads.items():
        noise = np.random.default_rng([zlib.crc32(name.encode()), seed]).standard_normal(out[name].shape)
        drawn = base * np.exp(spread * noise) if base else spread * noise
        out[name] = __import__('jax').numpy.asarray(drawn.astype(out[name].dtype))
    for name, factor in factors.items():
        out[name] = (out[name] * factor).astype(out[name].dtype)
    return out
```

```python
from contextlib import ExitStack

import numpy as np

import concourse.bass as bass
from concourse import mybir

F32 = mybir.dt.float32
BF16 = mybir.dt.bfloat16
U8 = mybir.dt.uint8
U32 = mybir.dt.uint32
ALU = mybir.AluOpType
ACT = mybir.ActivationFunctionType
AX = mybir.AxisListType.X

STAGE = 99
NS = 8
LEVELS = [64, 32, 16, 8, 4, 2, 1]
EPS = 1e-6


class Queue:

    def __init__(self, eng, sem, chain):
        self.eng, self.sem, self.chain, self.n, self.seen = eng, sem, chain, 0, {}

    def wait(self, *tokens):
        for t in tokens:
            if t is not None and self.seen.get(t[0].name, 0) < t[1]:
                self.seen[t[0].name] = t[1]
                self.eng.wait_ge(t[0], t[1])

    def __call__(self, fn, *tokens):
        self.wait(*tokens)
        if self.chain and self.n:
            self.wait((self.sem, self.n))
        fn(self.eng).then_inc(self.sem, 1)
        self.n += 1
        return (self.sem, self.n)

    @property
    def last(self):
        return (self.sem, self.n) if self.n else None


def program(nc, d, out):
    with ExitStack() as ctx:
        def sem(name):
            return ctx.enter_context(nc.semaphore(name))

        class Region:

            def __init__(self, lo, hi):
                self.lo, self.at, self.hi = lo, lo, hi

            def take(self, shape, dt):
                size = mybir.dt.size(dt)
                count = int(np.prod(shape[1:]))
                words = -(-count * size // 4)
                assert self.at + words <= self.hi, (shape, self.at, self.hi)
                a = arena[0:shape[0], self.at:self.at + words]
                self.at += words
                if dt != F32:
                    a = a.bitcast(dt)
                if len(shape) > 2:
                    names = "abcdef"[:len(shape) - 1]
                    a = a.rearrange(f"p ({' '.join(names)}) -> p {' '.join(names)}", **dict(zip(names, shape[1:])))
                return a

        NA = 28280
        arena = ctx.enter_context(nc.sbuf_tensor("arena", [128, NA], F32))
        TOP = NA - 5632

        def sb(name, shape, dt=F32, at=None):
            if at is None:
                return ctx.enter_context(nc.sbuf_tensor(name, shape, dt))
            return at.take(shape, dt)

        V = Queue(nc.vector, sem("s_v"), True)
        A = Queue(nc.scalar, sem("s_a"), True)
        G = Queue(nc.gpsimd, sem("s_g"), True)
        PE = Queue(nc.tensor, sem("s_pe"), False)
        SP = Queue(nc.sync, sem("s_sp"), False)

        PS = ctx.enter_context(nc.psum_tensor("PS", [128, 8 * 512], F32))

        class Banks:

            def __init__(self):
                self.rel, self.at = [None] * 8, 0

            def take(self, n=1):
                if self.at + n > 8:
                    self.at = 0
                b = self.at
                self.at = (b + n) % 8
                for i in range(b, b + n):
                    assert self.rel[i] != "held", "bank still held"
                    PE.wait(self.rel[i])
                    self.rel[i] = "held"
                return PS[:, b * 512:(b + n) * 512], (b, n)

            def free(self, key, tok):
                for i in range(key[0], key[0] + key[1]):
                    self.rel[i] = tok

        banks = Banks()

        def dma(q, dst, src, s, *tokens):
            q.wait(*tokens)
            q.eng.dma_start(dst, src).then_inc(s, 16)
            return (s, 16)

        ring = sb("ring", [128, NS, 2048])
        slot_sem = [sem(f"s_w{i}") for i in range(NS)]

        def cols(w, a, n):
            return (w[:, a:a + n].rearrange("(k p) n -> p k n", p=128), w.shape[0] // 128, n)

        units = [cols(d["w_mod"], 512 * j, 512) for j in range(4)]
        units += [cols(d["w_in"], 2560, 512), cols(d["w_in"], 3072, 256)]
        units += [cols(d["w_in"], a, 512) for a in (512, 0, 1536, 1024)]
        units += [cols(d["w_mod"], 512 * j, 512) for j in range(4, 12)]
        units += [cols(d["w_in"], 2048, 512)]
        for a, wb in ((3328, "w_branch_a"), (4352, "w_branch_b")):
            units += [cols(d[wb], 0, 1024), cols(d["w_in"], a, 512), cols(d["w_in"], a + 512, 512)]
        units += [cols(d["w_out"], 0, 512), cols(d["w_out"], 512, 512)]
        for p in range(8):
            for name in ("w_exp_gate", "w_exp_up", "w_exp_down"):
                for hf in range(2):
                    for kh in range(2):
                        units += [cols(d[name][2 * p + e2][512 * kh:512 * kh + 512, :], 512 * hf, 512)
                                  for e2 in range(2)]
        w2 = d["w_in_2"]
        units += [cols(w2, 512, 512), cols(w2, 0, 512), cols(w2, 1024, 280)]
        units += [cols(d["w_cmp1_2"][0], 0, 256), cols(d["w_cmp1_2"][1], 0, 256)]
        units += [cols(w2, 1304, 512), cols(w2, 1816, 512), cols(w2, 2328, 512)]
        units += [cols(d["w_o_2"], 0, 512), cols(d["w_o_2"], 512, 512)]
        units += [cols(d["w_up_2"], 512 * j, 512) for j in range(8)]
        units += [cols(d["w_down_2"][512 * j:512 * j + 512, :], 0, 1024) for j in range(8)]

        class Stream:

            def __init__(self):
                self.loaded, self.got, self.freed = 0, 0, 0
                self.pos, at = [], 0
                for _, k, n in units:
                    self.pos.append(at)
                    at += 1 if k * n <= 2048 and k == 4 else 2
                self.pos.append(at)
                self.count, self.need = [0] * NS, []
                for i in range(len(units)):
                    s = self.pos[i] % NS
                    self.count[s] += 16
                    self.need.append((slot_sem[s], self.count[s]))

            def load(self, tok=None):
                read = self.pos[self.freed]
                while self.loaded < len(units) and self.pos[self.loaded + 1] - NS <= read:
                    i = self.loaded
                    SP.wait(tok)
                    nc.sync.dma_start(self.view(i), units[i][0]).then_inc(self.need[i][0], 16)
                    self.loaded += 1

            def view(self, i):
                _, k, n = units[i]
                a = ring[:, :, :].rearrange("p s n -> p (s n)")
                o = self.pos[i] % NS * 2048
                return a[:, o:o + k * n].rearrange("p (k n) -> p k n", k=k)

            def get(self):
                i = self.got
                assert i < self.loaded
                PE.wait(self.need[i])
                self.got += 1
                return self.view(i)

            def done(self, n=None):
                self.freed = self.got if n is None else self.freed + n
                self.load(PE.last)

        W = Stream()

        ident = sb("ident", [128, 128])
        ones = sb("ones", [128, 128])
        rows = sb("rows", [128, 2, 128])
        colA = sb("colA", [128, 128])
        colB = sb("colB", [128, 64])
        gb = sb("gb", [128, 8, 64])
        masks = sb("masks", [128, 14, 128], U8)
        small = [sem(f"s_c{i}") for i in range(8)]
        s_rows, s_gb = sem("s_rows"), sem("s_gb")
        t_ones = V(lambda e: e.memset(ones[:, :], 1.0))
        t_rows0 = V(lambda e: e.memset(rows[:, :, :], 0.0))
        n = 0
        for t, name, k in ((0, "c", 8), (0, "c_ctx", 8), (0, "norm1_g", 8), (0, "norm2_g", 8), (0, "final_norm_g", 8),
                           (0, "g_mix_norm_2", 8), (0, "g_out_2", 8), (0, "g_ffn_norm_2", 8), (0, "b_mod", 48),
                           (0, "hg_norm_g", 4), (1, "hg_lb_logits", 16), (1, "conv_w_2", 12), (1, "b_cmp1_2", 4),
                           (1, "pe_cmp_2", 32)):
            if n == 10:
                at = 0
            at = 0 if n == 0 else at
            A.wait(t_rows0)
            nc.scalar.dma_start(rows[at:at + k, t, :], d[name].rearrange("(r p) -> r p", p=128)).then_inc(s_rows, 16)
            at += k
            n += 1
        t_rows = (s_rows, 16 * n)
        t_ident = dma(A, ident[:, :], d["k_ident"], small[0])
        ngb = 0
        for i, (name, o) in enumerate((("q_norm_g", 0), ("k_norm_g", 0), ("g_q_2", 0), ("g_k_2", 0), ("g_k_2", 64),
                                       ("g_k_2", 128), ("b_cmp2_2", 0), ("b_cmp2_2", 64))):
            nc.scalar.dma_start(gb[:, i, :], d[name][o:o + 64].partition_broadcast(128)).then_inc(s_gb, 16)
            ngb += 1
        t_gb = (s_gb, 16 * ngb)
        mstage = sb("mstage", [128, 14, 128], at=Region(8192, NA))
        t_mst = dma(A, mstage, d["k_masks"], small[1])

        PE.wait(t_ident, t_rows)

        def transpose(dst, src, k=128):
            return nc.tensor.transpose(dst, src, ident[0:k, 0:k])

        bk, key = banks.take()
        transpose(bk[:, 0:128], rows[:, 0, :])
        tk = PE(lambda e: transpose(bk[:, 128:192], rows[0:64, 1, :], 64))
        V(lambda e: e.tensor_copy(colA[:, :], bk[:, 0:128]), tk)
        t_col = V(lambda e: e.tensor_copy(colB[:, :], bk[:, 128:192]))
        banks.free(key, t_col)
        t_masks = V(lambda e: e.tensor_copy(masks[:, :, :], mstage), t_mst)
        W.load()

        sil = sb("sil", [128, 2, 8])
        modc = sb("modc", [128, 48, 2])
        AB = sb("AB", [128, 3, 8])
        cc = colA[:, 0:16].rearrange("p (s k) -> p s k", s=2)
        tk = A(lambda e: e.activation(sil[:, :, :], cc, ACT.Sigmoid), t_col)
        t_sil = V(lambda e: e.tensor_tensor(sil[:, :, :], sil[:, :, :], cc, ALU.mult), tk)
        bmod = colA[:, 64:112]

        mrow = sb("mrow", [128, 512])
        V(lambda e: e.memset(mrow[:, :], 0.0))

        def modulation(j0, nu):
            PE.wait(t_sil)
            for u in range(nu):
                bk, key = banks.take()
                w = W.get()
                for k in range(8):
                    r = 32 * (k % 4)
                    mm = lambda e: e.matmul(bk[r:r + 2, :], sil[:, :, k], w[:, k, :], start=(k < 4), stop=(k >= 4))
                    tk = PE(mm) if k >= 4 else mm(nc.tensor)
                W.done()
                V.wait(modulation.free)
                for c in range(4):
                    t = V(lambda e: e.tensor_copy(mrow[32 * c:32 * c + 2, :], bk[32 * c:32 * c + 2, :]), tk)
                banks.free(key, t)
                bt, kt_ = banks.take()
                PE.wait(t)
                for j in range(4):
                    modulation.free = PE(lambda e: transpose(bt[:, 128 * j:128 * j + 128], mrow[:, 128 * j:128 * j + 128]))
                o = modc[:, j0 + 4 * u:j0 + 4 * u + 4, :]
                V(lambda e: e.tensor_reduce(o, bt.rearrange("p (j c x) -> p j x c", j=4, c=4)[:, :, 0:2, :], AX, ALU.add),
                  modulation.free)
                banks.free(kt_, V.last)
                t = V(lambda e: e.tensor_tensor(o, o, bmod[:, j0 + 4 * u:j0 + 4 * u + 4].unsqueeze(2)
                                                .broadcast_to([128, 4, 2]), ALU.add))
            return t

        modulation.free = None

        def inv_root(dst, src, scale):
            t = V(lambda e: e.tensor_scalar(dst, src, scale, EPS, ALU.mult, ALU.add))
            t = A(lambda e: e.activation(dst, dst, ACT.Sqrt), t)
            return V(lambda e: e.reciprocal(dst, dst), t)

        sem_dbg = [0]
        hT = sb("hT", [128, 8, 768])
        ss = sb("ss", [128, 8])
        A1 = sb("A1", [128, 2, 8])
        base = Region(0, NA)
        xt = sb("xt", [128, 6, 1024], at=base)
        sqj = sb("sqj", [128, 1024], at=base)
        s_x = sem("s_x")
        nc.gpsimd.dma_start(xt[:, 0:2, :], d["ctx"].rearrange("(t p) n -> p t n", p=128)).then_inc(s_x, 16)
        nc.gpsimd.dma_start(xt[:, 2:6, :], d["x"].rearrange("(t p) n -> p t n", p=128)).then_inc(s_x, 16)
        for i in range(6):
            tk = A(lambda e, i=i: e.activation(sqj[:, :], xt[:, i, :], ACT.Square, accum_out=ss[:, i:i + 1]), (s_x, 32))
        V.wait(tk)
        inv_root(ss[:, 0:6], ss[:, 0:6], 1.0 / 1024)
        for i in range(6):
            t_xn = V(lambda e, i=i: e.tensor_scalar(xt[:, i, :], xt[:, i, :], ss[:, i:i + 1], None, ALU.mult))
        t_mod = modulation(0, 4)
        for s in range(2):
            t_A1 = V(lambda e, s=s: e.scalar_tensor_tensor(A1[:, s, :], modc[:, 8:16, s], 1.0, colA[:, 16:24],
                                                           ALU.add, ALU.mult))
        PE.wait(t_xn)
        for k in range(8):
            b1, k1 = banks.take()
            for i in range(4):
                mm = lambda e, i=i: transpose(b1[:, 128 * i:128 * i + 128], xt[:, 2 + i, 128 * k:128 * k + 128])
                tk = PE(mm) if i == 3 else mm(nc.tensor)
            t1 = V(lambda e: e.tensor_scalar(hT[:, k, 256:768], b1, A1[:, 0, k:k + 1], modc[:, k, 0:1],
                                             ALU.mult, ALU.add), tk)
            banks.free(k1, t1)
            b2, k2 = banks.take()
            transpose(b2[:, 0:128], xt[:, 0, 128 * k:128 * k + 128])
            tk = PE(lambda e: transpose(b2[:, 128:256], xt[:, 1, 128 * k:128 * k + 128]))
            A.wait(t_A1)
            t2 = A(lambda e: e.activation(hT[:, k, 0:256], b2[:, 0:256], ACT.Identity, bias=modc[:, k, 1:2],
                                          scale=A1[:, 1, k:k + 1]), tk)
            banks.free(k2, t2)
        t_xt_free = PE.last
        PE.wait(t1, t2)

        def proj(dst, pairs):
            m = len(pairs)
            for i, (l, r) in enumerate(pairs):
                f = lambda e, l=l, r=r, i=i: e.matmul(dst, l, r, start=(i == 0), stop=(i == m - 1))
                if i == m - 1:
                    return PE(f)
                f(nc.tensor)

        if STAGE <= 1:
            return finish(nc, ctx, V, A, SP, sem)

        slot2 = Region(0, 4096)
        oattT = sb("oattT", [128, 4, 512], at=slot2)
        att = Region(4096, NA)
        aq = sb("aq", [128, 4, 512], at=att)
        akv = sb("akv", [128, 6, 256], at=att)
        rope = sb("rope", [128, 4, 2, 64], at=att)
        tA = sb("tA", [128, 512], at=att)
        tB = sb("tB", [128, 512], at=att)
        tC = sb("tC", [128, 512], at=att)
        rr = sb("rr", [128, 8], at=att)
        qT = sb("qT", [128, 4, 512], at=att)
        kz = sb("kz", [128, 2, 768], at=att)
        t_kz = G(lambda e: e.memset(kz[:, :, :], 0.0), t_xt_free)
        pb = sb("pb", [128, 2, 768], at=att)
        pT = sb("pT", [128, 2, 768], at=att)
        st = sb("st", [128, 4, 2], at=att)
        ot = sb("ot", [128, 2, 512], at=att)
        V.wait(t_xt_free)
        A.wait(t_xt_free)
        t_rope = dma(A, rope[:, :, :, :], d["k_rope"], small[3], t1)

        def tokens_proj(w, c0, n, tok0, dst_fn, eng):
            bk, key = banks.take()
            t = proj(bk[:, 0:n], [(hT[:, k, tok0:tok0 + 128], w[:, k, c0:c0 + n]) for k in range(8)])
            t = eng(lambda e: dst_fn(e, bk[:, 0:n]), t)
            banks.free(key, t)
            return t

        w = W.get()
        taq = [tokens_proj(w, 0, 512, 256 + 128 * i, lambda e, b, i=i: e.tensor_copy(aq[:, i, :], b), V) for i in range(4)]
        W.done()
        w = W.get()
        tak = [tokens_proj(w, 0, 256, 128 * i, lambda e, b, i=i: e.tensor_copy(akv[:, i, :], b), V) for i in range(6)]
        W.done()

        def head_norm(src, nh, gain, scale, dst):
            s3 = src.rearrange("p (h e) -> p h e", e=64)
            q3 = tA[:, 0:64 * nh].rearrange("p (h e) -> p h e", e=64)
            V(lambda e: e.tensor_tensor(tA[:, 0:64 * nh], src, src, ALU.mult))
            V(lambda e: e.tensor_reduce(rr[:, 0:nh], q3, AX, ALU.add))
            inv_root(rr[:, 0:nh], rr[:, 0:nh], 1.0 / 64)
            V(lambda e: e.tensor_tensor(q3, s3, rr[:, 0:nh].unsqueeze(2).broadcast_to([128, nh, 64]), ALU.mult))
            return V(lambda e: e.scalar_tensor_tensor(dst, q3, scale, gain.unsqueeze(1).broadcast_to([128, nh, 64]),
                                                      ALU.mult, ALU.mult))

        def rotate(src, nh, tile, dst):
            cs = rope[:, tile, 0, :].unsqueeze(1).broadcast_to([128, nh, 64])
            s4 = src.rearrange("p h (a u f) -> p (h a) u f", a=2, u=2)
            sw = tA[:, 0:64 * nh].rearrange("p (h a u f) -> p (h a) u f", a=2, u=2, f=16)
            V(lambda e: e.tensor_copy(sw[:, :, 0, :], s4[:, :, 1, :]))
            V(lambda e: e.tensor_copy(sw[:, :, 1, :], s4[:, :, 0, :]))
            a3 = tA[:, 0:64 * nh].rearrange("p (h e) -> p h e", e=64)
            V(lambda e: e.tensor_tensor(a3, a3, rope[:, tile, 1, :].unsqueeze(1).broadcast_to([128, nh, 64]), ALU.mult))
            V(lambda e: e.tensor_tensor(src, src, cs, ALU.mult))
            return V(lambda e: e.tensor_tensor(dst, src, a3, ALU.add))

        V.wait(t_gb, t_rope)
        for i in range(6):
            kd = tB[:, 0:128].rearrange("p (h e) -> p h e", e=64)
            if i:
                V.wait(tk)
            t = head_norm(akv[:, i, 0:128], 2, gb[:, 1, :], 1.0, kd)
            if i >= 2:
                t = rotate(kd, 2, i - 2, kd)
            bk, key = banks.take()
            tk = PE(lambda e: transpose(bk[:, 0:128], tB[:, 0:128]), t)
            for g in range(2):
                gs = slice(64 * g, 64 * g + 64)
                t = A(lambda e: e.copy(kz[gs, g, 128 * i:128 * i + 128], bk[gs, 0:128]), tk, t_kz)
            banks.free(key, t)
        for i in range(4):
            qd = tB[:, :].rearrange("p (h e) -> p h e", e=64)
            if i:
                V.wait(tk)
            head_norm(aq[:, i, :], 8, gb[:, 0, :], 0.125, qd)
            rotate(qd, 8, i, qd)
            t = V(lambda e: e.tensor_copy(tC[:, :].rearrange("p (j g e) -> p j g e", g=2, e=64),
                                          tB[:, :].rearrange("p (g j e) -> p j g e", g=2, e=64)))
            bk, key = banks.take()
            for j in range(4):
                mm = lambda e, j=j: transpose(bk[:, 128 * j:128 * j + 128], tC[:, 128 * j:128 * j + 128])
                tk = PE(mm, t) if j == 3 else (PE.wait(t), mm(nc.tensor))[0]
            t = A(lambda e: e.copy(qT[:, :, 128 * i:128 * i + 128],
                                   bk.rearrange("p (j q) -> p j q", j=4)), tk)
            banks.free(key, t)
        PE.wait(t)
        PE.wait(tak[-1])
        its = [(i, h) for i in range(4) for h in range(8)]
        prev = {}
        rel_p, rel_pT = [None, None], [None, None]
        t_norm = {}

        def scores1(n):
            i, h = its[n]
            j, g = h % 4, h // 4
            s = n % 2
            bk, key = banks.take(2)
            qq = qT[:, j, 128 * i:128 * i + 128]
            PE(lambda e: e.matmul(bk[:, 0:512], qq, kz[:, g, 0:512], start=True, stop=True))
            tk = PE(lambda e: e.matmul(bk[:, 512:768], qq, kz[:, g, 512:768], start=True, stop=True))
            t = V(lambda e: e.tensor_reduce(st[:, s, 0:1], bk[:, 0:768], AX, ALU.max, negate=True), tk)
            A.wait(rel_p[s])
            t = A(lambda e: e.activation(pb[:, s, :], bk[:, 0:768], ACT.Exp, bias=st[:, s, 0:1],
                                         accum_out=st[:, s, 1:2]), t)
            banks.free(key, t)
            prev[n] = t

        def values1(n):
            i, h = its[n]
            g, s = h // 4, n % 2
            bk, key = banks.take(2)
            PE.wait(prev[n])
            for c in range(6):
                mm = lambda e, c=c: transpose(bk[:, 128 * c:128 * c + 128], pb[:, s, 128 * c:128 * c + 128])
                tk = PE(mm) if c == 5 else mm(nc.tensor)
            rel_p[s] = tk
            t = V(lambda e: e.tensor_copy(pT[:, s, :], bk[:, 0:768]), tk, rel_pT[s])
            banks.free(key, t)
            bo, ko = banks.take()
            PE.wait(t)
            tk = proj(bo[:, 0:128], [(pT[:, s, 128 * c:128 * c + 128], akv[:, c, 128:256])
                                    for c in range(6)])
            rel_pT[s] = tk
            V(lambda e: e.reciprocal(st[:, 2 + s, 0:1], st[:, s, 1:2]), prev[n])
            if h == 0 and i >= 2:
                V.wait(t_norm[i - 2])
            t = V(lambda e: e.tensor_scalar(ot[:, i % 2, 64 * h:64 * h + 64], bo[:, 64 * g:64 * g + 64], st[:, 2 + s, 0:1], None,
                                            ALU.mult), tk)
            banks.free(ko, t)
            if h == 7:
                bt, kt_ = banks.take()
                PE.wait(t)
                for j in range(4):
                    mm = lambda e, j=j: transpose(bt[:, 128 * j:128 * j + 128], ot[:, i % 2, 128 * j:128 * j + 128])
                    tk = PE(mm) if j == 3 else mm(nc.tensor)
                t_norm[i] = tk
                t = V(lambda e: e.tensor_copy(oattT[:, :, 128 * i:128 * i + 128],
                                              bt.rearrange("p (j q) -> p j q", j=4)), tk)
                banks.free(kt_, t)
            return t

        for n in range(33):
            if n < 32:
                scores1(n)
            if n:
                t_oatt = values1(n - 1)
        t_att = PE.last
        if STAGE <= 2:
            return finish(nc, ctx, V, A, SP, sem)

        oT = sb("oT", [128, 4, 512], at=slot2)
        hg = Region(4096, NA)
        qh = sb("qh", [128, 4, 512], at=hg)
        vh = sb("vh", [128, 6, 512], at=hg)
        KK = sb("KK", [128, 4, 768], at=hg)
        GG = sb("GG", [128, 4, 768], at=hg)
        LF = sb("LF", [128, 4, 768], at=hg)
        X = LF[:, :, 0:512]
        SS = sb("SS", [128, 4, 512], at=hg)
        qe = sb("qe", [128, 4, 512], at=hg)
        keT = sb("keT", [128, 5, 512], at=hg)
        Y = keT[:, 0:4, :]
        St = sb("St", [128, 5, 512], at=hg)
        dec = sb("dec", [128, 4, 6], at=hg)
        lbt = sb("lbt", [128, 6, 8], at=hg)
        reset = sb("reset", [128, 768], U8, at=hg)
        lb, omlb = lbt[:, 4, :], lbt[:, 5, :]
        V.wait(t_oatt, t_att)
        A.wait(t_oatt, t_att)
        G.wait(t_oatt, t_att)
        V(lambda e: e.memset(reset[:, :], 1))
        t_reset = V(lambda e: e.memset(reset[:, 0:768:128], 0))
        lg = colB[:, 0:16].rearrange("p (r l h) -> p r l h", r=2, l=2)
        l3 = lbt[:, :, :].rearrange("p i (r h) -> p i r h", r=2)
        V(lambda e: e.tensor_tensor(l3[:, 0], lg[:, :, 0, :], lg[:, :, 1, :], ALU.max))
        V(lambda e: e.tensor_tensor(l3[:, 1], lg[:, :, 0, :], l3[:, 0], ALU.subtract))
        t = V(lambda e: e.tensor_tensor(l3[:, 2], lg[:, :, 1, :], l3[:, 0], ALU.subtract))
        t = A(lambda e: e.activation(lbt[:, 1:3, :], lbt[:, 1:3, :], ACT.Exp), t)
        V(lambda e: e.tensor_tensor(lbt[:, 3, :], lbt[:, 1, :], lbt[:, 2, :], ALU.add), t)
        V(lambda e: e.reciprocal(lbt[:, 3, :], lbt[:, 3, :]))
        V(lambda e: e.tensor_tensor(lb, lbt[:, 1, :], lbt[:, 3, :], ALU.mult))
        t_lb = V(lambda e: e.tensor_tensor(omlb, lbt[:, 2, :], lbt[:, 3, :], ALU.mult))

        def gate_proj(r, *tokens):
            w = W.get()
            A.wait(*tokens)
            for h in range(4):
                bk, key = banks.take(2)
                proj(bk[:, 0:512], [(w[:, k, 128 * h:128 * h + 128], hT[:, k, 256:768]) for k in range(8)])
                tk = proj(bk[:, 512:768], [(w[:, k, 128 * h:128 * h + 128], hT[:, k, 0:256]) for k in range(8)])
                for dst, sc in ((LF, 1.0), (KK, -1.0)):
                    A(lambda e: e.activation(dst[:, h, 256:768], bk[:, 0:512], ACT.Sigmoid, scale=sc), tk)
                    t = A(lambda e: e.activation(dst[:, h, 0:256], bk[:, 512:768], ACT.Sigmoid, scale=sc))
                banks.free(key, t)
            W.done()
            return t

        def gates(r, t):
            V.wait(t, t_lb, t_reset)
            for h in range(4):
                i = 4 * r + h
                V(lambda e: e.tensor_scalar(LF[:, h, :], LF[:, h, :], omlb[:, i:i + 1], lb[:, i:i + 1],
                                            ALU.mult, ALU.add))
                t = V(lambda e: e.tensor_scalar(KK[:, h, :], KK[:, h, :], omlb[:, i:i + 1], None, ALU.mult))
            t = A(lambda e: e.activation(LF[:, :, :], LF[:, :, :], ACT.Ln), t)
            V.wait(t)
            for h in range(4):
                V(lambda e: e.tensor_tensor_scan(GG[:, h, :], reset[:, :], LF[:, h, :], 0.0, ALU.mult, ALU.add))
            ends = GG[:, :, :].rearrange("p h (c t) -> p h c t", t=128)[:, :, :, 127]
            t = V(lambda e: e.tensor_copy(dec[:, :, :], ends))
            if r == 1:
                t = V(lambda e: e.tensor_tensor(GG[:, :, :], GG[:, :, :], LF[:, :, :], ALU.subtract))
            return t

        tg = gate_proj(0)
        w = W.get()
        for h in range(4):
            bk, key = banks.take()
            tk = proj(bk, [(w[:, k, 128 * h:128 * h + 128], hT[:, k, 256:768]) for k in range(8)])
            t_q = A(lambda e: e.copy(qh[:, h, :], bk), tk)
            banks.free(key, t_q)
        W.done()
        w = W.get()
        for i in range(6):
            bk, key = banks.take()
            tk = proj(bk, [(hT[:, k, 128 * i:128 * i + 128], w[:, k, :]) for k in range(8)])
            t_vh = A(lambda e: e.copy(vh[:, i, :], bk), tk)
            banks.free(key, t_vh)
        W.done()

        S4 = SS[:, :, :].rearrange("p c (h t) -> p c h t", h=4)

        def state_part(r, t_g):
            T6 = dec[:, :, :].unsqueeze(3).broadcast_to([128, 4, 6, 128])
            G6 = GG[:, :, :].rearrange("p h (c t) -> p h c t", t=128)
            L6 = LF[:, :, :].rearrange("p h (c t) -> p h c t", t=128)
            if r == 0:
                t2 = A(lambda e: e.activation(X, GG[:, :, 256:768], ACT.Exp), t_g)
            else:
                tx = V(lambda e: e.tensor_tensor(X.rearrange("p h (c t) -> p h c t", t=128), T6[:, :, 2:6, :],
                                                 G6[:, :, 2:6, :], ALU.subtract))
                t2 = A(lambda e: e.activation(X, X, ACT.Exp), tx)
            V.wait(t_q)
            t_qe = V(lambda e: e.tensor_tensor(qe[:, :, :], X, qh[:, :, :], ALU.mult), t2)
            if r == 0:
                t = V(lambda e: e.tensor_tensor(L6, T6, G6, ALU.subtract))
                t = A(lambda e: e.activation(LF[:, :, :], LF[:, :, :], ACT.Exp), t)
            else:
                t = A(lambda e: e.activation(LF[:, :, :], GG[:, :, :], ACT.Exp), t_qe)
            A.wait(levels.free)
            t = V(lambda e: e.tensor_tensor(LF[:, :, :], LF[:, :, :], KK[:, :, :], ALU.mult), t)
            PE.wait(t)
            order = [0, 1, 2, 3, 4] if r == 0 else [1, 0, 5, 4, 3]
            for n, c in enumerate(order):
                bk, key = banks.take()
                for h in range(4):
                    mm = lambda e, h=h: transpose(bk[:, 128 * h:128 * h + 128], LF[:, h, 128 * c:128 * c + 128])
                    tk = PE(mm) if h == 3 else mm(nc.tensor)
                t = A(lambda e: e.copy(keT[:, n, :], bk), tk)
                banks.free(key, t)
            t_lf = tk
            t_dec = A(lambda e: e.activation(dec[:, :, :], dec[:, :, :], ACT.Exp), t_qe)
            V.wait(t_dec)
            PE.wait(t, t_vh)
            for n, c in enumerate(order):
                bk, key = banks.take()
                for h in range(4):
                    mm = lambda e, h=h: e.matmul(bk[:, 128 * h:128 * h + 128], keT[:, n, 128 * h:128 * h + 128],
                                                 vh[:, c, 128 * h:128 * h + 128], start=True, stop=True)
                    tk = PE(mm) if h == 3 else mm(nc.tensor)
                if n == 0:
                    t = V(lambda e: e.tensor_copy(St[:, 0, :], bk), tk)
                else:
                    for h in range(4):
                        hs = slice(128 * h, 128 * h + 128)
                        t = V(lambda e: e.scalar_tensor_tensor(St[:, n, hs], St[:, n - 1, hs], dec[:, h, c:c + 1],
                                                               bk[:, hs], ALU.mult, ALU.add), tk)
                banks.free(key, t)
            return t, t_qe, t_lf

        def levels(r, chunk0_init):
            V.wait(PE.last)
            for l, m in enumerate(LEVELS):
                nb = 512 // (2 * m)
                gv = GG[:, :, 256:768].rearrange("p h (b u m) -> p h b u m", u=2, m=m)
                xv = X.rearrange("p h (b u m) -> p h b u m", u=2, m=m)
                yv = Y[:, :, :].rearrange("p h (b u m) -> p h b u m", u=2, m=m)
                kv = KK[:, :, 256:768].rearrange("p h (b u m) -> p h b u m", u=2, m=m)
                qv = qh[:, :, :].rearrange("p h (b u m) -> p h b u m", u=2, m=m)
                ref = gv[:, :, :, 0, m - 1:m] if r == 0 else gv[:, :, :, 1, 0:1]
                ref = ref.broadcast_to([128, 4, nb, m])
                V(lambda e: e.tensor_tensor(xv[:, :, :, 0, :], ref, gv[:, :, :, 0, :], ALU.subtract))
                t = V(lambda e: e.tensor_tensor(xv[:, :, :, 1, :], gv[:, :, :, 1, :], ref, ALU.subtract))
                t = A(lambda e: e.activation(X, X, ACT.Exp), t)
                a, b = (kv, qv) if r == 0 else (qv, kv)
                V.wait(t, *([levels.free] if levels.free else []))
                V(lambda e: e.tensor_tensor(yv[:, :, :, 0, :], xv[:, :, :, 0, :], a[:, :, :, 0, :], ALU.mult))
                t = V(lambda e: e.tensor_tensor(yv[:, :, :, 1, :], xv[:, :, :, 1, :], b[:, :, :, 1, :], ALU.mult))
                PE.wait(t)
                for c in range(4):
                    bk, key = banks.take()
                    for h in range(4):
                        yy = Y[:, h, 128 * c:128 * c + 128]
                        mm = lambda e, h=h, yy=yy: e.matmul(bk[:, 128 * h:128 * h + 128], yy, yy, start=True, stop=True)
                        tk = PE(mm) if h == 3 else mm(nc.tensor)
                    mk = masks[:, 7 * r + l, :].unsqueeze(1).broadcast_to([128, 4, 128])
                    t = V(lambda e: e.copy_predicated(S4[:, c], mk, bk.rearrange("p (h t) -> p h t", h=4)), tk, t_masks)
                    banks.free(key, t)
                levels.free = tk
            return t


        def diagonal():
            for c in range(4):
                bk, key = banks.take()
                for h in range(4):
                    mm = lambda e: e.matmul(bk[:, 128 * h:128 * h + 128], KK[:, h, 256 + 128 * c:384 + 128 * c],
                                            qh[:, h, 128 * c:128 * c + 128], start=True, stop=True)
                    tk = PE(mm) if h == 3 else mm(nc.tensor)
                y4 = Y[:, c, :].rearrange("p (h t) -> p h t", h=4)
                V.wait(levels.free)
                V(lambda e: e.tensor_tensor(y4, bk.rearrange("p (h t) -> p h t", h=4),
                                            ident[:, :].unsqueeze(1).broadcast_to([128, 4, 128]), ALU.mult), tk)
                banks.free(key, V.last)
                t = V(lambda e: e.tensor_tensor(S4[:, c], S4[:, c], y4, ALU.add))
            return t

        levels.free = None
        t_g = gates(0, tg)
        t_st, t_qe, t_lf = state_part(0, t_g)
        V(lambda e: e.memset(SS[:, :, :], 0.0))
        V.wait(t_q)
        levels(0, None)
        diagonal()
        PE.wait(t_st, t_qe)
        for c in range(4):
            bk, key = banks.take()
            for h in range(4):
                hs = slice(128 * h, 128 * h + 128)
                mm = lambda e, h=h, hs=hs: e.matmul(bk[:, hs], St[:, 1 + c, hs], qe[:, h, 128 * c:128 * c + 128],
                                                    start=True, stop=True)
                tk = PE(mm) if h == 3 else mm(nc.tensor)
            t_of = A(lambda e: e.copy(oT[:, :, 128 * c:128 * c + 128], bk.rearrange("p (h t) -> p h t", h=4)), tk)
            banks.free(key, t_of)
        t_inter = tk
        tg = gate_proj(1, V.last, t_lf, PE.last)
        t_g = gates(1, tg)
        V.wait(t_inter)
        t_st, t_qe, t_lf = state_part(1, t_g)
        t = levels(1, None)
        t = diagonal()
        PE.wait(t, t_st, t_qe)
        for c in range(4):
            bk, key = banks.take()
            for h in range(4):
                hs = slice(128 * h, 128 * h + 128)
                tk = proj(bk[:, hs], [(vh[:, 2 + c, hs], SS[:, c, hs]),
                                      (St[:, 4 - c, hs], qe[:, h, 128 * c:128 * c + 128])])
            ov = oT[:, :, 128 * c:128 * c + 128]
            t_o = V(lambda e: e.tensor_tensor(ov, bk.rearrange("p (h t) -> p h t", h=4), ov, ALU.add), tk, t_of)
            banks.free(key, t_o)
        t_hg_pe = PE.last
        if STAGE <= 3:
            return finish(nc, ctx, V, A, SP, sem)

        t_mod = modulation(16, 8)
        big = Region(4096, TOP)
        top = Region(TOP, NA)
        uT = sb("uT", [128, 8, 512], at=big)
        sg = sb("sg", [128, 2, 512], at=big)
        rn = sb("rn", [128, 512], at=big)
        aT = sb("aT", [128, 4, 512], at=big)
        xk = sb("xk", [128, 4, 1024], at=big)
        V.wait(t_hg_pe)
        A.wait(t_hg_pe, t_o)
        s_x2 = sem("s_x2")
        A.wait(t_o)
        nc.scalar.dma_start(xk[:, :, :], d["x"].rearrange("(t p) n -> p t n", p=128)).then_inc(s_x2, 16)

        w = W.get()
        for h in range(4):
            s = h % 2
            bk, key = banks.take()
            tk = proj(bk, [(w[:, k, 128 * h:128 * h + 128], hT[:, k, 256:768]) for k in range(8)])
            t = A(lambda e: e.activation(aT[:, h, :], bk, ACT.Sigmoid), tk)
            t = V(lambda e: e.tensor_tensor(aT[:, h, :], aT[:, h, :], bk, ALU.mult), t)
            banks.free(key, t)
            t = A(lambda e: e.activation(sg[:, s, :], oT[:, h, :], ACT.Square), t)
            bk2, key2 = banks.take()
            PE.wait(t)
            tk = proj(bk2, [(ones[:, :], sg[:, s, :])])
            V(lambda e: e.tensor_scalar(rn[:, :], bk2, 1.0 / 128, EPS, ALU.mult, ALU.add), tk)
            banks.free(key2, V.last)
            t = A(lambda e: e.activation(rn[:, :], rn[:, :], ACT.Sqrt), V.last)
            V(lambda e: e.reciprocal(rn[:, :], rn[:, :]), t)
            V(lambda e: e.tensor_tensor(rn[:, :], rn[:, :], oT[:, h, :], ALU.mult))
            t_a = V(lambda e: e.scalar_tensor_tensor(aT[:, h, :], rn[:, :], colA[:, 112 + h:113 + h], aT[:, h, :],
                                                     ALU.mult, ALU.mult))
            A.wait(t_a)
        W.done()
        PE.wait(t_a)
        sgn = 0
        for br, src in enumerate((aT, oattT)):
            wb = W.get()
            for hf in range(2):
                w = W.get()
                for j in range(4):
                    dt_ = 4 * hf + j
                    b1, k1 = banks.take()
                    tk = proj(b1, [(w[:, k, 128 * j:128 * j + 128], hT[:, k, 256:768]) for k in range(8)])
                    s = sgn % 2
                    sgn += 1
                    t = A(lambda e: e.activation(sg[:, s, :], b1, ACT.Sigmoid), tk, V.last)
                    banks.free(k1, t)
                    b2, k2 = banks.take()
                    tk = proj(b2, [(wb[:, k, 128 * dt_:128 * dt_ + 128], src[:, k, :]) for k in range(4)])
                    if br == 0:
                        t_u = V(lambda e: e.tensor_tensor(uT[:, dt_, :], sg[:, s, :], b2, ALU.mult), t, tk)
                    else:
                        V(lambda e: e.tensor_tensor(sg[:, s, :], sg[:, s, :], b2, ALU.mult), t, tk)
                        t_u = V(lambda e: e.tensor_tensor(uT[:, dt_, :], uT[:, dt_, :], sg[:, s, :], ALU.add))
                    banks.free(k2, t_u if br == 0 else (V.sem, V.n - 1))
            W.done()
        PE.wait(t_u)
        xT = sb("xT", [128, 8, 512], at=top)
        PE.wait((s_x2, 16))
        for k in range(8):
            b1, k1 = banks.take()
            for i in range(4):
                mm = lambda e, i=i: transpose(b1[:, 128 * i:128 * i + 128], xk[:, i, 128 * k:128 * k + 128])
                tk = PE(mm) if i == 3 else mm(nc.tensor)
            t_xT = A(lambda e: e.copy(xT[:, k, :], b1), tk)
            banks.free(k1, t_xT)
        for hf in range(2):
            w = W.get()
            for j in range(4):
                dt_ = 4 * hf + j
                b1, k1 = banks.take()
                tk = proj(b1, [(w[:, k, 128 * j:128 * j + 128], uT[:, k, :]) for k in range(8)])
                t_x1 = V(lambda e: e.scalar_tensor_tensor(xT[:, dt_, :], b1, modc[:, 16 + dt_, 0:1], xT[:, dt_, :],
                                                          ALU.mult, ALU.add), tk, t_xT, t_mod)
                banks.free(k1, t_x1)
            W.done()
        t_u_free = PE.last

        def column_norm(srcT, nk, sq, rinv, tok):
            bk, key = banks.take()
            rel = [None, None]
            for k in range(nk):
                t = A(lambda e: e.activation(sq[:, k % 2, :], srcT[:, k, :], ACT.Square), tok, rel[k % 2])
                f = lambda e: e.matmul(bk, ones[:, :], sq[:, k % 2, :], start=(k == 0), stop=(k == nk - 1))
                rel[k % 2] = PE(f, t)
            t = V(lambda e: e.tensor_scalar(rinv, bk, 1.0 / (128 * nk), EPS, ALU.mult, ALU.add), PE.last)
            banks.free(key, t)
            t = A(lambda e: e.activation(rinv, rinv, ACT.Sqrt), t)
            return V(lambda e: e.reciprocal(rinv, rinv), t)

        if STAGE <= 4:
            return finish(nc, ctx, V, A, SP, sem)

        moe = Region(0, TOP)
        h2T = hT[:, 0:8, 0:512]
        sq = sb("sq", [128, 2, 512], at=top)
        rinv = sb("rinv", [128, 512], at=top)
        xeT = sb("xeT", [128, 8, 2, 128], at=moe)
        h2k = sb("h2k", [128, 4, 1024], at=moe)
        xe = sb("xe", [128, 1024], at=moe)
        ye = sb("ye", [128, 8, 1024], at=moe)
        hid = sb("hid", [128, 2, 512], at=moe)
        hidT = sb("hidT", [128, 8, 128], at=moe)
        wr = sb("wr", [128, 8, 16], at=moe)
        iot = sb("iot", [128, 512], at=moe)
        lgt = sb("lgt", [128, 4, 16], at=moe)
        lst = sb("lst", [128, 3, 4], at=moe)
        aff = sb("aff", [16, 512], at=moe)
        gv = sb("gv", [16, 64], at=moe)
        iu = sb("iu", [16, 64], U32, at=moe)
        ifl = sb("ifl", [16, 64], at=moe)
        gi8 = sb("gi8", [8, 2, 128], at=moe)
        giT = sb("giT", [128, 2, 8], at=moe)
        idx = sb("idx", [128, 8], U32, at=moe)
        s_wr, s_iot, s_h2, s_gi, s_ga = sem("s_wr"), sem("s_iot"), sem("s_h2"), sem("s_gi"), sem("s_ga")
        V.wait(t_u_free)
        A.wait(t_u_free, t_x1)
        G.wait(t_u_free, t_x1)
        nc.scalar.dma_start(wr[:, :, :], d["w_router"].rearrange("(k p) n -> p k n", p=128)).then_inc(s_wr, 16)
        nc.scalar.dma_start(iot[:, :], d["k_iota"].partition_broadcast(128)).then_inc(s_iot, 16)
        column_norm(xT, 8, sq, rinv[:, :], t_x1)
        t = V(lambda e: e.scalar_tensor_tensor(AB[:, 0, :], modc[:, 32:40, 0], 1.0, colA[:, 24:32], ALU.add, ALU.mult))
        for k in range(8):
            V(lambda e: e.tensor_tensor(h2T[:, k, :], xT[:, k, :], rinv[:, :], ALU.mult))
            t_h2 = V(lambda e: e.tensor_scalar(h2T[:, k, :], h2T[:, k, :], AB[:, 0, k:k + 1], modc[:, 24 + k, 0:1],
                                               ALU.mult, ALU.add))
        PE.wait(t_h2, (s_wr, 16))
        for i in range(4):
            bk, key = banks.take()
            tk = proj(bk[:, 0:16], [(h2T[:, k, 128 * i:128 * i + 128], wr[:, k, :]) for k in range(8)])
            t = V(lambda e: e.tensor_copy(lgt[:, i, :], bk[:, 0:16]), tk)
            banks.free(key, t)
        h2d = nc.dram_tensor("h2_scratch", (512, 1024), F32, kind="Internal").ap()
        for i in range(4):
            for q in range(2):
                bk, key = banks.take()
                for k in range(4):
                    mm = lambda e, k=k: transpose(bk[:, 128 * k:128 * k + 128],
                                                  h2T[:, 4 * q + k, 128 * i:128 * i + 128])
                    tk = PE(mm) if k == 3 else mm(nc.tensor)
                t_h2k = A(lambda e: e.copy(h2k[:, i, 512 * q:512 * q + 512], bk), tk)
                banks.free(key, t_h2k)
        A.wait(t_h2k)
        nc.scalar.dma_start(h2d.rearrange("(t p) n -> p t n", p=128), h2k[:, :, :]).then_inc(s_h2, 16)
        V(lambda e: e.tensor_reduce(lst[:, 0, :], lgt[:, :, :], AX, ALU.max))
        t = V(lambda e: e.tensor_tensor(lgt[:, :, :], lgt[:, :, :], lst[:, 0, :].unsqueeze(2).broadcast_to([128, 4, 16]),
                                        ALU.subtract))
        t = A(lambda e: e.activation(lgt[:, :, :], lgt[:, :, :], ACT.Exp), t)
        V(lambda e: e.tensor_reduce(lst[:, 1, :], lgt[:, :, :], AX, ALU.add), t)
        V(lambda e: e.reciprocal(lst[:, 2, :], lst[:, 1, :]))
        t = V(lambda e: e.tensor_tensor(lgt[:, :, :], lgt[:, :, :], lst[:, 2, :].unsqueeze(2).broadcast_to([128, 4, 16]),
                                        ALU.mult))
        bk, key = banks.take()
        PE.wait(t)
        for i in range(4):
            tk = PE(lambda e: transpose(bk[0:16, 128 * i:128 * i + 128], lgt[:, i, :]))
        t = V(lambda e: e.tensor_copy(aff[:, :], bk[0:16, :]), tk)
        banks.free(key, t)
        for r in range(8):
            rs = slice(8 * r, 8 * r + 8)
            V(lambda e: e.max(gv[:, rs], aff[:, :]))
            V(lambda e: e.max_index(iu[:, rs], gv[:, rs], aff[:, :]))
            if r < 7:
                V(lambda e: e.match_replace(aff[:, :], gv[:, rs], aff[:, :], -1.0))
        t = V(lambda e: e.tensor_copy(ifl[:, :], iu[:, :]))
        A.wait(t)
        for e2 in range(2):
            for n, src in enumerate((gv, ifl)):
                nc.scalar.dma_start(gi8[:, n, 64 * e2:64 * e2 + 64], src[e2:16:2, :]).then_inc(s_gi, 16)
        bk, key = banks.take()
        PE.wait((s_gi, 64))
        transpose(bk[:, 0:8], gi8[:, 0, :], 8)
        tk = PE(lambda e: transpose(bk[:, 8:16], gi8[:, 1, :], 8))
        V(lambda e: e.tensor_copy(giT[:, :, :], bk[:, 0:16].rearrange("p (a b) -> p a b", a=2)), tk)
        t_idx = V(lambda e: e.tensor_copy(idx[:, :], bk[:, 8:16]))
        banks.free(key, t_idx)

        def gather(p, tok):
            G.wait(t_idx, (s_h2, 16), tok)
            nc.gpsimd.indirect_dma_start(xe[:, :], None, h2d, bass.IndirectOffsetOnAxis(ap=idx[:, p:p + 1], axis=0))\
                .then_inc(s_ga, 16)
            return (s_ga, 16 * (p + 1))

        def expert_in(p, ta):
            for q in range(2):
                bk, key = banks.take()
                PE.wait(ta)
                for k in range(4):
                    mm = lambda e, k=k: transpose(bk[:, 128 * k:128 * k + 128],
                                                  xe[:, 512 * q + 128 * k:512 * q + 128 * k + 128])
                    tk = PE(mm) if k == 3 else mm(nc.tensor)
                t = A(lambda e: e.copy(xeT[:, 4 * q:4 * q + 4, p % 2, :], bk.rearrange("p (k s) -> p k s", k=4)), tk)
                banks.free(key, t)
            return tk, t

        tg_ = gather(0, None)
        t_free, t_xe = expert_in(0, tg_)
        rel_hid, rel_hidT = None, None

        def pair_product(stat):
            out = []
            for hf in range(2):
                bk, key = banks.take()
                for kh in range(2):
                    ww = [W.get(), W.get()]
                    for k in range(4):
                        for e2 in range(2):
                            es = slice(64 * e2, 64 * e2 + 64)
                            f = lambda e: e.matmul(bk[es, :], stat[:, 4 * kh + k, es], ww[e2][:, k, :],
                                                   start=(kh == 0 and k == 0), stop=(kh == 1 and k == 3))
                            tk = PE(f) if k == 3 else f(nc.tensor)
                    W.done()
                out.append((bk, key, tk))
            return out

        for p in range(8):
            if p < 7:
                tg_ = gather(p + 1, t_free)
            PE.wait(t_xe)
            bg = pair_product(xeT[:, :, p % 2, :])
            t = None
            for hf in range(2):
                bk, key, tk = bg[hf]
                t = A(lambda e: e.activation(hid[:, hf, :], bk, ACT.Sigmoid), tk, rel_hid)
                t = V(lambda e: e.tensor_tensor(hid[:, hf, :], hid[:, hf, :], bk, ALU.mult), t)
                banks.free(key, t)
            bu = pair_product(xeT[:, :, p % 2, :])
            if p < 7:
                t_free, t_xe = expert_in(p + 1, tg_)
            for hf in range(2):
                bk, key, tk = bu[hf]
                t = V(lambda e: e.tensor_tensor(hid[:, hf, :], hid[:, hf, :], bk, ALU.mult), tk)
                banks.free(key, t)
                bt, kt_ = banks.take()
                PE.wait(t)
                for k in range(4):
                    mm = lambda e: transpose(bt[:, 128 * k:128 * k + 128], hid[:, hf, 128 * k:128 * k + 128])
                    tk = PE(mm) if k == 3 else mm(nc.tensor)
                t_hT = A(lambda e: e.copy(hidT[:, 4 * hf:4 * hf + 4, :], bt.rearrange("p (k s) -> p k s", k=4)), tk,
                         rel_hidT)
                banks.free(kt_, t_hT)
            rel_hid = tk
            PE.wait(t_hT)
            for hf, (bk, key, tk) in enumerate(pair_product(hidT)):
                t_yek = V(lambda e: e.tensor_scalar(ye[:, p, 512 * hf:512 * hf + 512], bk, giT[:, 0, p:p + 1], None,
                                                    ALU.mult), tk)
                banks.free(key, t_yek)
            rel_hidT = PE.last
        PT = hT[:, :, 0:512]
        V.wait((s_iot, 16), t_h2k, PE.last)
        for p in range(8):
            t = V(lambda e: e.tensor_scalar(PT[:, p, :], iot[:, :], giT[:, 1, p:p + 1], None, ALU.is_equal))
        PE.wait(t, t_yek)
        for k in range(8):
            bk, key = banks.take()
            tk = proj(bk, [(ye[:, p, 128 * k:128 * k + 128], PT[:, p, :]) for p in range(8)])
            t_x2 = V(lambda e: e.scalar_tensor_tensor(xT[:, k, :], bk, modc[:, 40 + k, 0:1], xT[:, k, :],
                                                      ALU.mult, ALU.add), tk)
            banks.free(key, t_x2)
        t_moe = PE.last
        if STAGE <= 5:
            return finish(nc, ctx, V, A, SP, sem)

        column_norm(xT, 8, sq, rinv[:, :], t_x2)
        for k in range(8):
            t_x3 = V(lambda e: e.scalar_tensor_tensor(xT[:, k, :], xT[:, k, :], colA[:, 32 + k:33 + k], rinv[:, :],
                                                      ALU.mult, ALU.mult))
        column_norm(xT, 8, sq, rinv[:, :], t_x3)
        V.wait(t_moe)
        for k in range(8):
            t_h3 = V(lambda e: e.scalar_tensor_tensor(hT[:, k, 0:512], xT[:, k, :], colA[:, 40 + k:41 + k], rinv[:, :],
                                                      ALU.mult, ALU.mult))

        mixT = sb("mixT", [128, 8, 512], at=Region(0, 4096))
        b2 = Region(4096, TOP)
        ksw = sb("ksw", [128, 4, 256], at=b2)
        kww = sb("kww", [128, 4, 256], at=b2)
        gat = sb("gat", [128, 4, 24], at=b2)
        q2 = sb("q2", [128, 4, 512], at=b2)
        tA = sb("tA2", [128, 512], at=b2)
        tB = sb("tB2", [128, 512], at=b2)
        tC = sb("tC2", [128, 512], at=b2)
        rr = sb("rr2", [128, 8], at=b2)
        q2T = sb("q2T", [128, 4, 512], at=b2)
        kz2 = sb("kz2", [128, 2, 2, 512], at=b2)
        hdn = sb("hdn", [128, 2, 2, 64], at=b2)
        kcm = sb("kcm", [32, 2, 128], at=b2)
        kcz = sb("kcz", [128, 2, 32], at=b2)
        wc2 = sb("wc2", [128, 2, 2, 64], at=b2)
        dist = sb("dist", [128, 512], at=b2)
        cb = sb("cb", [128, 4, 8, 32], at=b2)
        cmk = sb("cmk", [128, 4, 32], at=b2)
        b3 = Region(b2.at, TOP)
        kcv = sb("kcv", [128, 2, 512], at=b2)
        shA = sb("shA", [128, 4, 512], at=b2)
        blkT = sb("blkT", [128, 2, 16, 2, 32], at=b2)
        V.wait(t_moe)
        A.wait(t_moe, t_x3)
        s_k2 = sem("s_k2")
        nc.scalar.dma_start(wc2[:, :, :, :], d["w_cmp2_2"].rearrange("v (k p) n -> p v k n", p=128)).then_inc(s_k2, 16)
        nc.scalar.dma_start(dist[:, :], d["k_dist"]).then_inc(s_k2, 16)
        nc.scalar.dma_start(cb[:, :, :, :], d["k_cb"]).then_inc(s_k2, 16)
        nc.scalar.dma_start(cmk[:, :, :], d["k_cm"]).then_inc(s_k2, 16)
        V.wait((s_k2, 64))
        G(lambda e: e.memset(kz2[:, :, :, :], 0.0), t_moe, t_x3)
        t_kz2 = G(lambda e: e.memset(kcz[:, :, :], 0.0))

        def proj_tok(w, c0, n, i):
            bk, key = banks.take()
            t = proj(bk[:, 0:n], [(hT[:, k, 128 * i:128 * i + 128], w[:, k, c0:c0 + n]) for k in range(8)])
            return bk, key, t

        PE.wait(t_h3)
        w = W.get()
        for v in range(2):
            bk, key = banks.take()
            tk = proj(bk, [(w[:, k, 128 * v:128 * v + 128], hT[:, k, 0:512]) for k in range(8)])
            t_kcv = A(lambda e: e.copy(kcv[:, v, :], bk), tk)
            banks.free(key, t_kcv)
        for i in range(4):
            bk, key, tk = proj_tok(w, 256, 256, i)
            t = A(lambda e: e.copy(ksw[:, i, :], bk[:, 0:256]), tk)
            banks.free(key, t)
        W.done()
        s_sh = sem("s_sh")
        A.wait(t_kcv)
        for v in range(2):
            for g in range(2):
                src = kcv[64 * g:64 * g + 64, v, :]
                nc.scalar.dma_start(shA[0:64, 2 * v + g, :], src).then_inc(s_sh, 16)
                nc.scalar.dma_start(shA[64:128, 2 * v + g, 0:511], src[:, 1:512]).then_inc(s_sh, 16)
        w = W.get()
        for i in range(4):
            bk, key, tk = proj_tok(w, 0, 512, i)
            t_q2 = V(lambda e: e.tensor_copy(q2[:, i, :], bk), tk)
            banks.free(key, t_q2)
        W.done()
        w = W.get()
        for i in range(4):
            bk, key, tk = proj_tok(w, 0, 280, i)
            V(lambda e: e.tensor_copy(kww[:, i, :], bk[:, 0:256]), tk)
            t = A(lambda e: e.activation(gat[:, i, :], bk[:, 256:280], ACT.Sigmoid), V.last)
            banks.free(key, t)
        t_gat = t
        W.done()
        for v in range(2):
            for g in range(2):
                base_ap = shA[:, 2 * v + g, :].rearrange("p (i l) -> p i l", l=16)
                for half in range(2):
                    src = base_ap[:, half:half + 31, :].rearrange("p i (l u) -> p l u i", u=2)[:, :, 0, :]
                    dstv = blkT[:, v, 8 * half:8 * half + 8, g, 0:31]
                    pe = colB[:, 32 + 16 * v + 8 * half:40 + 16 * v + 8 * half].unsqueeze(2).broadcast_to([128, 8, 31])
                    V(lambda e: e.tensor_tensor(dstv, src, pe, ALU.add), (s_sh, 128))
            t_blk = V(lambda e: e.memset(blkT[:, v, :, :, 31:32], 0.0))
        for v in range(2):
            w = W.get()
            PE.wait(t_blk)
            bk, key = banks.take()
            for hh in range(2):
                tk = proj(bk[:, 64 * hh:64 * hh + 64],
                          [(w[:, l, 128 * hh:128 * hh + 128], blkT[:, v, l].rearrange("p g i -> p (g i)"))
                           for l in range(16)])
            W.done()
            for hh in range(2):
                t_hd = A(lambda e: e.activation(hdn[:, v, hh, :], bk[:, 64 * hh:64 * hh + 64], ACT.Gelu_apprx_tanh,
                                                bias=colB[:, 28 + 2 * v + hh:29 + 2 * v + hh]), tk)
            banks.free(key, t_hd)
            bk, key = banks.take()
            PE.wait(t_hd, (s_k2, 64))
            for g in range(2):
                tk = proj(bk[0:32, 64 * g:64 * g + 64],
                          [(hdn[:, v, hh, 32 * g:32 * g + 32], wc2[:, v, hh, :]) for hh in range(2)])
            t_kcm = V(lambda e: e.tensor_tensor(kcm[:, v, :].rearrange("p (g e) -> p g e", g=2),
                                                bk[0:32, 0:128].rearrange("p (g e) -> p g e", g=2),
                                                gb[0:32, 6 + v, :].unsqueeze(1).broadcast_to([32, 2, 64]), ALU.add), tk)
            banks.free(key, t_kcm)

        def head_norm2(src, nh, gain, scale, dst, P=128):
            s3 = src.rearrange("p (h e) -> p h e", e=64)
            q3 = tA[0:P, 0:64 * nh].rearrange("p (h e) -> p h e", e=64)
            V(lambda e: e.tensor_tensor(tA[0:P, 0:64 * nh], src, src, ALU.mult))
            V(lambda e: e.tensor_reduce(rr[0:P, 0:nh], q3, AX, ALU.add))
            inv_root(rr[0:P, 0:nh], rr[0:P, 0:nh], 1.0 / 64)
            V(lambda e: e.tensor_tensor(q3, s3, rr[0:P, 0:nh].unsqueeze(2).broadcast_to([P, nh, 64]), ALU.mult))
            return V(lambda e: e.scalar_tensor_tensor(dst, q3, scale, gain.unsqueeze(1).broadcast_to([P, nh, 64]),
                                                      ALU.mult, ALU.mult))

        kc3 = kcm[:, 0, :].rearrange("p (g e) -> p g e", g=2)
        t = head_norm2(kcm[:, 0, :], 2, gb[0:32, 3, :], 1.0, kc3, 32)
        bk, key = banks.take()
        tk = PE(lambda e: transpose(bk[:, 0:32], kcm[:, 0, :], 32), t)
        for g in range(2):
            gs = slice(64 * g, 64 * g + 64)
            t = A(lambda e: e.copy(kcz[gs, g, :], bk[gs, 0:32]), tk, t_kz2)
        banks.free(key, t)
        for v, (src_t, gi) in enumerate(((ksw, 4), (kww, 5))):
            for i in range(4):
                V.wait(tk)
                t = head_norm2(src_t[:, i, 0:128], 2, gb[:, gi, :], 1.0, tB[:, 0:128].rearrange("p (h e) -> p h e", e=64))
                bk, key = banks.take()
                tk = PE(lambda e: transpose(bk[:, 0:128], tB[:, 0:128]), t)
                for g in range(2):
                    gs = slice(64 * g, 64 * g + 64)
                    t = A(lambda e: e.copy(kz2[gs, g, v, 128 * i:128 * i + 128], bk[gs, 0:128]), tk)
                banks.free(key, t)
        for i in range(4):
            V.wait(tk)
            head_norm2(q2[:, i, :], 8, gb[:, 2, :], 0.125, tB[:, :].rearrange("p (h e) -> p h e", e=64))
            t = V(lambda e: e.tensor_copy(tC[:, :].rearrange("p (j g e) -> p j g e", g=2, e=64),
                                          tB[:, :].rearrange("p (g j e) -> p j g e", g=2, e=64)))
            bk, key = banks.take()
            PE.wait(t)
            for j in range(4):
                mm = lambda e, j=j: transpose(bk[:, 128 * j:128 * j + 128], tC[:, 128 * j:128 * j + 128])
                tk = PE(mm) if j == 3 else mm(nc.tensor)
            t = A(lambda e: e.copy(q2T[:, :, 128 * i:128 * i + 128], bk.rearrange("p (j q) -> p j q", j=4)), tk)
            banks.free(key, t)
        PE.wait(t)

        cp = sb("cp", [128, 8, 32], at=b3)
        cst = sb("cst", [128, 3, 8], at=b3)
        cpT = sb("cpT", [32, 8, 128], at=b3)
        sc2 = sb("sc2", [128, 2, 512], at=b3)
        p2 = sb("p2", [128, 2, 512], at=b3)
        p2T = sb("p2T", [128, 2, 512], at=b3)
        st2 = sb("st2", [128, 2, 3], at=b3)
        o2 = sb("o2", [128, 512], at=b3)
        o2n = sb("o2n", [128, 512], at=b3)
        on = sb("on", [128, 1], at=b3)
        V.wait(PE.last)
        A.wait(PE.last, V.last)
        rel_p, rel_pT = [None, None], [None, None]
        its = [(i, h, v) for i in range(4) for h in range(8) for v in range(2)]
        prev = {}
        rel_cp, rel_cpT, rel_on = None, None, None

        def cmp_part(i):
            nonlocal rel_cp, rel_cpT
            bk, key = banks.take(2)
            for h in range(8):
                j, g = h % 4, h // 4
                tk = PE(lambda e: e.matmul(bk[:, 512 * g + 32 * j:512 * g + 32 * j + 32],
                                           q2T[:, j, 128 * i:128 * i + 128], kcz[:, g, :], start=True, stop=True))
            V.wait(rel_cp)
            V(lambda e: e.tensor_tensor(cp[:, :, :].rearrange("p (g j) s -> p g j s", g=2),
                                        bk.rearrange("p (g j s) -> p g j s", g=2, s=32)[:, :, 0:4, :],
                                        cb[:, i].rearrange("p (g j) s -> p g j s", g=2), ALU.add), tk)
            banks.free(key, V.last)
            V(lambda e: e.tensor_reduce(cst[:, 0, :], cp[:, :, 0:31], AX, ALU.max))
            t = V(lambda e: e.tensor_tensor(cp[:, :, :], cp[:, :, :], cst[:, 0, :].unsqueeze(2).broadcast_to([128, 8, 32]),
                                            ALU.subtract))
            t = A(lambda e: e.activation(cp[:, :, 0:31], cp[:, :, 0:31], ACT.Exp), t)
            V(lambda e: e.tensor_tensor(cp[:, :, :], cp[:, :, :], cmk[:, i, :].unsqueeze(1).broadcast_to([128, 8, 32]),
                                        ALU.mult), t)
            V(lambda e: e.tensor_reduce(cst[:, 1, :], cp[:, :, 0:31], AX, ALU.add))
            V(lambda e: e.tensor_scalar(cst[:, 1, :], cst[:, 1, :], 1e-30, None, ALU.max))
            V(lambda e: e.reciprocal(cst[:, 1, :], cst[:, 1, :]))
            V(lambda e: e.tensor_tensor(cst[:, 2, :], cst[:, 1, :], gat[:, i, 0:24:3], ALU.mult), t_gat)
            t = V(lambda e: e.tensor_tensor(cp[:, :, :], cp[:, :, :], cst[:, 2, :].unsqueeze(2).broadcast_to([128, 8, 32]),
                                            ALU.mult))
            bk, key = banks.take(2)
            PE.wait(t)
            for h in range(8):
                tk = PE(lambda e: transpose(bk[0:32, 128 * h:128 * h + 128], cp[:, h, :]))
            rel_cp = tk
            t = V(lambda e: e.tensor_copy(cpT[:, :, :], bk[0:32, :].rearrange("p (h q) -> p h q", h=8)), tk, rel_cpT)
            banks.free(key, t)
            bk, key = banks.take()
            PE.wait(t)
            for h in range(8):
                g = h // 4
                tk = PE(lambda e: e.matmul(bk[:, 64 * h:64 * h + 64], cpT[0:31, h, :], kcm[0:31, 1, 64 * g:64 * g + 64],
                                           start=True, stop=True))
            rel_cpT = tk
            t = V(lambda e: e.tensor_copy(o2[:, :], bk), tk, rel_on)
            banks.free(key, t)

        def scores2(n):
            i, h, v = its[n]
            j, g, s = h % 4, h // 4, n % 2
            nk = 128 * (i + 1)
            bk, key = banks.take()
            tk = PE(lambda e: e.matmul(bk[:, 0:nk], q2T[:, j, 128 * i:128 * i + 128], kz2[:, g, v, 0:nk],
                                       start=True, stop=True))
            slope = float(np.float32(2.0 ** -(h + 1)))
            if n >= 2:
                V.wait(prev[n - 2])
            V(lambda e: e.scalar_tensor_tensor(sc2[:, s, 0:nk], dist[:, 512 - nk:512], slope, bk[:, 0:nk],
                                               ALU.mult, ALU.add), tk)
            banks.free(key, V.last)
            t = V(lambda e: e.tensor_reduce(st2[:, s, 0:1], sc2[:, s, 0:nk], AX, ALU.max, negate=True))
            prev[n] = A(lambda e: e.activation(p2[:, s, 0:nk], sc2[:, s, 0:nk], ACT.Exp, bias=st2[:, s, 0:1],
                                               accum_out=st2[:, s, 1:2]), t, rel_p[s])

        def values2(n):
            nonlocal rel_on
            i, h, v = its[n]
            g, s = h // 4, n % 2
            nk = 128 * (i + 1)
            bk, key = banks.take()
            PE.wait(prev[n])
            for c in range(i + 1):
                tk = PE(lambda e: transpose(bk[:, 128 * c:128 * c + 128], p2[:, s, 128 * c:128 * c + 128]))
            rel_p[s] = tk
            t = A(lambda e: e.copy(p2T[:, s, 0:nk], bk[:, 0:nk]), tk, rel_pT[s])
            banks.free(key, t)
            bo, ko = banks.take()
            PE.wait(t)
            vt = ksw if v == 0 else kww
            tk = proj(bo[:, 0:128], [(p2T[:, s, 128 * c:128 * c + 128], vt[:, c, 128:256])
                                    for c in range(i + 1)])
            rel_pT[s] = tk
            V(lambda e: e.reciprocal(st2[:, s, 2:3], st2[:, s, 1:2]), prev[n])
            V(lambda e: e.tensor_tensor(st2[:, s, 2:3], st2[:, s, 2:3], gat[:, i, 3 * h + 1 + v:3 * h + 2 + v], ALU.mult))
            oh = o2[:, 64 * h:64 * h + 64]
            t = V(lambda e: e.scalar_tensor_tensor(oh, bo[:, 64 * g:64 * g + 64], st2[:, s, 2:3], oh, ALU.mult, ALU.add), tk)
            banks.free(ko, t)
            if h == 7 and v == 1:
                t = A(lambda e: e.activation(o2n[:, :], o2[:, :], ACT.Square, accum_out=on[:, :]), t, rel_on)
                V.wait(t)
                inv_root(on[:, :], on[:, :], 1.0 / 512)
                t = V(lambda e: e.tensor_scalar(o2n[:, :], o2[:, :], on[:, :], None, ALU.mult))
                bt, kt_ = banks.take()
                PE.wait(t)
                for k in range(4):
                    tk = PE(lambda e: transpose(bt[:, 128 * k:128 * k + 128], o2n[:, 128 * k:128 * k + 128]))
                rel_on = tk
                for k in range(4):
                    t = V(lambda e: e.tensor_scalar(mixT[:, k, 128 * i:128 * i + 128], bt[:, 128 * k:128 * k + 128],
                                                    colA[:, 48 + k:49 + k], None, ALU.mult), tk)
                banks.free(kt_, t)
            return t

        for n in range(65):
            if n < 64:
                scores2(n)
            if n:
                if (n - 1) % 16 == 0:
                    cmp_part((n - 1) // 16)
                t_mix = values2(n - 1)
        t_b2 = PE.last
        if STAGE <= 6:
            return finish(nc, ctx, V, A, SP, sem)

        cv = Region(4096, TOP)
        uh = sb("uh", [128, 4, 514], at=cv)
        vc = sb("vc", [128, 4, 512], at=cv)
        A.wait(t_b2, t_mix)
        V.wait(t_b2)
        V(lambda e: e.memset(uh[:, :, 0:2], 0.0))
        wh = W.get()
        for c in range(4):
            bk, key = banks.take()
            tk = proj(bk, [(wh[:, k, 128 * c:128 * c + 128], hT[:, k, 0:512]) for k in range(8)])
            t = A(lambda e: e.copy(uh[:, c, 2:514], bk), tk)
            banks.free(key, t)
        W.done()
        wh = W.get()
        for c in range(4):
            bk, key = banks.take()
            tk = proj(bk, [(wh[:, k, 128 * c:128 * c + 128], hT[:, k, 0:512]) for k in range(8)])
            V(lambda e: e.tensor_tensor(uh[:, c, 2:514], uh[:, c, 2:514], bk, ALU.mult), tk, t)
            banks.free(key, V.last)
            for tap in range(3):
                w1 = colB[:, 16 + 4 * tap + c:17 + 4 * tap + c]
                if tap == 0:
                    V(lambda e: e.tensor_scalar(vc[:, c, :], uh[:, c, 0:512], w1, None, ALU.mult))
                else:
                    V(lambda e: e.scalar_tensor_tensor(vc[:, c, :], uh[:, c, tap:tap + 512], w1, vc[:, c, :],
                                                       ALU.mult, ALU.add))
        W.done()
        wh = W.get()
        for c in range(4):
            bk, key = banks.take()
            tk = proj(bk, [(wh[:, k, 128 * c:128 * c + 128], hT[:, k, 0:512]) for k in range(8)])
            t = V(lambda e: e.tensor_tensor(vc[:, c, :], vc[:, c, :], bk, ALU.mult), tk)
            banks.free(key, t)
        W.done()
        column_norm(vc, 4, sq, rinv[:, :], t)
        for c in range(4):
            t_mix = V(lambda e: e.scalar_tensor_tensor(mixT[:, 4 + c, :], vc[:, c, :], colA[:, 52 + c:53 + c],
                                                       rinv[:, :], ALU.mult, ALU.mult))
        PE.wait(t_mix)
        for hf in range(2):
            w = W.get()
            for j in range(4):
                dt_ = 4 * hf + j
                bk, key = banks.take()
                tk = proj(bk, [(w[:, k, 128 * j:128 * j + 128], mixT[:, k, :]) for k in range(8)])
                t_x4 = V(lambda e: e.tensor_tensor(xT[:, dt_, :], xT[:, dt_, :], bk, ALU.add), tk)
                banks.free(key, t_x4)
            W.done()
        ff = Region(4096, TOP)
        ut = sb("ut", [128, 32, 512], at=ff)
        column_norm(xT, 8, sq, rinv[:, :], t_x4)
        for k in range(8):
            t_h4 = V(lambda e: e.scalar_tensor_tensor(hT[:, k, 0:512], xT[:, k, :], colA[:, 56 + k:57 + k], rinv[:, :],
                                                      ALU.mult, ALU.mult))
        A.wait(t_h4)
        xo = mixT[:, :, :].rearrange("p (i q) n -> p i q n", q=2)
        for i in range(4):
            for q in range(2):
                bk, key = banks.take()
                PE.wait(t_x4)
                for k in range(4):
                    tk = PE(lambda e: transpose(bk[:, 128 * k:128 * k + 128], xT[:, 4 * q + k, 128 * i:128 * i + 128]))
                t_xo = A(lambda e: e.copy(xo[:, i, q, :], bk), tk)
                banks.free(key, t_xo)
        PE.wait(t_h4)
        for u in range(8):
            w = W.get()
            for j in range(4):
                f = 4 * u + j
                bk, key = banks.take()
                tk = proj(bk, [(w[:, k, 128 * j:128 * j + 128], hT[:, k, 0:512]) for k in range(8)])
                t = A(lambda e: e.activation(ut[:, f, :], bk, ACT.Relu), tk)
                banks.free(key, t)
                t_ut = V(lambda e: e.tensor_tensor(ut[:, f, :], ut[:, f, :], ut[:, f, :], ALU.mult), t)
            W.done()
        PE.wait(t_ut)
        acc = [banks.take() for _ in range(8)]
        for u in range(8):
            w = W.get()
            for b in range(8):
                i, q = b // 2, b % 2
                for k in range(4):
                    f = 4 * u + k
                    mm = lambda e: e.matmul(acc[b][0], ut[:, f, 128 * i:128 * i + 128], w[:, k, 512 * q:512 * q + 512],
                                            start=(f == 0), stop=(f == 31))
                    tk = PE(mm) if k == 3 else mm(nc.tensor)
                if u == 7:
                    t = V(lambda e: e.tensor_tensor(xo[:, i, q, :], xo[:, i, q, :], acc[b][0], ALU.add), tk, t_xo)
                    banks.free(acc[b][1], t)
            W.done()
        s_out = sem("s_out")
        SP.wait(t)
        nc.sync.dma_start(out.rearrange("(i p) n -> p i n", p=128),
                          mixT[:, :, :].rearrange("p (i q) n -> p i (q n)", q=2)).then_inc(s_out, 16)
        SP.wait((s_out, 16))


def finish(nc, ctx, V, A, SP, sem):
    pass


def constants():
    c = {}
    c["k_ident"] = np.eye(128, dtype=np.float32)
    s, t = np.meshgrid(np.arange(128), np.arange(128), indexing="ij")
    m = np.zeros((128, 14, 128), np.float32)
    for i, h in enumerate(LEVELS):
        same = (s // (2 * h)) == (t // (2 * h))
        m[:, i] = same & (s % (2 * h) < h) & (t % (2 * h) >= h)
        m[:, 7 + i] = same & (s % (2 * h) >= h) & (t % (2 * h) < h)
    c["k_masks"] = m
    inv = np.float32(10000.0) ** (-np.arange(0, 32, 2, dtype=np.float32) / np.float32(32))
    tt = np.arange(512)
    ang = np.stack([(tt // 64).astype(np.float32)[:, None] * inv, (tt % 64).astype(np.float32)[:, None] * inv], 1)
    co, si = np.cos(ang), np.sin(ang)
    cs = np.concatenate([co, co], -1).reshape(512, 64)
    sn = np.concatenate([-si, si], -1).reshape(512, 64)
    c["k_rope"] = np.ascontiguousarray(np.stack([cs, sn], 1).reshape(4, 128, 2, 64).transpose(1, 0, 2, 3)).astype(np.float32)
    c["k_iota"] = np.arange(512, dtype=np.float32)
    q, j = np.meshgrid(np.arange(128), np.arange(512), indexing="ij")
    dd = (q + 384 - j).astype(np.float32)
    c["k_dist"] = np.where(dd >= 0, -dd, np.float32(-1e33)).astype(np.float32)
    t4 = (np.arange(4)[None, :, None] * 128 + np.arange(128)[:, None, None]).astype(np.float32)
    dc = t4 - (16 * np.arange(32)[None, None, :] + 31).astype(np.float32)
    dc[:, :, 31] = -1
    slope = np.power(np.float32(2.0), -np.arange(1, 9, dtype=np.float32))
    cb = np.where(dc[:, :, None, :] >= 0, -slope[None, None, :, None] * dc[:, :, None, :], np.float32(-1e30))
    c["k_cb"] = np.ascontiguousarray(cb).astype(np.float32)
    c["k_cm"] = np.ascontiguousarray(dc >= 0).astype(np.float32)
    return c


_FLAT = ["c", "c_ctx", "b_mod", "norm1_g", "norm2_g", "hg_lb_logits", "hg_norm_g", "q_norm_g", "k_norm_g",
         "final_norm_g", "g_mix_norm_2", "g_q_2", "g_k_2", "pe_cmp_2", "b_cmp1_2", "b_cmp2_2", "conv_w_2", "g_out_2",
         "g_ffn_norm_2"]
_FIRST = ["x", "ctx", "w_mod", "w_in", "w_branch_a", "w_branch_b", "w_out", "w_router", "w_exp_gate", "w_exp_up",
          "w_exp_down", "w_in_2", "w_cmp1_2", "w_cmp2_2", "w_o_2", "w_up_2", "w_down_2"]


def kernel(**inputs):
    import concourse.bacc as _bacc
    from concourse.bass_utils import run_bass_kernel_spmd as _run

    nc = _bacc.Bacc("TRN2", target_bir_lowering=False, num_devices=1)
    arrays = {}
    for name in _FLAT:
        arrays[name] = np.ascontiguousarray(inputs[name]).reshape(-1)
    for name in _FIRST:
        a = np.ascontiguousarray(inputs[name])
        arrays[name] = a.reshape(a.shape[1:]) if a.shape[0] == 1 else a
    arrays.update(constants())
    d, sent = {}, {}
    for name, a in arrays.items():
        sent[f"in_{name}_dram"] = a
        d[name] = nc.dram_tensor(f"in_{name}_dram", a.shape, mybir.dt.from_np(a.dtype), kind="ExternalInput").ap()
    out = nc.dram_tensor("out_0_dram", (512, 1024), F32, kind="ExternalOutput").ap()
    program(nc, d, out)
    r = _run(nc, [sent], core_ids=[0])
    return np.asarray(r.results[0]["out_0_dram"]).reshape(1, 512, 1024)
```

```python
from contextlib import ExitStack

import numpy as np

import concourse.bass as bass
from concourse import mybir

F32 = mybir.dt.float32
F32R = mybir.dt.float32r
U8 = mybir.dt.uint8
U32 = mybir.dt.uint32
ALU = mybir.AluOpType
ACT = mybir.ActivationFunctionType
AX = mybir.AxisListType.X

STAGE = 99
NS = 8
LEVELS = [64, 32, 16, 8, 4, 2, 1]
EPS = 1e-6


class Queue:

    def __init__(self, eng, sem, chain):
        self.eng, self.sem, self.chain, self.n, self.seen = eng, sem, chain, 0, {}

    def wait(self, *tokens):
        for t in tokens:
            if t is not None and self.seen.get(t[0].name, 0) < t[1]:
                self.seen[t[0].name] = t[1]
                self.eng.wait_ge(t[0], t[1])

    def __call__(self, fn, *tokens):
        self.wait(*tokens)
        if self.chain and self.n:
            self.wait((self.sem, self.n))
        fn(self.eng).then_inc(self.sem, 1)
        self.n += 1
        return (self.sem, self.n)

    @property
    def last(self):
        return (self.sem, self.n) if self.n else None


def program(nc, d, out):
    with ExitStack() as ctx:
        def sem(name):
            return ctx.enter_context(nc.semaphore(name))

        class Region:

            def __init__(self, tensor, lo, hi):
                self.tensor, self.at, self.hi = tensor, lo, hi

            def take(self, shape, dt):
                size = mybir.dt.size(dt)
                count = int(np.prod(shape[1:]))
                words = -(-count * size // 4)
                assert self.at + words <= self.hi, (shape, self.at, self.hi)
                a = self.tensor[0:shape[0], self.at:self.at + words]
                self.at += words
                if dt != F32:
                    a = a.bitcast(dt)
                if len(shape) > 2:
                    names = "abcdef"[:len(shape) - 1]
                    a = a.rearrange(f"p ({' '.join(names)}) -> p {' '.join(names)}", **dict(zip(names, shape[1:])))
                return a

        ND = 18552
        keep = ctx.enter_context(nc.sbuf_tensor("keep", [128, 9728], F32))
        KEEP, TOP = 4096, 9728

        def sb(name, shape, dt=F32, at=None):
            if at is None:
                return ctx.enter_context(nc.sbuf_tensor(name, shape, dt))
            if isinstance(at, ExitStack):
                return at.enter_context(nc.sbuf_tensor(name, shape, dt))
            return at.take(shape, dt)

        V = Queue(nc.vector, sem("s_v"), True)
        A = Queue(nc.scalar, sem("s_a"), True)
        G = Queue(nc.gpsimd, sem("s_g"), True)
        PE = Queue(nc.tensor, sem("s_pe"), False)
        SP = Queue(nc.sync, sem("s_sp"), False)

        PS = ctx.enter_context(nc.psum_tensor("PS", [128, 8 * 512], F32))

        released = [None] * 8

        class Banks:

            def __init__(self, lo, hi):
                self.lo, self.hi, self.at = lo, hi, lo

            def take(self, n=1):
                if self.at + n > self.hi:
                    self.at = self.lo
                b = self.at
                self.at = b + n if b + n < self.hi else self.lo
                for i in range(b, b + n):
                    assert released[i] != "held", "bank still held"
                    PE.wait(released[i])
                    released[i] = "held"
                return PS[:, b * 512:(b + n) * 512], (b, n)

            def free(self, key, tok):
                for i in range(key[0], key[0] + key[1]):
                    released[i] = tok

        banks = Banks(0, 8)

        def dma(q, dst, src, s, *tokens):
            q.wait(*tokens)
            q.eng.dma_start(dst, src).then_inc(s, 16)
            return (s, 16)

        ring = sb("ring", [128, NS, 2048])
        slot_sem = [sem(f"s_w{i}") for i in range(NS)]

        def cols(w, a, n):
            return (w[:, a:a + n].rearrange("(k p) n -> p k n", p=128), w.shape[0] // 128, n)

        units = [cols(d["w_mod"], 512 * j, 512) for j in range(4)]
        units += [cols(d["w_in"], 2560, 512), cols(d["w_in"], 3072, 256)]
        for n in range(8):
            units += [cols(d["w_in"], (512, 0, 1536, 1024)[n % 4] + 256 * (n // 4), 256),
                      cols(d["w_mod"], 2048 + 512 * n, 512)]
        units += [cols(d["w_in"], 2048, 512)]
        for a, wb in ((3328, "w_branch_a"), (4352, "w_branch_b")):
            units += [cols(d[wb], 0, 1024), cols(d["w_in"], a, 512), cols(d["w_in"], a + 512, 512)]
        units += [cols(d["w_out"], 0, 512), cols(d["w_out"], 512, 512)]
        for p in range(8):
            for name in ("w_exp_gate", "w_exp_up", "w_exp_down"):
                for hf in range(2):
                    for kh in range(2):
                        units += [cols(d[name][2 * p + e2][512 * kh:512 * kh + 512, :], 512 * hf, 512)
                                  for e2 in range(2)]
        w2 = d["w_in_2"]
        units += [cols(w2, 512, 512), cols(w2, 0, 512), cols(w2, 1024, 280)]
        units += [cols(w2, 1304, 512), cols(w2, 1816, 512), cols(w2, 2328, 512)]
        units += [cols(d["w_cmp1_2"][0], 0, 256), cols(d["w_cmp1_2"][1], 0, 256)]
        units += [cols(d["w_o_2"], 0, 512), cols(d["w_o_2"], 512, 512)]
        ups = [cols(d["w_up_2"], 512 * j, 512) for j in range(8)]
        downs = [cols(d["w_down_2"][512 * j:512 * j + 512, :], 0, 1024) for j in range(8)]
        units += ups[:1] + [u for pair in zip(ups[1:], downs) for u in pair] + downs[7:]

        class Stream:

            def __init__(self):
                self.loaded, self.got, self.freed = 0, 0, 0
                self.pos, at = [], 0
                for _, k, n in units:
                    self.pos.append(at)
                    at += 1 if k * n <= 2048 and k == 4 else 2
                self.pos.append(at)
                self.count, self.need = [0] * NS, []
                for i in range(len(units)):
                    s = self.pos[i] % NS
                    self.count[s] += 16
                    self.need.append((slot_sem[s], self.count[s]))

            def load(self, tok=None):
                read = self.pos[self.freed]
                while self.loaded < len(units) and self.pos[self.loaded + 1] - NS <= read:
                    i = self.loaded
                    SP.wait(tok)
                    nc.sync.dma_start(self.view(i), units[i][0]).then_inc(self.need[i][0], 16)
                    self.loaded += 1

            def view(self, i):
                _, k, n = units[i]
                a = ring[:, :, :].rearrange("p s n -> p (s n)")
                o = self.pos[i] % NS * 2048
                return a[:, o:o + k * n].rearrange("p (k n) -> p k n", k=k)

            def get(self, *queues):
                i = self.got
                assert i < self.loaded
                for q in queues or (PE,):
                    q.wait(self.need[i])
                self.got += 1
                return self.view(i)

            def done(self, tok=None):
                self.freed = self.got
                self.load(tok or PE.last)

        W = Stream()

        ident = sb("ident", [128, 128])
        ones = sb("ones", [128, 128])
        rows = sb("rows", [128, 2, 128])
        colA = sb("colA", [128, 128])
        colB = sb("colB", [128, 64])
        gb = sb("gb", [128, 8, 64])
        masks = sb("masks", [128, 14, 128], U8)
        small = [sem(f"s_c{i}") for i in range(8)]
        s_rows, s_gb = sem("s_rows"), sem("s_gb")
        t_ones = V(lambda e: e.memset(ones[:, :], 1.0))
        t_rows0 = V(lambda e: e.memset(rows[:, :, :], 0.0))
        n = 0
        for t, name, k in ((0, "c", 8), (0, "c_ctx", 8), (0, "norm1_g", 8), (0, "norm2_g", 8), (0, "final_norm_g", 8),
                           (0, "g_mix_norm_2", 8), (0, "g_out_2", 8), (0, "g_ffn_norm_2", 8), (0, "b_mod", 48),
                           (0, "hg_norm_g", 4), (1, "hg_lb_logits", 16), (1, "conv_w_2", 12), (1, "b_cmp1_2", 4),
                           (1, "pe_cmp_2", 32)):
            if n == 10:
                at = 0
            at = 0 if n == 0 else at
            A.wait(t_rows0)
            nc.scalar.dma_start(rows[at:at + k, t, :], d[name].rearrange("(r p) -> r p", p=128)).then_inc(s_rows, 16)
            at += k
            n += 1
        t_rows = (s_rows, 16 * n)
        t_ident = dma(A, ident[:, :], d["k_ident"], small[0])
        ngb = 0
        for i, (name, o) in enumerate((("q_norm_g", 0), ("k_norm_g", 0), ("g_q_2", 0), ("g_k_2", 0), ("g_k_2", 64),
                                       ("g_k_2", 128), ("b_cmp2_2", 0), ("b_cmp2_2", 64))):
            nc.scalar.dma_start(gb[:, i, :], d[name][o:o + 64].partition_broadcast(128)).then_inc(s_gb, 16)
            ngb += 1
        t_gb = (s_gb, 16 * ngb)
        hctx, phase = ExitStack(), ExitStack()
        ss = sb("ss", [128, 8])
        A1 = sb("A1", [128, 2, 8])
        mrow = sb("mrow", [128, 512])
        sil = sb("sil", [128, 2, 8])
        modc = sb("modc", [128, 48, 2])
        AB = sb("AB", [128, 3, 8])
        hT = sb("hT", [128, 8, 768], at=hctx)
        dyn = sb("dyn1", [128, ND], at=phase)
        base = Region(dyn, 0, ND)
        mstage = sb("mstage", [128, 14, 128], at=base)
        t_mst = dma(A, mstage, d["k_masks"], small[1])

        PE.wait(t_ident, t_rows)

        def transpose(dst, src, k=128):
            return nc.tensor.transpose(dst, src, ident[0:k, 0:k])

        bk, key = banks.take()
        transpose(bk[:, 0:128], rows[:, 0, :])
        tk = PE(lambda e: transpose(bk[:, 128:192], rows[0:64, 1, :], 64))
        V(lambda e: e.tensor_copy(colA[:, :], bk[:, 0:128]), tk)
        t_col = V(lambda e: e.tensor_copy(colB[:, :], bk[:, 128:192]))
        banks.free(key, t_col)
        t_masks = V(lambda e: e.tensor_copy(masks[:, :, :], mstage), t_mst)
        SP.wait(t_rows)
        W.load()

        cc = colA[:, 0:16].rearrange("p (s k) -> p s k", s=2)
        tk = A(lambda e: e.activation(sil[:, :, :], cc, ACT.Sigmoid), t_col)
        t_sil = V(lambda e: e.tensor_tensor(sil[:, :, :], sil[:, :, :], cc, ALU.mult), tk)
        bmod = colA[:, 64:112]

        V(lambda e: e.memset(mrow[:, :], 0.0))

        def modulation(j0, nu):
            PE.wait(t_sil)
            for u in range(nu):
                bk, key = banks.take()
                w = W.get()
                for k in range(8):
                    r = 32 * (k % 4)
                    mm = lambda e: e.matmul(bk[r:r + 2, :], sil[:, :, k], w[:, k, :], start=(k < 4), stop=(k >= 4))
                    tk = PE(mm) if k >= 4 else mm(nc.tensor)
                W.done()
                V.wait(modulation.free)
                for c in range(4):
                    t = V(lambda e: e.tensor_copy(mrow[32 * c:32 * c + 2, :], bk[32 * c:32 * c + 2, :]), tk)
                banks.free(key, t)
                bt, kt_ = banks.take()
                PE.wait(t)
                for j in range(4):
                    modulation.free = PE(lambda e: transpose(bt[:, 128 * j:128 * j + 128], mrow[:, 128 * j:128 * j + 128]))
                o = modc[:, j0 + 4 * u:j0 + 4 * u + 4, :]
                V(lambda e: e.tensor_reduce(o, bt.rearrange("p (j c x) -> p j x c", j=4, c=4)[:, :, 0:2, :], AX, ALU.add),
                  modulation.free)
                banks.free(kt_, V.last)
                t = V(lambda e: e.tensor_tensor(o, o, bmod[:, j0 + 4 * u:j0 + 4 * u + 4].unsqueeze(2)
                                                .broadcast_to([128, 4, 2]), ALU.add))
            return t

        modulation.free = None

        def inv_root(dst, src, scale):
            t = V(lambda e: e.tensor_scalar(dst, src, scale, EPS, ALU.mult, ALU.add))
            t = A(lambda e: e.activation(dst, dst, ACT.Sqrt), t)
            return V(lambda e: e.reciprocal(dst, dst), t)

        sem_dbg = [0]
        xt = sb("xt", [128, 6, 1024], at=base)
        sqj = sb("sqj", [128, 1024], at=base)
        s_x = sem("s_x")
        nc.gpsimd.dma_start(xt[:, 0:2, :], d["ctx"].rearrange("(t p) n -> p t n", p=128)).then_inc(s_x, 16)
        nc.gpsimd.dma_start(xt[:, 2:6, :], d["x"].rearrange("(t p) n -> p t n", p=128)).then_inc(s_x, 16)
        for i in range(6):
            tk = A(lambda e, i=i: e.activation(sqj[:, :], xt[:, i, :], ACT.Square, accum_out=ss[:, i:i + 1]), (s_x, 32))
        V.wait(tk)
        inv_root(ss[:, 0:6], ss[:, 0:6], 1.0 / 1024)
        for i in range(6):
            t_xn = V(lambda e, i=i: e.tensor_scalar(xt[:, i, :], xt[:, i, :], ss[:, i:i + 1], None, ALU.mult))
        t_mod = modulation(0, 4)
        for s in range(2):
            t_A1 = V(lambda e, s=s: e.scalar_tensor_tensor(A1[:, s, :], modc[:, 8:16, s], 1.0, colA[:, 16:24],
                                                           ALU.add, ALU.mult))
        PE.wait(t_xn)
        for k in range(8):
            b1, k1 = banks.take()
            for i in range(4):
                mm = lambda e, i=i: transpose(b1[:, 128 * i:128 * i + 128], xt[:, 2 + i, 128 * k:128 * k + 128])
                tk = PE(mm) if i == 3 else mm(nc.tensor)
            t1 = V(lambda e: e.tensor_scalar(hT[:, k, 256:768], b1, A1[:, 0, k:k + 1], modc[:, k, 0:1],
                                             ALU.mult, ALU.add), tk)
            banks.free(k1, t1)
            b2, k2 = banks.take()
            transpose(b2[:, 0:128], xt[:, 0, 128 * k:128 * k + 128])
            tk = PE(lambda e: transpose(b2[:, 128:256], xt[:, 1, 128 * k:128 * k + 128]))
            A.wait(t_A1)
            t2 = A(lambda e: e.activation(hT[:, k, 0:256], b2[:, 0:256], ACT.Identity, bias=modc[:, k, 1:2],
                                          scale=A1[:, 1, k:k + 1]), tk)
            banks.free(k2, t2)
        t_xt_free = PE.last
        PE.wait(t1, t2)

        def proj(dst, pairs):
            m = len(pairs)
            for i, (l, r) in enumerate(pairs):
                f = lambda e, l=l, r=r, i=i: e.matmul(dst, l, r, start=(i == 0), stop=(i == m - 1))
                if i == m - 1:
                    return PE(f)
                f(nc.tensor)

        if STAGE <= 1:
            return finish(nc, ctx, V, A, SP, sem)

        slot2 = Region(keep, 0, KEEP)
        oattT = sb("oattT", [128, 4, 512], at=slot2)
        oT = sb("oT", [128, 4, 512], at=slot2)
        att, att2 = Region(keep, KEEP, TOP), Region(dyn, 0, ND)
        qT = sb("qT", [128, 4, 512], at=att)
        kz = sb("kz", [128, 2, 768], at=att)
        avs = sb("avs", [128, 6, 128], at=att2)
        pb = sb("pb", [128, 2, 768], at=att)
        pT = sb("pT", [128, 2, 768], at=att2)
        ot = sb("ot", [128, 2, 512], at=att2)
        st = sb("st", [128, 4, 3], at=att2)
        hg = Region(dyn, att2.at, ND)
        qh = sb("qh", [128, 2, 512], at=hg)
        vh = sb("vh", [128, 6, 256], at=hg)
        KK = sb("KK", [128, 2, 768], at=hg)
        GG = sb("GG", [128, 2, 768], at=hg)
        LF = sb("LF", [128, 2, 768], at=hg)
        lbt = sb("lbt", [128, 6, 8], at=hg)
        reset = sb("reset", [128, 768], U8, at=hg)
        dec = sb("dec", [128, 2, 6], at=hg)
        pre = Region(dyn, hg.at, ND)
        X1 = sb("X1", [128, 2, 512], at=hg)
        Ys = [sb(f"Y{i}", [128, 2, 512], at=hg) for i in range(2)]
        SS = sb("SS", [128, 4, 2, 128], at=hg)
        qe = sb("qe", [128, 2, 512], at=hg)
        keT = sb("keT", [128, 5, 256], at=hg)
        St = sb("St", [128, 5, 256], at=hg)
        Xs = [keT[:, 0:4, :].rearrange("p a b -> p (a b)").rearrange("p (h t) -> p h t", h=2), X1]
        aq = sb("aq", [128, 4, 512], at=pre)
        akv = sb("akv", [128, 6, 128], at=pre)
        rope = sb("rope", [128, 4, 2, 64], at=pre)
        tA = sb("tA", [128, 2048], at=pre)
        tC = sb("tC", [128, 2, 512], at=pre)
        rr = sb("rr", [128, 32], at=pre)
        V.wait(t_xt_free)
        A.wait(t_xt_free)
        t_kz = G(lambda e: e.memset(kz[:, :, :], 0.0), t_xt_free)
        t_rope = dma(A, rope[:, :, :, :], d["k_rope"], small[3], t1)

        w = W.get()
        for i in range(4):
            bk, key = banks.take()
            tk = proj(bk, [(hT[:, k, 256 + 128 * i:384 + 128 * i], w[:, k, :]) for k in range(8)])
            t_aq = A(lambda e: e.copy(aq[:, i, :], bk), tk)
            banks.free(key, t_aq)
        W.done()
        w = W.get()
        for i in range(6):
            bk, key = banks.take()
            tk = proj(bk[:, 0:256], [(hT[:, k, 128 * i:128 * i + 128], w[:, k, :]) for k in range(8)])
            A(lambda e: e.copy(akv[:, i, :], bk[:, 0:128]), tk)
            t_ak = A(lambda e: e.copy(avs[:, i, :], bk[:, 128:256]))
            banks.free(key, t_ak)
        W.done()

        def head_norm(src, nt, nh, gain, scale, *tokens):
            n = nt * nh
            flat = src.rearrange("p t h e -> p (t h) e") if nt > 1 and nh == 8 else None
            sq4 = tA[:, 0:64 * n].rearrange("p (t h e) -> p t h e", h=nh, e=64)
            V(lambda e: e.tensor_tensor(sq4, src, src, ALU.mult), *tokens)
            V(lambda e: e.tensor_reduce(rr[:, 0:n], tA[:, 0:64 * n].rearrange("p (n e) -> p n e", e=64), AX, ALU.add))
            inv_root(rr[:, 0:n], rr[:, 0:n], 1.0 / 64)
            r4 = rr[:, 0:n].rearrange("p (t h) -> p t h", h=nh).unsqueeze(3).broadcast_to([128, nt, nh, 64])
            V(lambda e: e.tensor_tensor(src, src, r4, ALU.mult))
            g4 = gain.unsqueeze(1).unsqueeze(1).broadcast_to([128, nt, nh, 64])
            t = V(lambda e: e.tensor_tensor(src, src, g4, ALU.mult))
            if scale != 1.0:
                t = V(lambda e: e.tensor_scalar(src, src, scale, None, ALU.mult))
            return t

        def rotate(src, nt, nh, dst):
            s4 = src.rearrange("p t h (a u f) -> p t (h a) u f", a=2, u=2)
            sw = tA[:, 0:64 * nt * nh].rearrange("p (t h u f) -> p t h u f", t=nt, u=2, f=16)
            V(lambda e: e.tensor_copy(sw[:, :, :, 0, :], s4[:, :, :, 1, :]))
            V(lambda e: e.tensor_copy(sw[:, :, :, 1, :], s4[:, :, :, 0, :]))
            a4 = tA[:, 0:64 * nt * nh].rearrange("p (t h e) -> p t h e", h=nh, e=64)
            sn = rope[:, :, 1, :].unsqueeze(2).broadcast_to([128, nt, nh, 64])
            cs = rope[:, :, 0, :].unsqueeze(2).broadcast_to([128, nt, nh, 64])
            V(lambda e: e.tensor_tensor(a4, a4, sn, ALU.mult))
            V(lambda e: e.tensor_tensor(src, src, cs, ALU.mult))
            for i in range(nt):
                yield dst(i, src[:, i], a4[:, i])

        def attention1():
            its = [(i, h) for i in range(4) for h in range(8)]
            e_done, rel_p, t_pT, rel_pT, rel_ot = {}, {}, {}, {}, {}
            PE.wait(t_qT)
            for n in range(34):
                if n < 32:
                    i, h = its[n]
                    s = n % 2
                    bk, key = banks.take(2)
                    qq = qT[:, h % 4, 128 * i:128 * i + 128]
                    nc.tensor.matmul(bk[:, 0:512], qq, kz[:, h // 4, 0:512], start=True, stop=True)
                    tk = PE(lambda e: e.matmul(bk[:, 512:768], qq, kz[:, h // 4, 512:768], start=True, stop=True))
                    t = V(lambda e: e.tensor_reduce(st[:, n % 4, 0:1], bk[:, 0:768], AX, ALU.max, negate=True), tk)
                    t = A(lambda e: e.activation(pb[:, s, :], bk[:, 0:768], ACT.Exp, bias=st[:, n % 4, 0:1],
                                                 accum_out=st[:, n % 4, 1:2]), t, rel_p.get(n - 2))
                    banks.free(key, t)
                    e_done[n] = t
                    yield
                if 1 <= n < 33:
                    m = n - 1
                    bk, key = banks.take(2)
                    PE.wait(e_done[m])
                    for c in range(6):
                        mm = lambda e: transpose(bk[:, 128 * c:128 * c + 128], pb[:, m % 2, 128 * c:128 * c + 128])
                        tk = PE(mm) if c == 5 else mm(nc.tensor)
                    rel_p[m] = tk
                    t = A(lambda e: e.copy(pT[:, m % 2, :], bk[:, 0:768]), tk, rel_pT.get(m - 2))
                    banks.free(key, t)
                    t_pT[m] = t
                if n >= 2:
                    m = n - 2
                    i, h = its[m]
                    g = h // 4
                    bo, ko = banks.take()
                    PE.wait(t_pT[m])
                    tk = proj(bo[:, 0:128], [(pT[:, m % 2, 128 * c:128 * c + 128], avs[:, c, :]) for c in range(6)])
                    rel_pT[m] = tk
                    V(lambda e: e.reciprocal(st[:, m % 4, 2:3], st[:, m % 4, 1:2]), e_done[m])
                    t = V(lambda e: e.tensor_scalar(ot[:, i % 2, 64 * h:64 * h + 64], bo[:, 64 * g:64 * g + 64],
                                                    st[:, m % 4, 2:3], None, ALU.mult), tk, rel_ot.get(i - 2))
                    banks.free(ko, t)
                    if h == 7:
                        bt, kt_ = banks.take()
                        PE.wait(t)
                        for j in range(4):
                            mm = lambda e: transpose(bt[:, 128 * j:128 * j + 128], ot[:, i % 2, 128 * j:128 * j + 128])
                            tk = PE(mm) if j == 3 else mm(nc.tensor)
                        rel_ot[i] = tk
                        t = A(lambda e: e.copy(oattT[:, :, 128 * i:128 * i + 128],
                                               bt.rearrange("p (j q) -> p j q", j=4)), tk)
                        banks.free(kt_, t)
                yield

        lb, omlb = lbt[:, 4, :], lbt[:, 5, :]
        lg = colB[:, 0:16].rearrange("p (r l h) -> p r l h", r=2, l=2)
        l3 = lbt[:, :, :].rearrange("p i (r h) -> p i r h", r=2)
        V(lambda e: e.tensor_tensor(l3[:, 0], lg[:, :, 0, :], lg[:, :, 1, :], ALU.max))
        V(lambda e: e.tensor_tensor(l3[:, 1], lg[:, :, 0, :], l3[:, 0], ALU.subtract))
        t = V(lambda e: e.tensor_tensor(l3[:, 2], lg[:, :, 1, :], l3[:, 0], ALU.subtract))
        t = A(lambda e: e.activation(lbt[:, 1:3, :], lbt[:, 1:3, :], ACT.Exp), t)
        V(lambda e: e.tensor_tensor(lbt[:, 3, :], lbt[:, 1, :], lbt[:, 2, :], ALU.add), t)
        V(lambda e: e.reciprocal(lbt[:, 3, :], lbt[:, 3, :]))
        V(lambda e: e.tensor_tensor(lb, lbt[:, 1, :], lbt[:, 3, :], ALU.mult))
        V(lambda e: e.tensor_tensor(omlb, lbt[:, 2, :], lbt[:, 3, :], ALU.mult))
        V(lambda e: e.memset(reset[:, :], 1))
        V(lambda e: e.memset(reset[:, 0:768:128], 0))

        level_banks = Banks(6, 8)
        t_mods = []

        def scan():
            t_of = None
            t_y = [None, None]
            for hp in range(2):
                for r in range(2):
                    w = W.get()
                    A.wait(V.last, G.last, PE.last)
                    for h in range(2):
                        bk, key = banks.take(2)
                        proj(bk[:, 0:512], [(w[:, k, 128 * h:128 * h + 128], hT[:, k, 256:768]) for k in range(8)])
                        tk = proj(bk[:, 512:768], [(w[:, k, 128 * h:128 * h + 128], hT[:, k, 0:256]) for k in range(8)])
                        for dst, sc in ((LF, 1.0), (KK, -1.0)):
                            A(lambda e: e.activation(dst[:, h, 256:768], bk[:, 0:512], ACT.Sigmoid, scale=sc), tk)
                            t = A(lambda e: e.activation(dst[:, h, 0:256], bk[:, 512:768], ACT.Sigmoid, scale=sc))
                        banks.free(key, t)
                        yield
                    W.done()
                    modulation(16 + 4 * (4 * hp + 3 * r), 1)
                    for h in range(2):
                        i = 4 * r + 2 * hp + h
                        V(lambda e: e.tensor_scalar(LF[:, h, :], LF[:, h, :], omlb[:, i:i + 1], lb[:, i:i + 1],
                                                    ALU.mult, ALU.add), t)
                        t_kk = V(lambda e: e.tensor_scalar(KK[:, h, :], KK[:, h, :], omlb[:, i:i + 1], None, ALU.mult))
                    t = A(lambda e: e.activation(LF[:, :, :], LF[:, :, :], ACT.Ln), t_kk)
                    yield
                    if r == 0:
                        w = W.get()
                        A.wait(V.last, PE.last)
                        for h in range(2):
                            bk, key = banks.take()
                            tk = proj(bk, [(w[:, k, 128 * h:128 * h + 128], hT[:, k, 256:768]) for k in range(8)])
                            t_q = A(lambda e: e.copy(qh[:, h, :], bk), tk)
                            banks.free(key, t_q)
                        W.done()
                        yield
                        modulation(20 + 16 * hp, 1)
                    for h in range(2):
                        t_scan = V(lambda e: e.tensor_tensor_scan(GG[:, h, :], reset[:, :], LF[:, h, :], 0.0,
                                                                  ALU.mult, ALU.add), t)
                    t_dec = V(lambda e: e.tensor_copy(
                        dec[:, :, :], GG[:, :, :].rearrange("p h (c t) -> p h c t", t=128)[:, :, :, 127]))
                    t_gg = t_dec
                    if r == 1:
                        t_gg = G(lambda e: e.tensor_tensor(GG[:, :, :], GG[:, :, :], LF[:, :, :], ALU.subtract), t_dec)
                    if r == 0:
                        w = W.get()
                        for i in range(6):
                            bk, key = banks.take()
                            tk = proj(bk[:, 0:256], [(hT[:, k, 128 * i:128 * i + 128], w[:, k, :]) for k in range(8)])
                            t_v = A(lambda e: e.copy(vh[:, i, :], bk[:, 0:256]), tk)
                            banks.free(key, t_v)
                            if i % 3 == 2:
                                yield
                        W.done()
                        t_mods.append(modulation(24 + 16 * hp, 1))
                    V.wait(*t_pre, t_q)
                    A.wait(*t_pre)
                    G.wait(*t_pre)
                    T6 = dec[:, :, :].unsqueeze(3).broadcast_to([128, 2, 6, 128])
                    G6 = GG[:, :, :].rearrange("p h (c t) -> p h c t", t=128)
                    L6 = LF[:, :, :].rearrange("p h (c t) -> p h c t", t=128)
                    if r == 0:
                        t = A(lambda e: e.activation(X1[:, :, :], GG[:, :, 256:768], ACT.Exp), t_gg, V.last)
                        tl = G(lambda e: e.tensor_tensor(L6, T6, G6, ALU.subtract), t_dec)
                        tl = A(lambda e: e.activation(LF[:, :, :], LF[:, :, :], ACT.Exp), tl)
                    else:
                        t = G(lambda e: e.tensor_tensor(X1[:, :, :].rearrange("p h (c t) -> p h c t", t=128),
                                                        T6[:, :, 2:6, :], G6[:, :, 2:6, :], ALU.subtract), V.last)
                        tl = A(lambda e: e.activation(LF[:, :, :], GG[:, :, :], ACT.Exp), t_gg)
                        t = A(lambda e: e.activation(X1[:, :, :], X1[:, :, :], ACT.Exp), t)
                    V.wait(PE.last)
                    t_qe = V(lambda e: e.tensor_tensor(qe[:, :, :], X1[:, :, :], qh[:, :, :], ALU.mult), t)
                    t_ke = V(lambda e: e.tensor_tensor(LF[:, :, :], LF[:, :, :], KK[:, :, :], ALU.mult), tl)
                    t_dec = A(lambda e: e.activation(dec[:, :, :], dec[:, :, :], ACT.Exp), t_qe)
                    yield
                    order = [0, 1, 2, 3, 4] if r == 0 else [1, 0, 5, 4, 3]
                    A.wait(V.last)
                    for n0 in range(0, 5, 2):
                        cs = order[n0:n0 + 2]
                        bk, key = banks.take()
                        PE.wait(t_ke)
                        for a, c in enumerate(cs):
                            for h in range(2):
                                o = 256 * a + 128 * h
                                mm = lambda e: transpose(bk[:, o:o + 128], LF[:, h, 128 * c:128 * c + 128])
                                tk = PE(mm) if h == 1 else mm(nc.tensor)
                        m = len(cs)
                        t_keT = A(lambda e: e.copy(keT[:, n0:n0 + m, :],
                                                   bk[:, 0:256 * m].rearrange("p (a x) -> p a x", a=m)), tk)
                        banks.free(key, t_keT)
                    for c0 in range(0, 4, 2):
                        bk, key = banks.take()
                        PE.wait(t_q, t_kk)
                        for a in range(2):
                            for h in range(2):
                                c, o = c0 + a, 256 * a + 128 * h
                                mm = lambda e: e.matmul(bk[:, o:o + 128], KK[:, h, 256 + 128 * c:384 + 128 * c],
                                                        qh[:, h, 128 * c:128 * c + 128], start=True, stop=True)
                                tk = PE(mm) if a + h == 2 else mm(nc.tensor)
                        s4 = SS[:, c0:c0 + 2].rearrange("p c h t -> p (c h) t")
                        b4 = bk.rearrange("p (x t) -> p x t", x=4)
                        id4 = ident[:, :].unsqueeze(1).broadcast_to([128, 4, 128])
                        if r == 0:
                            V(lambda e: e.tensor_tensor(s4, b4, id4, ALU.mult), tk)
                            banks.free(key, V.last)
                        else:
                            y4 = Ys[0][:, :, :].rearrange("p h (x t) -> p (h x) t", t=128)[:, 4 * (c0 // 2):4 * (c0 // 2) + 4]
                            V(lambda e: e.tensor_tensor(y4, b4, id4, ALU.mult), tk)
                            banks.free(key, V.last)
                            V(lambda e: e.tensor_tensor(s4, s4, y4, ALU.add))
                    yield
                    PE.wait(t_keT, t_v)
                    V.wait(t_dec)
                    for n, c in enumerate(order):
                        bk, key = banks.take()
                        for h in range(2):
                            hs = slice(128 * h, 128 * h + 128)
                            mm = lambda e: e.matmul(bk[:, hs], keT[:, n, hs], vh[:, c, hs], start=True, stop=True)
                            tk = PE(mm) if h == 1 else mm(nc.tensor)
                        if n == 0:
                            t_st = V(lambda e: e.tensor_copy(St[:, 0, :], bk[:, 0:256]), tk)
                        else:
                            for h in range(2):
                                hs = slice(128 * h, 128 * h + 128)
                                t_st = V(lambda e: e.scalar_tensor_tensor(St[:, n, hs], St[:, n - 1, hs],
                                                                          dec[:, h, c:c + 1], bk[:, hs], ALU.mult,
                                                                          ALU.add), tk)
                        banks.free(key, t_st)
                        if n == 2:
                            yield
                    t_keT_read = tk
                    yield
                    t_x, t_mul, t_mm, got = {}, {-2: t_keT_read, -1: t_qe}, {}, {}

                    def views(l):
                        m = LEVELS[l]
                        v = lambda a: a.rearrange("p h (b u m) -> p h b u m", u=2, m=m)
                        return m, v(Xs[l % 2]), v(GG[:, :, 256:768]), v(KK[:, :, 256:768]), v(qh[:, :, :]), v(Ys[l % 2])

                    def exponents(l):
                        m, xv, gv, _, _, _ = views(l)
                        ref = gv[:, :, :, 0, m - 1:m] if r == 0 else gv[:, :, :, 1, 0:1]
                        ref = ref.broadcast_to([128, 2, 256 // m, m])
                        G(lambda e: e.tensor_tensor(xv[:, :, :, 0, :], ref, gv[:, :, :, 0, :], ALU.subtract),
                          t_mul[l - 2], t_gg)
                        t = G(lambda e: e.tensor_tensor(xv[:, :, :, 1, :], gv[:, :, :, 1, :], ref, ALU.subtract))
                        t_x[l] = A(lambda e: e.activation(Xs[l % 2], Xs[l % 2], ACT.Exp), t)

                    def select(l):
                        mk = masks[:, 7 * r + l, :].unsqueeze(1).broadcast_to([128, 4, 128])
                        for a in range(2):
                            bk, key, tk = got[l][a]
                            t = V(lambda e: e.copy_predicated(SS[:, 2 * a:2 * a + 2].rearrange("p c h t -> p (c h) t"),
                                                              mk, bk.rearrange("p (x t) -> p x t", x=4)), tk, t_masks)
                            banks.free(key, t)
                        return t

                    def scale(l):
                        _, xv, _, kv, qv, yv = views(l)
                        a, b = (kv, qv) if r == 0 else (qv, kv)
                        V.wait(t_x[l], t_y[l % 2])
                        V(lambda e: e.tensor_tensor(yv[:, :, :, 0, :], xv[:, :, :, 0, :], a[:, :, :, 0, :], ALU.mult))
                        t_mul[l] = V(lambda e: e.tensor_tensor(yv[:, :, :, 1, :], xv[:, :, :, 1, :], b[:, :, :, 1, :],
                                                               ALU.mult))

                    exponents(0)
                    exponents(1)
                    scale(0)
                    yield
                    for l in range(len(LEVELS)):
                        if l + 2 < len(LEVELS):
                            exponents(l + 2)
                        if l:
                            select(l - 1)
                        if l + 1 < len(LEVELS):
                            scale(l + 1)
                        PE.wait(t_mul[l])
                        got[l] = []
                        for a in range(2):
                            bk, key = level_banks.take()
                            for x in range(4):
                                c, h = 2 * a + x // 2, x % 2
                                yy = Ys[l % 2][:, h, 128 * c:128 * c + 128]
                                mm = lambda e: e.matmul(bk[:, 128 * x:128 * x + 128], yy, yy, start=True, stop=True)
                                tk = PE(mm) if x == 3 else mm(nc.tensor)
                            got[l].append((bk, key, tk))
                        t_y[l % 2] = tk
                        yield
                    t_ss = select(len(LEVELS) - 1)
                    PE.wait(t_st, t_qe, t_ss)
                    for c0 in range(0, 4, 2):
                        bk, key = banks.take()
                        for a in range(2):
                            for h in range(2):
                                c, o, hs = c0 + a, 256 * a + 128 * h, slice(128 * h, 128 * h + 128)
                                qc = qe[:, h, 128 * c:128 * c + 128]
                                if r == 0:
                                    tk = proj(bk[:, o:o + 128], [(St[:, 1 + c, hs], qc)])
                                else:
                                    tk = proj(bk[:, o:o + 128], [(vh[:, 2 + c, hs], SS[:, c, h, :]),
                                                                 (St[:, 4 - c, hs], qc)])
                        ov = oT[:, 2 * hp:2 * hp + 2, 128 * c0:128 * c0 + 256].rearrange("p h (a t) -> p a h t", a=2)
                        b4 = bk.rearrange("p (a h t) -> p a h t", a=2, h=2)
                        if r == 0:
                            t_of = A(lambda e: e.copy(ov, b4), tk)
                            banks.free(key, t_of)
                        else:
                            banks.free(key, V(lambda e: e.tensor_tensor(ov, b4, ov, ALU.add), tk, t_of))
                    yield

        two = scan()
        next(two)
        next(two)
        V.wait(t_gb, t_rope)
        k4 = akv[:, :, :].rearrange("p t (h e) -> p t h e", e=64)
        t_k = head_norm(k4, 6, 2, gb[:, 1, :], 1.0, t_ak)
        for t_k in rotate(k4[:, 2:6], 4, 2, lambda i, a, b: V(lambda e: e.tensor_tensor(a, a, b, ALU.add))):
            pass
        for i in range(6):
            bk, key = banks.take()
            tk = PE(lambda e: transpose(bk[:, 0:128], akv[:, i, :]), t_k)
            for g in range(2):
                gs = slice(64 * g, 64 * g + 64)
                t = A(lambda e: e.copy(kz[gs, g, 128 * i:128 * i + 128], bk[gs, 0:128]), tk, t_kz)
            banks.free(key, t)
        next(two)
        q4 = aq[:, :, :].rearrange("p t (h e) -> p t h e", e=64)
        head_norm(q4, 4, 8, gb[:, 0, :], 0.125, t_aq)
        rel_tC = [None, None]
        next(two)

        def put_q(i, a, b):
            o = tC[:, i % 2, :].rearrange("p (j g e) -> p g j e", g=2, e=64)
            t = V(lambda e: e.tensor_tensor(o, a.rearrange("p (g j) e -> p g j e", g=2),
                                            b.rearrange("p (g j) e -> p g j e", g=2), ALU.add), rel_tC[i % 2])
            bk, key = banks.take()
            PE.wait(t)
            for j in range(4):
                mm = lambda e: transpose(bk[:, 128 * j:128 * j + 128], tC[:, i % 2, 128 * j:128 * j + 128])
                tk = PE(mm) if j == 3 else mm(nc.tensor)
            rel_tC[i % 2] = tk
            t = A(lambda e: e.copy(qT[:, :, 128 * i:128 * i + 128], bk.rearrange("p (j q) -> p j q", j=4)), tk)
            banks.free(key, t)
            return t

        for n, t_qT in enumerate(rotate(q4, 4, 8, put_q)):
            if n == 1:
                next(two)
        t_pre = (V.last, A.last, PE.last)

        banks.hi, banks.at = 6, 0
        one = attention1()
        more = [one, two]
        while more:
            for g_ in list(more):
                if g_ in more and next(g_, "end") == "end":
                    more = [x for x in more if x is not g_]
        t_oatt = t_o = (V.sem, V.n)
        t_hg_pe = PE.last
        t_hg_a = A.last
        banks.hi = 8

        def handover():
            last = (V.last, A.last, G.last, PE.last)
            for q in (V, A, G):
                q.wait(*last)

        def split(dst, src, *tokens, hi=None):
            t = (hi or A)(lambda e: e.copy(dst[0], src) if (hi or A) is A else e.tensor_copy(dst[0], src), *tokens)
            return V(lambda e: e.tensor_tensor(dst[1], src, dst[0].bitcast(F32), ALU.subtract), t)

        def split_scaled(dst, src, col, *tokens):
            t = A(lambda e: e.activation(dst[0], src, ACT.Copy, scale=col), *tokens)
            return V(lambda e: e.scalar_tensor_tensor(dst[1], src, col, dst[0].bitcast(F32), ALU.mult, ALU.subtract), t)

        class Parts:

            def __init__(self, tensor):
                self.t, self.n, self.free = tensor, 0, [None, None]

            def put(self, src):
                a, b = src.shape[1], src.shape[2]
                i = self.n % 2
                self.n += 1
                out = [self.t[:, i, x, 0:a * b].rearrange("p (a b) -> p a b", b=b) for x in range(2)]
                tok = split(out, src, self.free[i])
                return out, tok, i

        def run(parts, items):
            ahead = []
            for n in range(len(items) + 1):
                if n < len(items):
                    get, free, use = items[n]
                    out, tok, i = parts.put(get())
                    if free:
                        W.done(tok)
                    ahead.append((out, tok, i, use))
                if n:
                    out, tok, i, use = ahead.pop(0)
                    PE.wait(tok)
                    use(out)
                    parts.free[i] = PE.last

        def products(dst, w, x, ks, first=True, last=True, ready=None):
            m = len(ks)
            for n, k in enumerate(ks):
                if ready:
                    PE.wait(ready[k])
                for j, (a, b) in enumerate(((0, 0), (0, 1), (1, 0))):
                    f = lambda e: e.matmul(dst, w(a, k), x(b, k), start=(first and n == 0 and j == 0),
                                           stop=(last and n == m - 1 and j == 2))
                    tk = PE(f) if n == m - 1 and j == 2 else f(nc.tensor)
            return tk

        def column_items(slab_cols, nk, xR, evac, ready=None):
            items = []
            state = {}
            total = sum(slab_cols)
            n = 0
            for ncol in slab_cols:
                for j in range(ncol):
                    def get(j=j):
                        if j == 0:
                            state["w"] = W.get(A)
                        return state["w"][:, :, 128 * j:128 * j + 128]

                    def use(out, n=n):
                        bk, key = banks.take()
                        tk = products(bk, lambda a, k: out[a][:, k, :], lambda b, k: xR[b][:, k, :], range(nk),
                                      ready=ready)
                        evac(n, bk, key, tk)
                    items.append((get, j == ncol - 1, use))
                    n += 1
            return items

        t_mod = V.last
        phase.close()
        handover()
        phase = ExitStack()
        hR = sb("hR1", [128, 2, 8, 512], F32R, at=phase)
        wR = sb("wR1", [128, 2, 2, 1024], F32R, at=phase)
        aR = sb("aR1", [128, 2, 4, 512], F32R, at=phase)
        small2 = sb("small2", [128, 2048], at=phase)
        r2 = Region(small2, 0, 2048)
        sg = sb("sg", [128, 2, 512], at=r2)
        rn = sb("rn", [128, 512], at=r2)
        tm = sb("tm", [128, 512], at=r2)
        parts = Parts(wR)
        h2 = (hR[:, 0], hR[:, 1])
        a2 = (aR[:, 0], aR[:, 1])
        PE.wait(t_o, t_hg_a)
        t_hR = [split((hR[:, 0, k], hR[:, 1, k]), hT[:, k, 256:768]) for k in range(8)]
        wr = hT[:, 0, 512:640].rearrange("p (k n) -> p k n", k=8)
        iot = hT[:, 1:3, 512:768]
        s_wr, s_iot = sem("s_wr"), sem("s_iot")
        def out_gate(h, bk, key, tk):
            s = h % 2
            t = A(lambda e: e.activation(sg[:, s, :], bk, ACT.Sigmoid), tk, t_og.get(h - 2))
            t = V(lambda e: e.tensor_tensor(sg[:, s, :], sg[:, s, :], bk, ALU.mult), t)
            banks.free(key, t)
            t = V(lambda e: e.tensor_tensor(tm[:, :], sg[:, s, :], oT[:, h, :], ALU.mult), t_og.get(h - 1))
            t_og[h] = split((aR[:, 0, h], aR[:, 1, h]), tm[:, :], t)

        t_og, t_so = {}, [None, None]
        for h in range(4):
            t = A(lambda e: e.activation(sg[:, h % 2, :], oT[:, h, :], ACT.Square), t_so[h % 2])
            bk, key = banks.take()
            t_so[h % 2] = tk = PE(lambda e: e.matmul(bk, ones[:, :], sg[:, h % 2, :], start=True, stop=True), t)
            rh = (rn, tm)[h % 2]
            t = V(lambda e: e.tensor_scalar(rh[:, :], bk, 1.0 / 128, EPS, ALU.mult, ALU.add), tk)
            banks.free(key, t)
            t = A(lambda e: e.activation(rh[:, :], rh[:, :], ACT.Sqrt), t)
            V(lambda e: e.reciprocal(rh[:, :], rh[:, :]), t)
            t_on = V(lambda e: e.scalar_tensor_tensor(oT[:, h, :], rh[:, :], colA[:, 112 + h:113 + h], oT[:, h, :],
                                                      ALU.mult, ALU.mult))
        A.wait(t_on)

        run(parts, column_items([4], 8, h2, out_gate, t_hR))
        A.wait(t_hR[-1])
        nc.scalar.dma_start(wr, d["w_router"].rearrange("(k p) n -> p k n", p=128)).then_inc(s_wr, 16)
        nc.scalar.dma_start(iot, d["k_iota"].rearrange("(a b) -> a b", a=2).partition_broadcast(128)).then_inc(s_iot, 16)
        uT = hT[:, :, 0:512]
        t_sg = {}

        def branch(br):
            items, state = [], {}
            for dt_ in range(8):
                def get_b(dt_=dt_):
                    return state["b"][:, :, 128 * dt_:128 * dt_ + 128]

                def get_g(dt_=dt_):
                    if dt_ == 0:
                        state["b"] = W.get(A)
                    if dt_ % 4 == 0:
                        state["g"] = W.get(A)
                    return state["g"][:, :, 128 * (dt_ % 4):128 * (dt_ % 4) + 128]

                def use_g(out, dt_=dt_):
                    bk, key = banks.take()
                    tk = products(bk, lambda a, k: out[a][:, k, :], lambda b, k: hR[:, b, k, :], range(8))
                    t_sg[dt_] = A(lambda e: e.activation(sg[:, dt_ % 2, :], bk, ACT.Sigmoid), tk, t_sg.get(("u", dt_ - 2)))
                    banks.free(key, t_sg[dt_])

                def use_b(out, dt_=dt_):
                    bk, key = banks.take()
                    if dt_ == 0:
                        PE.wait(t_a2[br])
                    if br and dt_ == 7:
                        for k in range(7):
                            t_uR.append(split((hR[:, 0, k], hR[:, 1, k]), uT[:, k, :], V.last, PE.last))
                    tk = products(bk, lambda a, k: out[a][:, k, :], lambda b, k: aR[:, b, k, :], range(4))
                    s = dt_ % 2
                    if br == 0:
                        t = V(lambda e: e.tensor_tensor(uT[:, dt_, :], sg[:, s, :], bk, ALU.mult), tk, t_sg[dt_])
                        banks.free(key, t)
                    else:
                        t = V(lambda e: e.tensor_tensor(sg[:, s, :], sg[:, s, :], bk, ALU.mult), tk, t_sg[dt_])
                        banks.free(key, t)
                        t = V(lambda e: e.tensor_tensor(uT[:, dt_, :], uT[:, dt_, :], sg[:, s, :], ALU.add))
                        if 2 <= dt_ < 6:
                            turn_x(2 * dt_ - 4)
                            turn_x(2 * dt_ - 3)
                    t_sg[("u", dt_)] = t
                items += [(get_g, False, use_g), (get_b, dt_ == 7, use_b)]
            return items

        t_a2, t_uR, t_xs = [t_og[3]], [], {}
        top = Region(keep, KEEP, TOP)
        xT = sb("xT", [128, 8, 512], at=top)

        def turn_x(k):
            b1, k1 = banks.take()
            PE.wait((s_x2, 16))
            for i in range(4):
                mm = lambda e, i=i: transpose(b1[:, 128 * i:128 * i + 128], xk[:, i, 128 * k:128 * k + 128])
                tk = PE(mm) if i == 3 else mm(nc.tensor)
            t_xs[k] = A(lambda e: e.copy(xT[:, k, :], b1), tk)
            banks.free(k1, t_xs[k])

        for br in range(2):
            if br == 1:
                for k in range(4):
                    t = split((aR[:, 0, k], aR[:, 1, k]), oattT[:, k, :], PE.last)
                t_a2.append(t)
                xk = sb("xk", [128, 4, 1024], at=Region(keep, 0, KEEP))
                s_x2 = sem("s_x2")
                A.wait(t, t_o)
                nc.scalar.dma_start(xk[:, :, :], d["x"].rearrange("(t p) n -> p t n", p=128)).then_inc(s_x2, 16)
            t_sg.clear()
            run(parts, branch(br))
        t_uR.append(split((hR[:, 0, 7], hR[:, 1, 7]), uT[:, 7, :], V.last))
        t_xT = t_xs[7]
        V.wait(t_mod, t_xT)
        sq = sb("sq", [128, 2, 512], at=top)
        rinv = sb("rinv", [128, 512], at=top)

        class Squares:

            def __init__(self, nk, mats, pool):
                self.nk, self.mats = nk, mats
                self.banks = [pool.take() for _ in mats(0)]
                self.pending, self.rel = None, {}

            def add(self, k, src, tok):
                t = A(lambda e: e.activation(sq[:, k % 2, :], src, ACT.Square), tok, self.rel.get(k % 2))
                self.flush()
                self.pending = (k, t)

            def flush(self):
                if self.pending:
                    k, t = self.pending
                    for (bk, key), m in zip(self.banks, self.mats(k)):
                        self.rel[k % 2] = self.tok = PE(
                            lambda e: e.matmul(bk, m, sq[:, k % 2, :], start=(k == 0), stop=(k == self.nk - 1)), t)
                    self.pending = None

        def one_mat(k):
            return [ones[:, :]]

        def root(dst, total):
            total.flush()
            bk, key = total.banks[0]
            t = V(lambda e: e.tensor_scalar(dst, bk, 1.0 / 1024, EPS, ALU.mult, ALU.add), total.tok)
            banks.free(key, t)
            t = A(lambda e: e.activation(dst, dst, ACT.Sqrt), t)
            return V(lambda e: e.reciprocal(dst, dst), t)

        banks.hi, banks.at = 6, 0
        total = Squares(8, one_mat, Banks(6, 7))

        def add_y(n, bk, key, tk):
            t = V(lambda e: e.scalar_tensor_tensor(xT[:, n, :], bk, modc[:, 16 + n, 0:1], xT[:, n, :],
                                                   ALU.mult, ALU.add), tk)
            banks.free(key, t)
            total.add(n, xT[:, n, :], t)

        run(parts, column_items([4, 4], 8, h2, add_y, t_uR))
        t_x1 = V.last
        root(rinv[:, :], total)
        banks.hi = 8
        phase.close()
        handover()
        phase = ExitStack()
        dyn = sb("dyn2", [128, ND], at=phase)

        def column_norm(srcT, nk, sq, rinv, tok):
            bk, key = banks.take()
            rel = [None, None]
            for k in range(nk):
                t = A(lambda e: e.activation(sq[:, k % 2, :], srcT[:, k, :], ACT.Square), tok, rel[k % 2])
                f = lambda e: e.matmul(bk, ones[:, :], sq[:, k % 2, :], start=(k == 0), stop=(k == nk - 1))
                rel[k % 2] = PE(f, t)
            t = V(lambda e: e.tensor_scalar(rinv, bk, 1.0 / (128 * nk), EPS, ALU.mult, ALU.add), PE.last)
            banks.free(key, t)
            t = A(lambda e: e.activation(rinv, rinv, ACT.Sqrt), t)
            return V(lambda e: e.reciprocal(rinv, rinv), t)

        if STAGE <= 4:
            return finish(nc, ctx, V, A, SP, sem)

        moe, moe2 = Region(dyn, 0, ND), Region(keep, 0, KEEP)
        h2T = hT[:, 0:8, 0:512]
        xeT = sb("xeT", [128, 8, 2, 128], at=moe)
        h2k = sb("h2k", [128, 4, 1024], at=moe2)
        xe = sb("xe", [128, 1024], at=moe)
        ye = sb("ye", [128, 2, 1024], at=moe)
        PT = sb("PT", [128, 2, 512], at=moe)
        gmat = sb("gmat", [128, 8, 128], at=moe)
        hid = sb("hid", [128, 2, 512], at=moe)
        hidT = sb("hidT", [128, 8, 128], at=moe)
        lgt = sb("lgt", [128, 4, 16], at=moe)
        lst = sb("lst", [128, 3, 4], at=moe)
        aff = sb("aff", [16, 512], at=moe)
        gv = sb("gv", [16, 64], at=moe)
        iu = sb("iu", [16, 64], U32, at=moe)
        ifl = sb("ifl", [16, 64], at=moe)
        gi8 = sb("gi8", [8, 2, 128], at=moe)
        giT = sb("giT", [128, 2, 8], at=moe)
        idx = sb("idx", [128, 8], U32, at=moe)
        s_h2, s_gi, s_ga = sem("s_h2"), sem("s_gi"), sem("s_ga")
        V(lambda e: e.scalar_tensor_tensor(AB[:, 0, :], modc[:, 32:40, 0], 1.0, colA[:, 24:32], ALU.add, ALU.mult))
        t_h2 = []
        for k in range(8):
            t = V(lambda e: e.scalar_tensor_tensor(h2T[:, k, :], xT[:, k, :], AB[:, 0, k:k + 1], rinv[:, :],
                                                   ALU.mult, ALU.mult))
            t_h2.append(A(lambda e: e.activation(h2T[:, k, :], h2T[:, k, :], ACT.Identity, bias=modc[:, 24 + k, 0:1]), t))
        bk, key = banks.take()
        PE.wait((s_wr, 16))
        for k in range(8):
            r = 32 * (k % 4)
            tk = PE(lambda e: e.matmul(bk[r:r + 16, :], wr[:, k, :], h2T[:, k, :], start=(k < 4), stop=(k >= 4)), t_h2[k])
        for c in range(4):
            t = V(lambda e: e.tensor_copy(mrow[32 * c:32 * c + 16, :], bk[32 * c:32 * c + 16, :]), tk)
        banks.free(key, t)
        bk, key = banks.take()
        PE.wait(t)
        for i in range(4):
            mm = lambda e: transpose(bk[:, 128 * i:128 * i + 128], mrow[:, 128 * i:128 * i + 128])
            tk = PE(mm) if i == 3 else mm(nc.tensor)
        t = V(lambda e: e.tensor_reduce(lgt[:, :, :], bk.rearrange("p (i c x) -> p i x c", i=4, c=4)[:, :, 0:16, :],
                                        AX, ALU.add), tk)
        banks.free(key, t)
        h2d = nc.dram_tensor("h2_scratch", (512, 1024), F32, kind="Internal").ap()
        for i in range(4):
            for q in range(2):
                bk, key = banks.take()
                for k in range(4):
                    mm = lambda e, k=k: transpose(bk[:, 128 * k:128 * k + 128],
                                                  h2T[:, 4 * q + k, 128 * i:128 * i + 128])
                    tk = PE(mm) if k == 3 else mm(nc.tensor)
                t_h2k = A(lambda e: e.copy(h2k[:, i, 512 * q:512 * q + 512], bk), tk)
                banks.free(key, t_h2k)
        A.wait(t_h2k)
        nc.scalar.dma_start(h2d.rearrange("(t p) n -> p t n", p=128), h2k[:, :, :]).then_inc(s_h2, 16)
        V(lambda e: e.tensor_reduce(lst[:, 0, :], lgt[:, :, :], AX, ALU.max))
        t = V(lambda e: e.tensor_tensor(lgt[:, :, :], lgt[:, :, :], lst[:, 0, :].unsqueeze(2).broadcast_to([128, 4, 16]),
                                        ALU.subtract))
        t = A(lambda e: e.activation(lgt[:, :, :], lgt[:, :, :], ACT.Exp), t)
        V(lambda e: e.tensor_reduce(lst[:, 1, :], lgt[:, :, :], AX, ALU.add), t)
        V(lambda e: e.reciprocal(lst[:, 2, :], lst[:, 1, :]))
        t = V(lambda e: e.tensor_tensor(lgt[:, :, :], lgt[:, :, :], lst[:, 2, :].unsqueeze(2).broadcast_to([128, 4, 16]),
                                        ALU.mult))
        bk, key = banks.take()
        PE.wait(t)
        for i in range(4):
            tk = PE(lambda e: transpose(bk[0:16, 128 * i:128 * i + 128], lgt[:, i, :]))
        t = V(lambda e: e.tensor_copy(aff[:, :], bk[0:16, :]), tk)
        banks.free(key, t)
        for r in range(8):
            rs = slice(8 * r, 8 * r + 8)
            V(lambda e: e.max(gv[:, rs], aff[:, :]))
            V(lambda e: e.max_index(iu[:, rs], gv[:, rs], aff[:, :]))
            if r < 7:
                V(lambda e: e.match_replace(aff[:, :], gv[:, rs], aff[:, :], -1.0))
        t = V(lambda e: e.tensor_copy(ifl[:, :], iu[:, :]))
        A.wait(t)
        for e2 in range(2):
            for n, src in enumerate((gv, ifl)):
                nc.scalar.dma_start(gi8[:, n, 64 * e2:64 * e2 + 64], src[e2:16:2, :]).then_inc(s_gi, 16)
        bk, key = banks.take()
        PE.wait((s_gi, 64))
        transpose(bk[:, 0:8], gi8[:, 0, :], 8)
        tk = PE(lambda e: transpose(bk[:, 8:16], gi8[:, 1, :], 8))
        V(lambda e: e.tensor_copy(giT[:, :, :], bk[:, 0:16].rearrange("p (a b) -> p a b", a=2)), tk)
        t_idx = V(lambda e: e.tensor_copy(idx[:, :], bk[:, 8:16]))
        banks.free(key, t_idx)

        def gather(p, tok):
            G.wait(t_idx, (s_h2, 16), tok)
            nc.gpsimd.indirect_dma_start(xe[:, :], None, h2d, bass.IndirectOffsetOnAxis(ap=idx[:, p:p + 1], axis=0))\
                .then_inc(s_ga, 16)
            return (s_ga, 16 * (p + 1))

        def expert_in(p, ta):
            for q in range(2):
                bk, key = banks.take()
                PE.wait(ta)
                for k in range(4):
                    mm = lambda e, k=k: transpose(bk[:, 128 * k:128 * k + 128],
                                                  xe[:, 512 * q + 128 * k:512 * q + 128 * k + 128])
                    tk = PE(mm) if k == 3 else mm(nc.tensor)
                t = A(lambda e: e.copy(xeT[:, 4 * q:4 * q + 4, p % 2, :], bk.rearrange("p (k s) -> p k s", k=4)), tk)
                banks.free(key, t)
            return tk, t

        tg_ = gather(0, None)
        t_free, t_xe = expert_in(0, tg_)
        rel_hid, rel_hidT = None, None

        def pair_product(stat):
            out = []
            for hf in range(2):
                bk, key = banks.take()
                for kh in range(2):
                    ww = [W.get(), W.get()]
                    for k in range(4):
                        for e2 in range(2):
                            es = slice(64 * e2, 64 * e2 + 64)
                            f = lambda e: e.matmul(bk[es, :], stat[:, 4 * kh + k, es], ww[e2][:, k, :],
                                                   start=(kh == 0 and k == 0), stop=(kh == 1 and k == 3))
                            tk = PE(f) if k == 3 else f(nc.tensor)
                    W.done()
                out.append((bk, key, tk))
            return out

        t_sc = {}

        def scatter(p, after=None):
            for k in range(8):
                bk, key = banks.take()
                tk = PE(lambda e: e.matmul(bk, ye[:, p % 2, 128 * k:128 * k + 128], PT[:, p % 2, :], start=True, stop=True),
                        t_sc[("ye", p)])
                t = V(lambda e: e.scalar_tensor_tensor(xT[:, k, :], bk, modc[:, 40 + k, 0:1], xT[:, k, :],
                                                       ALU.mult, ALU.add), tk)
                banks.free(key, t)
                if after:
                    after(k, t)
            t_sc[p] = tk

        for k in range(8):
            G(lambda e: e.tensor_scalar(gmat[:, k, :], ones[:, :], colA[:, 32 + k:33 + k], colA[:, 32 + k:33 + k],
                                        ALU.mult, ALU.mult))
        for p in range(8):
            if p < 7:
                tg_ = gather(p + 1, t_free)
            PE.wait(t_xe)
            bg = pair_product(xeT[:, :, p % 2, :])
            t = None
            for hf in range(2):
                bk, key, tk = bg[hf]
                t = A(lambda e: e.activation(hid[:, hf, :], bk, ACT.Sigmoid), tk, rel_hid)
                t = V(lambda e: e.tensor_tensor(hid[:, hf, :], hid[:, hf, :], bk, ALU.mult), t)
                banks.free(key, t)
            if p:
                scatter(p - 1)
            bu = pair_product(xeT[:, :, p % 2, :])
            if p < 7:
                t_free, t_xe = expert_in(p + 1, tg_)
            for hf in range(2):
                bk, key, tk = bu[hf]
                t = V(lambda e: e.tensor_tensor(hid[:, hf, :], hid[:, hf, :], bk, ALU.mult), tk)
                banks.free(key, t)
                bt, kt_ = banks.take()
                PE.wait(t)
                for k in range(4):
                    mm = lambda e: transpose(bt[:, 128 * k:128 * k + 128], hid[:, hf, 128 * k:128 * k + 128])
                    tk = PE(mm) if k == 3 else mm(nc.tensor)
                t_hT = A(lambda e: e.copy(hidT[:, 4 * hf:4 * hf + 4, :], bt.rearrange("p (k s) -> p k s", k=4)), tk,
                         rel_hidT)
                banks.free(kt_, t_hT)
            rel_hid = tk
            PE.wait(t_hT)
            for hf, (bk, key, tk) in enumerate(pair_product(hidT)):
                t_yek = V(lambda e: e.tensor_scalar(ye[:, p % 2, 512 * hf:512 * hf + 512], bk, giT[:, 0, p:p + 1], None,
                                                    ALU.mult), tk, t_sc.get(p - 2))
                banks.free(key, t_yek)
            t_sc[("ye", p)] = V(lambda e: e.tensor_scalar(PT[:, p % 2, :].rearrange("p (a b) -> p a b", a=2), iot,
                                                          giT[:, 1, p:p + 1], None, ALU.is_equal), (s_iot, 16))
            rel_hidT = PE.last
        banks.hi, banks.at = 6, 0
        total = Squares(8, lambda k: [ones[:, :], gmat[:, k, :]], Banks(6, 8))
        PE.wait(G.last)
        scatter(7, lambda k, t: total.add(k, xT[:, k, :], t))
        total.flush()
        r1 = root(rinv[:, :], total)
        (b2_, key2) = total.banks[1]
        rm = sq[:, 0, :]
        V(lambda e: e.tensor_tensor(rm, rinv[:, :], rinv[:, :], ALU.mult), PE.last)
        V(lambda e: e.tensor_tensor(rm, rm, b2_, ALU.mult))
        banks.free(key2, V.last)
        t = V(lambda e: e.tensor_scalar(rm, rm, 1.0 / 1024, EPS, ALU.mult, ALU.add))
        t = A(lambda e: e.activation(rm, rm, ACT.Sqrt), t)
        for k in range(8):
            V(lambda e: e.scalar_tensor_tensor(xT[:, k, :], xT[:, k, :], colA[:, 32 + k:33 + k], rinv[:, :],
                                               ALU.mult, ALU.mult))
        V(lambda e: e.reciprocal(rinv[:, :], rm), t)
        banks.hi = 8
        phase.close()
        handover()
        phase = ExitStack()
        held = sb("held", [128, 5216], at=phase)
        rctx = ExitStack()
        hR = sb("hR2", [128, 2, 8, 512], F32R, at=rctx)
        wR = sb("wR2", [128, 2, 2, 1024], F32R, at=rctx)
        tmp = sb("tmp2", [128, 2, 512], at=rctx)
        parts = Parts(wR)
        h2 = (hR[:, 0], hR[:, 1])
        t_h3 = []
        for k in range(8):
            t = V(lambda e: e.scalar_tensor_tensor(tmp[:, k % 2, :], xT[:, k, :], colA[:, 40 + k:41 + k], rinv[:, :],
                                                   ALU.mult, ALU.mult))
            t_h3.append(split((hR[:, 0, k], hR[:, 1, k]), tmp[:, k % 2, :], t))

        mixT = sb("mixT", [128, 8, 512], at=Region(keep, 0, KEEP))
        hl = Region(held, 0, 5216)
        kcv = sb("kcv", [128, 2, 512], at=hl)
        ksw = sb("ksw", [128, 4, 256], at=hl)
        kww = sb("kww", [128, 4, 256], at=hl)
        gat = sb("gat", [128, 4, 24], at=hl)
        q2 = sb("q2", [128, 4, 512], at=hl)
        hreg = hT[:, :, :].rearrange("p k t -> p (k t)")
        cv = Region(hreg, 0, 6144)
        uh = sb("uh", [128, 4, 514], at=cv)
        vc = sb("vc", [128, 4, 512], at=cv)

        def token_items(n_cols, c0, evac, first=True):
            items, state = [], {}
            step = 2 if n_cols > 256 else 2
            for kk in range(0, 8, step):
                def get(kk=kk):
                    if first and kk == 0:
                        token_items.w = W.get(A)
                    return token_items.w[:, kk:kk + step, c0:c0 + n_cols]

                def use(out, kk=kk):
                    if kk == 0:
                        state["b"] = [banks.take() for _ in range(4)]
                    for i in range(4):
                        bk, key = state["b"][i]
                        for k in range(step):
                            for j, (a, b) in enumerate(((0, 0), (0, 1), (1, 0))):
                                f = lambda e: e.matmul(bk[:, 0:n_cols], hR[:, a, kk + k, 128 * i:128 * i + 128],
                                                       out[b][:, k, :], start=(kk + k + j == 0),
                                                       stop=(kk + k == 7 and j == 2))
                                tk = PE(f) if k == step - 1 and j == 2 else f(nc.tensor)
                        if kk + step == 8:
                            evac(i, bk, key, tk)
                items.append((get, kk + step == 8, use))
            return items

        def raw_items():
            items = []
            for v in range(2):
                def get(v=v):
                    if v == 0:
                        token_items.w = W.get(A)
                    return token_items.w[:, :, 128 * v:128 * v + 128]

                def use(out, v=v):
                    bk, key = banks.take()
                    tk = products(bk, lambda a, k: out[a][:, k, :], lambda b, k: hR[:, b, k, :], range(8),
                                  ready=t_h3)
                    banks.free(key, A(lambda e: e.copy(kcv[:, v, :], bk), tk))
                items.append((get, False, use))
            return items

        def to_ksw(i, bk, key, tk):
            banks.free(key, A(lambda e: e.copy(ksw[:, i, :], bk[:, 0:256]), tk))

        def to_q2(i, bk, key, tk):
            banks.free(key, A(lambda e: e.copy(q2[:, i, :], bk), tk))

        def to_kww(i, bk, key, tk):
            A(lambda e: e.copy(kww[:, i, :], bk[:, 0:256]), tk)
            banks.free(key, A(lambda e: e.activation(gat[:, i, :], bk[:, 256:280], ACT.Sigmoid)))

        def to_h(c, bk, key, tk):
            banks.free(key, A(lambda e: e.copy(uh[:, c % 4, 2:514], bk), tk))

        def conv(c, bk, key, tk):
            V(lambda e: e.tensor_tensor(uh[:, c, 2:514], uh[:, c, 2:514], bk, ALU.mult), tk, t_uh[c])
            banks.free(key, V.last)
            for tap in range(3):
                w1 = colB[:, 16 + 4 * tap + c:17 + 4 * tap + c]
                if tap == 0:
                    V(lambda e: e.tensor_scalar(vc[:, c, :], uh[:, c, 0:512], w1, None, ALU.mult))
                else:
                    V(lambda e: e.scalar_tensor_tensor(vc[:, c, :], uh[:, c, tap:tap + 512], w1, vc[:, c, :],
                                                       ALU.mult, ALU.add))

        t_uh = {}

        def conv_items(c, bk, key, tk):
            if c < 4:
                t_uh[c] = A(lambda e: e.copy(uh[:, c, 2:514], bk), tk)
                banks.free(key, t_uh[c])
            elif c < 8:
                conv(c - 4, bk, key, tk)
            else:
                banks.free(key, V(lambda e: e.tensor_tensor(vc[:, c - 8, :], vc[:, c - 8, :], bk, ALU.mult), tk))

        V(lambda e: e.memset(uh[:, :, 0:2], 0.0))
        run(parts, raw_items() + token_items(256, 256, to_ksw, False) + token_items(512, 0, to_q2)
            + token_items(280, 0, to_kww) + column_items([4, 4, 4], 8, h2, conv_items))
        t_gat = t_kcv = t_ksw = A.last
        column_norm(vc, 4, sq, rinv[:, :], V.last)
        for c in range(4):
            t_mix = V(lambda e: e.scalar_tensor_tensor(mixT[:, 4 + c, :], vc[:, c, :], colA[:, 52 + c:53 + c],
                                                       rinv[:, :], ALU.mult, ALU.mult))
        rctx.close()
        handover()
        dyn = sb("dyn3", [128, ND - 5216], at=phase)
        b2, hr = Region(dyn, 0, ND - 5216), Region(hreg, 0, 6144)
        q2T = sb("q2T", [128, 4, 512], at=hr)
        kz2 = sb("kz2", [128, 2, 2, 512], at=hr)
        dist = sb("dist", [128, 512], at=hr)
        cb = sb("cb", [128, 4, 8, 32], at=hr)
        rr = sb("rr2", [128, 32], at=hr)
        hdn = sb("hdn", [128, 2, 256], at=b2)
        hdk = sb("hdk", [128, 256], at=b2)
        kcm = sb("kcm", [32, 2, 128], at=b2)
        kcz = sb("kcz", [128, 2, 32], at=b2)
        wc2 = sb("wc2", [128, 2, 2, 64], at=b2)
        cmk = sb("cmk", [128, 4, 32], at=b2)
        b3 = Region(dyn, b2.at, ND - 5216)
        shA = sb("shA", [128, 4, 512], at=b2)
        blkT = sb("blkT", [128, 16, 2, 2, 32], at=b2)
        tA = sb("tA2", [128, 2048], at=b2)
        tC = kcv
        s_k2 = sem("s_k2")
        nc.scalar.dma_start(wc2[:, :, :, :], d["w_cmp2_2"].rearrange("v (k p) n -> p v k n", p=128)).then_inc(s_k2, 16)
        nc.scalar.dma_start(dist[:, :], d["k_dist"]).then_inc(s_k2, 16)
        nc.scalar.dma_start(cb[:, :, :, :], d["k_cb"]).then_inc(s_k2, 16)
        nc.scalar.dma_start(cmk[:, :, :], d["k_cm"]).then_inc(s_k2, 16)
        G(lambda e: e.memset(kz2[:, :, :, :], 0.0))
        t_kz2 = G(lambda e: e.memset(kcz[:, :, :], 0.0))
        s_sh = sem("s_sh")
        A.wait(t_kcv)
        for v in range(2):
            for g in range(2):
                src = kcv[64 * g:64 * g + 64, v, :]
                nc.scalar.dma_start(shA[0:64, 2 * v + g, :], src).then_inc(s_sh, 16)
                nc.scalar.dma_start(shA[64:128, 2 * v + g, 0:511], src[:, 1:512]).then_inc(s_sh, 16)
        V.wait((s_k2, 64))
        for v in range(2):
            for g in range(2):
                base_ap = shA[:, 2 * v + g, :].rearrange("p (i l) -> p i l", l=16)
                for half in range(2):
                    src = base_ap[:, half:half + 31, :].rearrange("p i (l u) -> p l u i", u=2)[:, :, 0, :]
                    dstv = blkT[:, 8 * half:8 * half + 8, v, g, 0:31]
                    pe = colB[:, 32 + 16 * v + 8 * half:40 + 16 * v + 8 * half].unsqueeze(2).broadcast_to([128, 8, 31])
                    V(lambda e: e.tensor_tensor(dstv, src, pe, ALU.add), (s_sh, 128))
        t_blk = V(lambda e: e.memset(blkT[:, :, :, :, 31:32], 0.0))
        PE.wait(t_blk)
        wv = [W.get(), W.get()]
        bk, key = banks.take()
        for l in range(16):
            for v in range(2):
                vs = slice(64 * v, 64 * v + 64)
                f = lambda e: e.matmul(bk[vs, 0:256], blkT[:, l, v].rearrange("p g i -> p (g i)"), wv[v][:, l, :],
                                       start=(l == 0), stop=(l == 15))
                tk = PE(f) if l == 15 else f(nc.tensor)
        W.done()
        t = A(lambda e: e.copy(hdk[:, :], bk[:, 0:256]), tk)
        banks.free(key, t)
        bk, key = banks.take()
        PE.wait(t)
        for hh in range(2):
            tk = PE(lambda e: transpose(bk[:, 128 * hh:128 * hh + 128], hdk[:, 128 * hh:128 * hh + 128]))
        for hh in range(2):
            for v in range(2):
                o = 128 * hh + 64 * v
                t_hd = A(lambda e: e.activation(hdn[:, hh, 64 * v:64 * v + 64], bk[:, o:o + 64], ACT.Gelu_apprx_tanh,
                                                bias=colB[:, 28 + 2 * v + hh:29 + 2 * v + hh]), tk)
        banks.free(key, t_hd)
        PE.wait(t_hd, (s_k2, 64))
        for v in range(2):
            bk, key = banks.take()
            for g in range(2):
                o = 64 * v + 32 * g
                tk = proj(bk[0:32, 64 * g:64 * g + 64], [(hdn[:, hh, o:o + 32], wc2[:, v, hh, :]) for hh in range(2)])
            t_kcm = V(lambda e: e.tensor_tensor(kcm[:, v, :].rearrange("p (g e) -> p g e", g=2),
                                                bk[0:32, 0:128].rearrange("p (g e) -> p g e", g=2),
                                                gb[0:32, 6 + v, :].unsqueeze(1).broadcast_to([32, 2, 64]), ALU.add), tk)
            banks.free(key, t_kcm)

        def head_norm2(src, nt, nh, gain, scale, *tokens, P=128):
            n = nt * nh
            V(lambda e: e.tensor_tensor(tA[0:P, 0:64 * n].rearrange("p (t h e) -> p t h e", h=nh, e=64), src, src,
                                        ALU.mult), *tokens)
            V(lambda e: e.tensor_reduce(rr[0:P, 0:n], tA[0:P, 0:64 * n].rearrange("p (n e) -> p n e", e=64), AX, ALU.add))
            inv_root(rr[0:P, 0:n], rr[0:P, 0:n], 1.0 / 64)
            r4 = rr[0:P, 0:n].rearrange("p (t h) -> p t h", h=nh).unsqueeze(3).broadcast_to([P, nt, nh, 64])
            V(lambda e: e.tensor_tensor(src, src, r4, ALU.mult))
            g4 = gain.unsqueeze(1).unsqueeze(1).broadcast_to([P, nt, nh, 64])
            t = V(lambda e: e.tensor_tensor(src, src, g4, ALU.mult))
            if scale != 1.0:
                t = V(lambda e: e.tensor_scalar(src, src, scale, None, ALU.mult))
            return t

        t_qn = head_norm2(q2[:, :, :].rearrange("p t (h e) -> p t h e", e=64), 4, 8, gb[:, 2, :], 0.125)
        rel_tC = [None, None]
        for i in range(4):
            t = G(lambda e: e.tensor_copy(tC[:, i % 2, :].rearrange("p (j g e) -> p g j e", g=2, e=64),
                                          q2[:, i, :].rearrange("p (g j e) -> p g j e", g=2, e=64)),
                  t_qn, rel_tC[i % 2])
            bk, key = banks.take()
            PE.wait(t)
            for j in range(4):
                mm = lambda e: transpose(bk[:, 128 * j:128 * j + 128], tC[:, i % 2, 128 * j:128 * j + 128])
                tk = PE(mm) if j == 3 else mm(nc.tensor)
            rel_tC[i % 2] = tk
            t_q2T = A(lambda e: e.copy(q2T[:, :, 128 * i:128 * i + 128], bk.rearrange("p (j q) -> p j q", j=4)), tk)
            banks.free(key, t_q2T)
        for v, (src_t, gi) in enumerate(((ksw, 4), (kww, 5))):
            t = head_norm2(src_t[:, :, 0:128].rearrange("p t (h e) -> p t h e", e=64), 4, 2, gb[:, gi, :], 1.0, t_ksw)
            bk, key = banks.take()
            PE.wait(t)
            for i in range(4):
                mm = lambda e: transpose(bk[:, 128 * i:128 * i + 128], src_t[:, i, 0:128])
                tk = PE(mm) if i == 3 else mm(nc.tensor)
            for g in range(2):
                gs = slice(64 * g, 64 * g + 64)
                t_kz = A(lambda e: e.copy(kz2[gs, g, v, :], bk[gs, :]), tk, t_kz2)
            banks.free(key, t_kz)
        t = head_norm2(kcm[:, 0, :].rearrange("p (t h e) -> p t h e", t=1, e=64), 1, 2, gb[0:32, 3, :], 1.0, P=32)
        bk, key = banks.take()
        tk = PE(lambda e: transpose(bk[:, 0:32], kcm[:, 0, :], 32), t)
        for g in range(2):
            gs = slice(64 * g, 64 * g + 64)
            t = A(lambda e: e.copy(kcz[gs, g, :], bk[gs, 0:32]), tk, t_kz2)
        banks.free(key, t)
        PE.wait(t)

        cp = sb("cp", [128, 8, 32], at=b3)
        cst = sb("cst", [128, 3, 8], at=b3)
        cpT = sb("cpT", [32, 8, 128], at=b3)
        p2 = sb("p2", [128, 4, 2, 512], at=b3)
        p2T = sb("p2T", [128, 2, 2, 512], at=b3)
        st2 = sb("st2", [128, 6, 3, 2], at=b3)
        o2 = sb("o2", [128, 2, 512], at=b3)
        o2n = sb("o2n", [128, 512], at=b3)
        on = sb("on", [128, 1], at=b3)
        G.wait(PE.last)
        V.wait(PE.last)
        A.wait(PE.last, V.last)
        rel_p, rel_pT, e_done, t_pT = {}, {}, {}, {}
        its = [(i, h) for i in range(3, -1, -1) for h in range(8)]
        rel_cp, rel_cpT, rel_on, rel_o2 = None, None, None, {}

        def cmp_part(i):
            nonlocal rel_cp, rel_cpT
            bk, key = banks.take(2)
            for h in range(8):
                j, g = h % 4, h // 4
                tk = PE(lambda e: e.matmul(bk[:, 512 * g + 32 * j:512 * g + 32 * j + 32],
                                           q2T[:, j, 128 * i:128 * i + 128], kcz[:, g, :], start=True, stop=True))
            V.wait(rel_cp)
            V(lambda e: e.tensor_tensor(cp[:, :, :].rearrange("p (g j) s -> p g j s", g=2),
                                        bk.rearrange("p (g j s) -> p g j s", g=2, s=32)[:, :, 0:4, :],
                                        cb[:, i].rearrange("p (g j) s -> p g j s", g=2), ALU.add), tk)
            banks.free(key, V.last)
            V(lambda e: e.tensor_reduce(cst[:, 0, :], cp[:, :, 0:31], AX, ALU.max))
            t = V(lambda e: e.tensor_tensor(cp[:, :, :], cp[:, :, :], cst[:, 0, :].unsqueeze(2).broadcast_to([128, 8, 32]),
                                            ALU.subtract))
            t = A(lambda e: e.activation(cp[:, :, 0:31], cp[:, :, 0:31], ACT.Exp), t)
            V(lambda e: e.tensor_tensor(cp[:, :, :], cp[:, :, :], cmk[:, i, :].unsqueeze(1).broadcast_to([128, 8, 32]),
                                        ALU.mult), t)
            V(lambda e: e.tensor_reduce(cst[:, 1, :], cp[:, :, 0:31], AX, ALU.add))
            V(lambda e: e.tensor_scalar(cst[:, 1, :], cst[:, 1, :], 1e-30, None, ALU.max))
            V(lambda e: e.reciprocal(cst[:, 1, :], cst[:, 1, :]))
            V(lambda e: e.tensor_tensor(cst[:, 2, :], cst[:, 1, :], gat[:, i, 0:24:3], ALU.mult), t_gat)
            t = V(lambda e: e.tensor_tensor(cp[:, :, :], cp[:, :, :], cst[:, 2, :].unsqueeze(2).broadcast_to([128, 8, 32]),
                                            ALU.mult))
            bk, key = banks.take(2)
            PE.wait(t)
            for h in range(8):
                tk = PE(lambda e: transpose(bk[0:32, 128 * h:128 * h + 128], cp[:, h, :]))
            rel_cp = tk
            t = V(lambda e: e.tensor_copy(cpT[:, :, :], bk[0:32, :].rearrange("p (h q) -> p h q", h=8)), tk, rel_cpT)
            banks.free(key, t)
            bk, key = banks.take()
            PE.wait(t)
            for h in range(8):
                g = h // 4
                tk = PE(lambda e: e.matmul(bk[:, 64 * h:64 * h + 64], cpT[0:31, h, :], kcm[0:31, 1, 64 * g:64 * g + 64],
                                           start=True, stop=True))
            rel_cpT = tk
            t = A(lambda e: e.copy(o2[:, i % 2, :], bk), tk, rel_o2.get(i + 2))
            banks.free(key, t)
            return t

        def scores2(n):
            i, h = its[n]
            s, nk = n % 4, 128 * (i + 1)
            slope = float(np.float32(2.0 ** -(h + 1)))
            for v in range(2):
                bk, key = banks.take()
                tk = PE(lambda e: e.matmul(bk[:, 0:nk], q2T[:, h % 4, 128 * i:128 * i + 128], kz2[:, h // 4, v, 0:nk],
                                           start=True, stop=True))
                t = V(lambda e: e.scalar_tensor_tensor(p2[:, s, v, 0:nk], dist[:, 512 - nk:512], slope, bk[:, 0:nk],
                                                       ALU.mult, ALU.add), tk, rel_p.get(n - 4))
                banks.free(key, t)
            t = V(lambda e: e.tensor_reduce(st2[:, n % 6, 0, :], p2[:, s, :, 0:nk], AX, ALU.max, negate=True))
            for v in range(2):
                e_done[n] = A(lambda e: e.activation(p2[:, s, v, 0:nk], p2[:, s, v, 0:nk], ACT.Exp,
                                                     bias=st2[:, n % 6, 0, v:v + 1],
                                                     accum_out=st2[:, n % 6, 1, v:v + 1]), t)

        def turn2(n):
            i, h = its[n]
            s, nk = n % 4, 128 * (i + 1)
            PE.wait(e_done[n])
            for v in range(2):
                bk, key = banks.take()
                for c in range(i + 1):
                    mm = lambda e: transpose(bk[:, 128 * c:128 * c + 128], p2[:, s, v, 128 * c:128 * c + 128])
                    tk = PE(mm) if c == i else mm(nc.tensor)
                t_pT[n] = A(lambda e: e.copy(p2T[:, n % 2, v, 0:nk], bk[:, 0:nk]), tk, rel_pT.get(n - 2))
                banks.free(key, t_pT[n])
            rel_p[n] = tk

        def values2(n, t_o2):
            nonlocal rel_on
            i, h = its[n]
            g, s = h // 4, n % 2
            bo, ko = banks.take()
            PE.wait(t_pT[n])
            for v, vt in enumerate((ksw, kww)):
                tk = proj(bo[:, 128 * v:128 * v + 128], [(p2T[:, n % 2, v, 128 * c:128 * c + 128], vt[:, c, 128:256])
                                                         for c in range(i + 1)])
            rel_pT[n] = tk
            r2 = st2[:, n % 6, 2, :]
            V(lambda e: e.reciprocal(r2, st2[:, n % 6, 1, :]), e_done[n])
            V(lambda e: e.tensor_tensor(r2, r2, gat[:, i, 3 * h + 1:3 * h + 3], ALU.mult))
            oh = o2[:, i % 2, 64 * h:64 * h + 64]
            for v in range(2):
                t = V(lambda e: e.scalar_tensor_tensor(oh, bo[:, 128 * v + 64 * g:128 * v + 64 * g + 64], r2[:, v:v + 1],
                                                       oh, ALU.mult, ALU.add), tk, t_o2)
            banks.free(ko, t)
            if h == 7:
                oi = o2[:, i % 2, :]
                V.wait(rel_on)
                V(lambda e: e.tensor_tensor(o2n[:, :], oi, oi, ALU.mult))
                V(lambda e: e.tensor_reduce(on[:, :], o2n[:, :], AX, ALU.add))
                inv_root(on[:, :], on[:, :], 1.0 / 512)
                t = V(lambda e: e.tensor_scalar(o2n[:, :], oi, on[:, :], None, ALU.mult))
                rel_o2[i] = t
                bt, kt_ = banks.take()
                PE.wait(t)
                for k in range(4):
                    mm = lambda e: transpose(bt[:, 128 * k:128 * k + 128], o2n[:, 128 * k:128 * k + 128])
                    rel_on = PE(mm) if k == 3 else mm(nc.tensor)
                t = V(lambda e: e.tensor_tensor(mixT[:, 0:4, 128 * i:128 * i + 128],
                                                bt.rearrange("p (k q) -> p k q", k=4),
                                                colA[:, 48:52].unsqueeze(2).broadcast_to([128, 4, 128]), ALU.mult), rel_on)
                banks.free(kt_, t)
            return t

        t_o2 = {}
        for n in range(36):
            if n < 32:
                scores2(n)
            if n % 8 == 2 and n < 32:
                i = its[n - 2][0]
                t_o2[i] = cmp_part(i)
            if 2 <= n < 34:
                turn2(n - 2)
            if 3 <= n < 35:
                t_mix = values2(n - 3, t_o2[its[n - 3][0]])
        t_b2 = PE.last
        if STAGE <= 6:
            return finish(nc, ctx, V, A, SP, sem)

        phase.close()
        hctx.close()
        handover()
        phase = ExitStack()
        hR = sb("hR3", [128, 2, 8, 512], F32R, at=phase)
        wR = sb("wR3", [128, 2, 2, 1024], F32R, at=phase)
        xR = sb("xR3", [128, 2, 8, 512], F32R, at=phase)
        tmp = sb("tmp3", [128, 4, 512], at=phase)
        parts = Parts(wR)
        h2 = (hR[:, 0], hR[:, 1])
        t_mR = [split((hR[:, 0, k], hR[:, 1, k]), mixT[:, k, :]) for k in range(8)]
        banks.hi, banks.at = 7, 0
        total = Squares(8, one_mat, Banks(7, 8))

        def add_o(n, bk, key, tk):
            t = V(lambda e: e.tensor_tensor(xT[:, n, :], xT[:, n, :], bk, ALU.add), tk)
            banks.free(key, t)
            total.add(n, xT[:, n, :], t)
            t_h4.append(split_scaled((xR[:, 0, n], xR[:, 1, n]), xT[:, n, :], colA[:, 56 + n:57 + n], t))

        t_h4 = []
        run(parts, column_items([4, 4], 8, h2, add_o, t_mR))
        t_x4 = V.last
        root(rinv[:, :], total)
        banks.hi = 8
        xo = mixT[:, :, :].rearrange("p (i q) n -> p i q n", q=2)
        for i in range(4):
            for q in range(2):
                bk, key = banks.take()
                PE.wait(t_x4)
                for k in range(4):
                    mm = lambda e: transpose(bk[:, 128 * k:128 * k + 128], xT[:, 4 * q + k, 128 * i:128 * i + 128])
                    tk = PE(mm) if k == 3 else mm(nc.tensor)
                t_xo = A(lambda e: e.copy(xo[:, i, q, :], bk), tk)
                banks.free(key, t_xo)
        rel_u = [PE.last, PE.last]
        uR = hR[:, :, :, :].rearrange("p x (s k) t -> p s x k t", s=2)
        h4 = (xR[:, 0], xR[:, 1])
        t_u = {}

        def up_items(r):
            def evac(j, bk, key, tk):
                m = tmp[:, j % 4, :]
                t = V(lambda e: e.scalar_tensor_tensor(m, bk, 0.0, rinv[:, :], ALU.max, ALU.mult), tk,
                      t_u.get(("tmp", j % 4)))
                banks.free(key, t)
                t = G(lambda e: e.tensor_tensor(m, m, m, ALU.mult), t)
                t_u[r] = t_u[("tmp", j % 4)] = split((uR[:, r % 2, 0, j], uR[:, r % 2, 1, j]), m, t, rel_u[r % 2])
            return column_items([4], 8, h4, evac, t_h4 if r == 0 else None)

        def down_items(r):
            items, state = [], {}
            for k in range(4):
                def get(k=k):
                    if k == 0:
                        state["w"] = W.get(A)
                    return state["w"][:, k:k + 1, :]

                def use(out, k=k):
                    if k == 0:
                        PE.wait(t_u[r])
                        state["b"] = [banks.take() for _ in range(8)]
                    for b in range(8):
                        i, q = b // 2, b % 2
                        bk, key = state["b"][b]
                        for n, (x, y) in enumerate(((0, 0), (0, 1), (1, 0))):
                            f = lambda e: e.matmul(bk, uR[:, r % 2, x, k, 128 * i:128 * i + 128],
                                                   out[y][:, 0, 512 * q:512 * q + 512],
                                                   start=(k == 0 and n == 0), stop=(k == 3 and n == 2))
                            tk = PE(f) if n == 2 else f(nc.tensor)
                        if k == 3:
                            rel_u[r % 2] = tk
                            state["t"] = V(lambda e: e.tensor_tensor(xo[:, i, q, :], xo[:, i, q, :], bk, ALU.add),
                                           tk, t_xo)
                            banks.free(key, state["t"])
                items.append((get, k == 3, use))
            return items

        items = up_items(0)
        for r in range(1, 8):
            items += up_items(r) + down_items(r - 1)
        run(parts, items + down_items(7))
        t = V.last
        s_out = sem("s_out")
        SP.wait(t)
        nc.sync.dma_start(out.rearrange("(i p) n -> p i n", p=128),
                          mixT[:, :, :].rearrange("p (i q) n -> p i (q n)", q=2)).then_inc(s_out, 16)
        SP.wait((s_out, 16))
        phase.close()


def finish(nc, ctx, V, A, SP, sem):
    pass


def constants():
    c = {}
    c["k_ident"] = np.eye(128, dtype=np.float32)
    s, t = np.meshgrid(np.arange(128), np.arange(128), indexing="ij")
    m = np.zeros((128, 14, 128), np.float32)
    for i, h in enumerate(LEVELS):
        same = (s // (2 * h)) == (t // (2 * h))
        m[:, i] = same & (s % (2 * h) < h) & (t % (2 * h) >= h)
        m[:, 7 + i] = same & (s % (2 * h) >= h) & (t % (2 * h) < h)
    c["k_masks"] = m
    inv = np.float32(10000.0) ** (-np.arange(0, 32, 2, dtype=np.float32) / np.float32(32))
    tt = np.arange(512)
    ang = np.stack([(tt // 64).astype(np.float32)[:, None] * inv, (tt % 64).astype(np.float32)[:, None] * inv], 1)
    co, si = np.cos(ang), np.sin(ang)
    cs = np.concatenate([co, co], -1).reshape(512, 64)
    sn = np.concatenate([-si, si], -1).reshape(512, 64)
    c["k_rope"] = np.ascontiguousarray(np.stack([cs, sn], 1).reshape(4, 128, 2, 64).transpose(1, 0, 2, 3)).astype(np.float32)
    c["k_iota"] = np.arange(512, dtype=np.float32)
    q, j = np.meshgrid(np.arange(128), np.arange(512), indexing="ij")
    dd = (q + 384 - j).astype(np.float32)
    c["k_dist"] = np.where(dd >= 0, -dd, np.float32(-1e33)).astype(np.float32)
    t4 = (np.arange(4)[None, :, None] * 128 + np.arange(128)[:, None, None]).astype(np.float32)
    dc = t4 - (16 * np.arange(32)[None, None, :] + 31).astype(np.float32)
    dc[:, :, 31] = -1
    slope = np.power(np.float32(2.0), -np.arange(1, 9, dtype=np.float32))
    cb = np.where(dc[:, :, None, :] >= 0, -slope[None, None, :, None] * dc[:, :, None, :], np.float32(-1e30))
    c["k_cb"] = np.ascontiguousarray(cb).astype(np.float32)
    c["k_cm"] = np.ascontiguousarray(dc >= 0).astype(np.float32)
    return c


_FLAT = ["c", "c_ctx", "b_mod", "norm1_g", "norm2_g", "hg_lb_logits", "hg_norm_g", "q_norm_g", "k_norm_g",
         "final_norm_g", "g_mix_norm_2", "g_q_2", "g_k_2", "pe_cmp_2", "b_cmp1_2", "b_cmp2_2", "conv_w_2", "g_out_2",
         "g_ffn_norm_2"]
_FIRST = ["x", "ctx", "w_mod", "w_in", "w_branch_a", "w_branch_b", "w_out", "w_router", "w_exp_gate", "w_exp_up",
          "w_exp_down", "w_in_2", "w_cmp1_2", "w_cmp2_2", "w_o_2", "w_up_2", "w_down_2"]


def kernel(**inputs):
    import concourse.bacc as _bacc
    from concourse.bass_utils import run_bass_kernel_spmd as _run

    nc = _bacc.Bacc("TRN2", target_bir_lowering=False, num_devices=1)
    arrays = {}
    for name in _FLAT:
        arrays[name] = np.ascontiguousarray(inputs[name]).reshape(-1)
    for name in _FIRST:
        a = np.ascontiguousarray(inputs[name])
        arrays[name] = a.reshape(a.shape[1:]) if a.shape[0] == 1 else a
    arrays.update(constants())
    d, sent = {}, {}
    for name, a in arrays.items():
        sent[f"in_{name}_dram"] = a
        d[name] = nc.dram_tensor(f"in_{name}_dram", a.shape, mybir.dt.from_np(a.dtype), kind="ExternalInput").ap()
    out = nc.dram_tensor("out_0_dram", (512, 1024), F32, kind="ExternalOutput").ap()
    program(nc, d, out)
    r = _run(nc, [sent], core_ids=[0])
    return np.asarray(r.results[0]["out_0_dram"]).reshape(1, 512, 1024)
```

```python
from contextlib import ExitStack

import numpy as np

import concourse.bass as bass
from concourse import mybir

F32 = mybir.dt.float32
F32R = mybir.dt.float32r
U8 = mybir.dt.uint8
U32 = mybir.dt.uint32
ALU = mybir.AluOpType
ACT = mybir.ActivationFunctionType
AX = mybir.AxisListType.X

NS = 8
LEVELS = [64, 32, 16, 8, 4, 2, 1]
EPS = 1e-6


class Queue:

    def __init__(self, eng, sem, chain):
        self.eng, self.sem, self.chain, self.n, self.seen = eng, sem, chain, 0, {}

    def wait(self, *tokens):
        for t in tokens:
            if t is not None and self.seen.get(t[0].name, 0) < t[1]:
                self.seen[t[0].name] = t[1]
                self.eng.wait_ge(t[0], t[1])

    def __call__(self, fn, *tokens):
        self.wait(*tokens)
        if self.chain and self.n:
            self.wait((self.sem, self.n))
        fn(self.eng).then_inc(self.sem, 1)
        self.n += 1
        return (self.sem, self.n)

    @property
    def last(self):
        return (self.sem, self.n) if self.n else None


def program(nc, d, out):
    with ExitStack() as ctx:
        def sem(name):
            return ctx.enter_context(nc.semaphore(name))

        class Region:

            def __init__(self, tensor, lo, hi):
                self.tensor, self.at, self.hi = tensor, lo, hi

            def take(self, shape, dt):
                size = mybir.dt.size(dt)
                count = int(np.prod(shape[1:]))
                words = -(-count * size // 4)
                assert self.at + words <= self.hi, (shape, self.at, self.hi)
                a = self.tensor[0:shape[0], self.at:self.at + words]
                self.at += words
                if dt != F32:
                    a = a.bitcast(dt)
                if len(shape) > 2:
                    names = "abcdef"[:len(shape) - 1]
                    a = a.rearrange(f"p ({' '.join(names)}) -> p {' '.join(names)}", **dict(zip(names, shape[1:])))
                return a

        ND = 18552
        keep = ctx.enter_context(nc.sbuf_tensor("keep", [128, 9728], F32))
        KEEP, TOP = 4096, 9728

        def sb(name, shape, dt=F32, at=None):
            if at is None:
                return ctx.enter_context(nc.sbuf_tensor(name, shape, dt))
            if isinstance(at, ExitStack):
                return at.enter_context(nc.sbuf_tensor(name, shape, dt))
            return at.take(shape, dt)

        V = Queue(nc.vector, sem("s_v"), True)
        A = Queue(nc.scalar, sem("s_a"), True)
        G = Queue(nc.gpsimd, sem("s_g"), True)
        PE = Queue(nc.tensor, sem("s_pe"), False)
        SP = Queue(nc.sync, sem("s_sp"), False)

        PS = ctx.enter_context(nc.psum_tensor("PS", [128, 8 * 512], F32))

        released = [None] * 8

        class Banks:

            def __init__(self, lo, hi):
                self.lo, self.hi, self.at = lo, hi, lo

            def take(self, n=1):
                if self.at + n > self.hi:
                    self.at = self.lo
                b = self.at
                self.at = b + n if b + n < self.hi else self.lo
                for i in range(b, b + n):
                    assert released[i] != "held", "bank still held"
                    PE.wait(released[i])
                    released[i] = "held"
                return PS[:, b * 512:(b + n) * 512], (b, n)

            def free(self, key, tok):
                for i in range(key[0], key[0] + key[1]):
                    released[i] = tok

        banks = Banks(0, 8)

        def dma(q, dst, src, s, *tokens):
            q.wait(*tokens)
            q.eng.dma_start(dst, src).then_inc(s, 16)
            return (s, 16)

        ring = sb("ring", [128, NS, 2048])
        slot_sem = [sem(f"s_w{i}") for i in range(NS)]

        def cols(w, a, n):
            return (w[:, a:a + n].rearrange("(k p) n -> p k n", p=128), w.shape[0] // 128, n)

        units = [cols(d["w_mod"], 512 * j, 512) for j in range(4)]
        units += [cols(d["w_in"], 2560, 512), cols(d["w_in"], 3072, 256)]
        for hp in range(2):
            for what in (("i", 512), ("m", 0), ("i", 0), ("i", 1536), ("i", 1024), ("m", 3), ("m", 1), ("m", 2)):
                units += [cols(d["w_in"], what[1] + 256 * hp, 256) if what[0] == "i" else
                          cols(d["w_mod"], 2048 + 512 * (4 * hp + what[1]), 512)]
        units += [cols(d["w_in"], 2048, 512)]
        for a, wb in ((3328, "w_branch_a"), (4352, "w_branch_b")):
            units += [cols(d[wb], 0, 1024), cols(d["w_in"], a, 512), cols(d["w_in"], a + 512, 512)]
        units += [cols(d["w_out"], 0, 512), cols(d["w_out"], 512, 512)]
        for p in range(8):
            for name in ("w_exp_gate", "w_exp_up", "w_exp_down"):
                for hf in range(2):
                    for kh in range(2):
                        units += [cols(d[name][2 * p + e2][512 * kh:512 * kh + 512, :], 512 * hf, 512)
                                  for e2 in range(2)]
        w2 = d["w_in_2"]
        units += [cols(w2, 512, 512), cols(w2, 0, 512), cols(w2, 1024, 280)]
        units += [cols(w2, 1304, 512), cols(w2, 1816, 512), cols(w2, 2328, 512)]
        units += [cols(d["w_cmp1_2"][0], 0, 256), cols(d["w_cmp1_2"][1], 0, 256)]
        units += [cols(d["w_o_2"], 0, 512), cols(d["w_o_2"], 512, 512)]
        ups = [cols(d["w_up_2"], 512 * j, 512) for j in range(8)]
        downs = [cols(d["w_down_2"][512 * j:512 * j + 512, :], 0, 1024) for j in range(8)]
        units += ups[:1] + [u for pair in zip(ups[1:], downs) for u in pair] + downs[7:]

        class Stream:

            def __init__(self):
                self.loaded, self.got, self.freed = 0, 0, 0
                self.pos, at = [], 0
                for _, k, n in units:
                    self.pos.append(at)
                    at += 1 if k * n <= 2048 and k == 4 else 2
                self.pos.append(at)
                self.count, self.need = [0] * NS, []
                for i in range(len(units)):
                    s = self.pos[i] % NS
                    self.count[s] += 16
                    self.need.append((slot_sem[s], self.count[s]))

            def load(self, tok=None):
                read = self.pos[self.freed]
                while self.loaded < len(units) and self.pos[self.loaded + 1] - NS <= read:
                    i = self.loaded
                    SP.wait(tok)
                    nc.sync.dma_start(self.view(i), units[i][0]).then_inc(self.need[i][0], 16)
                    self.loaded += 1

            def view(self, i):
                _, k, n = units[i]
                a = ring[:, :, :].rearrange("p s n -> p (s n)")
                o = self.pos[i] % NS * 2048
                return a[:, o:o + k * n].rearrange("p (k n) -> p k n", k=k)

            def get(self, *queues):
                i = self.got
                assert i < self.loaded
                for q in queues or (PE,):
                    q.wait(self.need[i])
                self.got += 1
                return self.view(i)

            def done(self, tok=None):
                self.freed = self.got
                self.load(tok or PE.last)

        W = Stream()

        ident = sb("ident", [128, 128])
        ones = sb("ones", [128, 128])
        rows = sb("rows", [128, 2, 128])
        colA = sb("colA", [128, 128])
        colB = sb("colB", [128, 64])
        gb = sb("gb", [128, 8, 64])
        masks = sb("masks", [128, 14, 128], U8)
        small = [sem(f"s_c{i}") for i in range(8)]
        s_rows, s_gb = sem("s_rows"), sem("s_gb")
        t_ones = V(lambda e: e.memset(ones[:, :], 1.0))
        t_rows0 = V(lambda e: e.memset(rows[:, :, :], 0.0))
        n = 0
        for t, name, k in ((0, "c", 8), (0, "c_ctx", 8), (0, "norm1_g", 8), (0, "norm2_g", 8), (0, "final_norm_g", 8),
                           (0, "g_mix_norm_2", 8), (0, "g_out_2", 8), (0, "g_ffn_norm_2", 8), (0, "b_mod", 48),
                           (0, "hg_norm_g", 4), (1, "hg_lb_logits", 16), (1, "conv_w_2", 12), (1, "b_cmp1_2", 4),
                           (1, "pe_cmp_2", 32)):
            if n in (0, 10):
                at = 0
            A.wait(t_rows0)
            nc.scalar.dma_start(rows[at:at + k, t, :], d[name].rearrange("(r p) -> r p", p=128)).then_inc(s_rows, 16)
            at += k
            n += 1
        t_rows = (s_rows, 16 * n)
        t_ident = dma(A, ident[:, :], d["k_ident"], small[0])
        ngb = 0
        for i, (name, o) in enumerate((("q_norm_g", 0), ("k_norm_g", 0), ("g_q_2", 0), ("g_k_2", 0), ("g_k_2", 64),
                                       ("g_k_2", 128), ("b_cmp2_2", 0), ("b_cmp2_2", 64))):
            nc.scalar.dma_start(gb[:, i, :], d[name][o:o + 64].partition_broadcast(128)).then_inc(s_gb, 16)
            ngb += 1
        t_gb = (s_gb, 16 * ngb)
        hctx, phase = ExitStack(), ExitStack()
        ss = sb("ss", [128, 8])
        A1 = sb("A1", [128, 2, 8])
        mrow = sb("mrow", [128, 512])
        sil = sb("sil", [128, 2, 8])
        modc = sb("modc", [128, 48, 2])
        AB = sb("AB", [128, 3, 8])
        hT = sb("hT", [128, 8, 768], at=hctx)
        dyn = sb("dyn1", [128, ND], at=phase)
        base = Region(dyn, 0, ND)
        mstage = sb("mstage", [128, 14, 128], at=base)
        t_mst = dma(A, mstage, d["k_masks"], small[1])

        PE.wait(t_ident, t_rows)

        def transpose(dst, src, k=128):
            return nc.tensor.transpose(dst, src, ident[0:k, 0:k])

        bk, key = banks.take()
        transpose(bk[:, 0:128], rows[:, 0, :])
        tk = PE(lambda e: transpose(bk[:, 128:192], rows[0:64, 1, :], 64))
        V(lambda e: e.tensor_copy(colA[:, :], bk[:, 0:128]), tk)
        t_col = V(lambda e: e.tensor_copy(colB[:, :], bk[:, 128:192]))
        banks.free(key, t_col)
        t_masks = V(lambda e: e.tensor_copy(masks[:, :, :], mstage), t_mst)
        SP.wait(t_rows)
        W.load()

        cc = colA[:, 0:16].rearrange("p (s k) -> p s k", s=2)
        tk = A(lambda e: e.activation(sil[:, :, :], cc, ACT.Sigmoid), t_col)
        t_sil = V(lambda e: e.tensor_tensor(sil[:, :, :], sil[:, :, :], cc, ALU.mult), tk)
        bmod = colA[:, 64:112]

        V(lambda e: e.memset(mrow[:, :], 0.0))

        def mod_products(row, free=None):
            bk, key = banks.take()
            w = W.get()
            PE.wait(t_sil)
            for k in range(8):
                r = 32 * (k % 4)
                mm = lambda e: e.matmul(bk[r:r + 2, :], sil[:, :, k], w[:, k, :], start=(k < 4), stop=(k >= 4))
                tk = PE(mm) if k >= 4 else mm(nc.tensor)
            W.done()
            V.wait(free)
            for c in range(4):
                t = V(lambda e: e.tensor_copy(row[32 * c:32 * c + 2, :], bk[32 * c:32 * c + 2, :]), tk)
            banks.free(key, t)
            return row, t

        def mod_columns(j0, state):
            row, t = state
            bt, kt_ = banks.take()
            PE.wait(t)
            for j in range(4):
                mod_columns.read = PE(lambda e: transpose(bt[:, 128 * j:128 * j + 128], row[:, 128 * j:128 * j + 128]))
            o = modc[:, j0:j0 + 4, :]
            t = V(lambda e: e.tensor_reduce(o, bt.rearrange("p (j c x) -> p j x c", j=4, c=4)[:, :, 0:2, :], AX, ALU.add),
                  mod_columns.read)
            banks.free(kt_, t)
            return V(lambda e: e.tensor_tensor(o, o, bmod[:, j0:j0 + 4].unsqueeze(2).broadcast_to([128, 4, 2]), ALU.add))

        def inv_root(dst, src, scale):
            t = V(lambda e: e.tensor_scalar(dst, src, scale, EPS, ALU.mult, ALU.add))
            t = A(lambda e: e.activation(dst, dst, ACT.Sqrt), t)
            return V(lambda e: e.reciprocal(dst, dst), t)

        xt = sb("xt", [128, 6, 1024], at=base)
        mrow2 = sb("mrow2", [128, 512], at=base)
        V(lambda e: e.memset(mrow2[:, :], 0.0))
        sqj = sb("sqj", [128, 1024], at=base)
        s_x = sem("s_x")
        nc.gpsimd.dma_start(xt[:, 0:2, :], d["ctx"].rearrange("(t p) n -> p t n", p=128)).then_inc(s_x, 16)
        nc.gpsimd.dma_start(xt[:, 2:6, :], d["x"].rearrange("(t p) n -> p t n", p=128)).then_inc(s_x, 16)
        for i in range(6):
            tk = A(lambda e, i=i: e.activation(sqj[:, :], xt[:, i, :], ACT.Square, accum_out=ss[:, i:i + 1]), (s_x, 32))
        V.wait(tk)
        inv_root(ss[:, 0:6], ss[:, 0:6], 1.0 / 1024)
        for i in range(6):
            t_xn = V(lambda e, i=i: e.tensor_scalar(xt[:, i, :], xt[:, i, :], ss[:, i:i + 1], None, ALU.mult))
        state, read = None, [None, None]
        for j in range(5):
            last_state = state
            if j < 4:
                state = mod_products((mrow, mrow2)[j % 2], read[j % 2])
            if j:
                t_mod = mod_columns(4 * j - 4, last_state)
                read[(j - 1) % 2] = mod_columns.read
        for s in range(2):
            t_A1 = V(lambda e, s=s: e.scalar_tensor_tensor(A1[:, s, :], modc[:, 8:16, s], 1.0, colA[:, 16:24],
                                                           ALU.add, ALU.mult))
        PE.wait(t_xn)
        for k in range(8):
            b1, k1 = banks.take()
            for i in range(4):
                mm = lambda e, i=i: transpose(b1[:, 128 * i:128 * i + 128], xt[:, 2 + i, 128 * k:128 * k + 128])
                tk = PE(mm) if i == 3 else mm(nc.tensor)
            t1 = V(lambda e: e.tensor_scalar(hT[:, k, 256:768], b1, A1[:, 0, k:k + 1], modc[:, k, 0:1],
                                             ALU.mult, ALU.add), tk)
            banks.free(k1, t1)
            b2, k2 = banks.take()
            transpose(b2[:, 0:128], xt[:, 0, 128 * k:128 * k + 128])
            tk = PE(lambda e: transpose(b2[:, 128:256], xt[:, 1, 128 * k:128 * k + 128]))
            A.wait(t_A1)
            t2 = A(lambda e: e.activation(hT[:, k, 0:256], b2[:, 0:256], ACT.Identity, bias=modc[:, k, 1:2],
                                          scale=A1[:, 1, k:k + 1]), tk)
            banks.free(k2, t2)
        t_xt_free = PE.last
        PE.wait(t1, t2)

        def proj(dst, pairs):
            m = len(pairs)
            for i, (l, r) in enumerate(pairs):
                f = lambda e, l=l, r=r, i=i: e.matmul(dst, l, r, start=(i == 0), stop=(i == m - 1))
                if i == m - 1:
                    return PE(f)
                f(nc.tensor)

        slot2 = Region(keep, 0, KEEP)
        oattT = sb("oattT", [128, 4, 512], at=slot2)
        oT = sb("oT", [128, 4, 512], at=slot2)
        att, att2 = Region(keep, KEEP, TOP), Region(dyn, 0, ND)
        qT = sb("qT", [128, 4, 512], at=att)
        kz = sb("kz", [128, 2, 768], at=att)
        avs = sb("avs", [128, 6, 128], at=att2)
        pb = sb("pb", [128, 2, 768], at=att)
        pT = sb("pT", [128, 2, 768], at=att2)
        ot = sb("ot", [128, 2, 512], at=att2)
        st = sb("st", [128, 4, 3], at=att2)
        hg = Region(dyn, att2.at, ND)
        qh = sb("qh", [128, 2, 512], at=hg)
        vh = sb("vh", [128, 6, 256], at=hg)
        KK = sb("KK", [128, 2, 768], at=hg)
        GG = sb("GG", [128, 2, 768], at=hg)
        LF = sb("LF", [128, 2, 768], at=hg)
        lbt = sb("lbt", [128, 6, 8], at=hg)
        reset = sb("reset", [128, 768], U8, at=hg)
        dec = sb("dec", [128, 2, 6], at=hg)
        pre = Region(dyn, hg.at, ND)
        X1 = sb("X1", [128, 2, 512], at=hg)
        Ys = [sb(f"Y{i}", [128, 2, 512], at=hg) for i in range(2)]
        SS = sb("SS", [128, 4, 2, 128], at=hg)
        qe = sb("qe", [128, 2, 512], at=hg)
        keT = sb("keT", [128, 5, 256], at=hg)
        St = sb("St", [128, 5, 256], at=hg)
        Xs = [keT[:, 0:4, :].rearrange("p a b -> p (a b)").rearrange("p (h t) -> p h t", h=2), X1]
        aq = sb("aq", [128, 4, 512], at=pre)
        akv = sb("akv", [128, 6, 128], at=pre)
        rope = sb("rope", [128, 4, 2, 64], at=pre)
        tA = sb("tA", [128, 2048], at=pre)
        tC = sb("tC", [128, 2, 512], at=pre)
        rr = sb("rr", [128, 32], at=pre)
        V.wait(t_xt_free)
        A.wait(t_xt_free)
        t_kz = G(lambda e: e.memset(kz[:, :, :], 0.0), t_xt_free)
        t_rope = dma(A, rope[:, :, :, :], d["k_rope"], small[3], t1)

        w = W.get()
        for i in range(4):
            bk, key = banks.take()
            tk = proj(bk, [(hT[:, k, 256 + 128 * i:384 + 128 * i], w[:, k, :]) for k in range(8)])
            t_aq = A(lambda e: e.copy(aq[:, i, :], bk), tk)
            banks.free(key, t_aq)
        W.done()
        w = W.get()
        for i in range(6):
            bk, key = banks.take()
            tk = proj(bk[:, 0:256], [(hT[:, k, 128 * i:128 * i + 128], w[:, k, :]) for k in range(8)])
            A(lambda e: e.copy(akv[:, i, :], bk[:, 0:128]), tk)
            t_ak = A(lambda e: e.copy(avs[:, i, :], bk[:, 128:256]))
            banks.free(key, t_ak)
        W.done()

        def head_norm(src, nt, nh, gain, scale, *tokens):
            n = nt * nh
            sq4 = tA[:, 0:64 * n].rearrange("p (t h e) -> p t h e", h=nh, e=64)
            V(lambda e: e.tensor_tensor(sq4, src, src, ALU.mult), *tokens)
            V(lambda e: e.tensor_reduce(rr[:, 0:n], tA[:, 0:64 * n].rearrange("p (n e) -> p n e", e=64), AX, ALU.add))
            inv_root(rr[:, 0:n], rr[:, 0:n], 1.0 / 64)
            if scale != 1.0:
                V(lambda e: e.tensor_scalar(rr[:, 0:n], rr[:, 0:n], scale, None, ALU.mult))
            r4 = rr[:, 0:n].rearrange("p (t h) -> p t h", h=nh).unsqueeze(3).broadcast_to([128, nt, nh, 64])
            V(lambda e: e.tensor_tensor(src, src, r4, ALU.mult))
            g4 = gain.unsqueeze(1).unsqueeze(1).broadcast_to([128, nt, nh, 64])
            return V(lambda e: e.tensor_tensor(src, src, g4, ALU.mult))

        def rotate(src, nt, nh, dst):
            s4 = src.rearrange("p t h (a u f) -> p t (h a) u f", a=2, u=2)
            sw = tA[:, 0:64 * nt * nh].rearrange("p (t h u f) -> p t h u f", t=nt, u=2, f=16)
            V(lambda e: e.tensor_copy(sw[:, :, :, 0, :], s4[:, :, :, 1, :]))
            V(lambda e: e.tensor_copy(sw[:, :, :, 1, :], s4[:, :, :, 0, :]))
            a4 = tA[:, 0:64 * nt * nh].rearrange("p (t h e) -> p t h e", h=nh, e=64)
            sn = rope[:, :, 1, :].unsqueeze(2).broadcast_to([128, nt, nh, 64])
            cs = rope[:, :, 0, :].unsqueeze(2).broadcast_to([128, nt, nh, 64])
            V(lambda e: e.tensor_tensor(a4, a4, sn, ALU.mult))
            V(lambda e: e.tensor_tensor(src, src, cs, ALU.mult))
            for i in range(nt):
                yield dst(i, src[:, i], a4[:, i])

        def attention1():
            its = [(i, h) for i in range(4) for h in range(8)]
            e_done, rel_p, t_pT, rel_pT, rel_ot, turned = {}, {}, {}, {}, {}, []
            PE.wait(t_qT)
            for n in range(34):
                if n < 32:
                    i, h = its[n]
                    s = n % 2
                    bk, key = banks.take(2)
                    qq = qT[:, h % 4, 128 * i:128 * i + 128]
                    nc.tensor.matmul(bk[:, 0:512], qq, kz[:, h // 4, 0:512], start=True, stop=True)
                    tk = PE(lambda e: e.matmul(bk[:, 512:768], qq, kz[:, h // 4, 512:768], start=True, stop=True))
                    t = V(lambda e: e.tensor_reduce(st[:, n % 4, 0:1], bk[:, 0:768], AX, ALU.max, negate=True), tk)
                    t = A(lambda e: e.activation(pb[:, s, :], bk[:, 0:768], ACT.Exp, bias=st[:, n % 4, 0:1],
                                                 accum_out=st[:, n % 4, 1:2]), t, rel_p.get(n - 2))
                    banks.free(key, t)
                    e_done[n] = t
                    yield
                if 1 <= n < 33:
                    m = n - 1
                    bk, key = banks.take(2)
                    PE.wait(e_done[m])
                    for c in range(6):
                        mm = lambda e: transpose(bk[:, 128 * c:128 * c + 128], pb[:, m % 2, 128 * c:128 * c + 128])
                        tk = PE(mm) if c == 5 else mm(nc.tensor)
                    rel_p[m] = tk
                    t = A(lambda e: e.copy(pT[:, m % 2, :], bk[:, 0:768]), tk, rel_pT.get(m - 2))
                    banks.free(key, t)
                    t_pT[m] = t
                if n >= 2:
                    m = n - 2
                    i, h = its[m]
                    g = h // 4
                    bo, ko = banks.take()
                    PE.wait(t_pT[m])
                    tk = proj(bo[:, 0:128], [(pT[:, m % 2, 128 * c:128 * c + 128], avs[:, c, :]) for c in range(6)])
                    rel_pT[m] = tk
                    V(lambda e: e.reciprocal(st[:, m % 4, 2:3], st[:, m % 4, 1:2]), e_done[m])
                    t = V(lambda e: e.tensor_scalar(ot[:, i % 2, 64 * h:64 * h + 64], bo[:, 64 * g:64 * g + 64],
                                                    st[:, m % 4, 2:3], None, ALU.mult), tk, rel_ot.get(i - 2))
                    banks.free(ko, t)
                    if h == 7:
                        turned.append((i, t))
                if turned:
                    i, t = turned.pop()
                    bt, kt_ = banks.take()
                    PE.wait(t)
                    for j in range(4):
                        mm = lambda e: transpose(bt[:, 128 * j:128 * j + 128], ot[:, i % 2, 128 * j:128 * j + 128])
                        tk = PE(mm) if j == 3 else mm(nc.tensor)
                    rel_ot[i] = tk
                    t = A(lambda e: e.copy(oattT[:, :, 128 * i:128 * i + 128],
                                           bt.rearrange("p (j q) -> p j q", j=4)), tk)
                    banks.free(kt_, t)
                yield

        lb, omlb = lbt[:, 4, :], lbt[:, 5, :]
        lg = colB[:, 0:16].rearrange("p (r l h) -> p r l h", r=2, l=2)
        l3 = lbt[:, :, :].rearrange("p i (r h) -> p i r h", r=2)
        V(lambda e: e.tensor_tensor(l3[:, 0], lg[:, :, 0, :], lg[:, :, 1, :], ALU.max))
        V(lambda e: e.tensor_tensor(l3[:, 1], lg[:, :, 0, :], l3[:, 0], ALU.subtract))
        t = V(lambda e: e.tensor_tensor(l3[:, 2], lg[:, :, 1, :], l3[:, 0], ALU.subtract))
        t = A(lambda e: e.activation(lbt[:, 1:3, :], lbt[:, 1:3, :], ACT.Exp), t)
        V(lambda e: e.tensor_tensor(lbt[:, 3, :], lbt[:, 1, :], lbt[:, 2, :], ALU.add), t)
        V(lambda e: e.reciprocal(lbt[:, 3, :], lbt[:, 3, :]))
        V(lambda e: e.tensor_tensor(lb, lbt[:, 1, :], lbt[:, 3, :], ALU.mult))
        V(lambda e: e.tensor_tensor(omlb, lbt[:, 2, :], lbt[:, 3, :], ALU.mult))
        V(lambda e: e.memset(reset[:, :], 1))
        V(lambda e: e.memset(reset[:, 0:768:128], 0))

        level_banks = Banks(6, 8)
        t_mods = []

        def scan():
            t_of = None
            t_y = [None, None]
            for hp in range(2):
                for r in range(2):
                    w = W.get()
                    A.wait(V.last, G.last, PE.last)
                    for h in range(2):
                        bk, key = banks.take(2)
                        proj(bk[:, 0:512], [(w[:, k, 128 * h:128 * h + 128], hT[:, k, 256:768]) for k in range(8)])
                        tk = proj(bk[:, 512:768], [(w[:, k, 128 * h:128 * h + 128], hT[:, k, 0:256]) for k in range(8)])
                        for dst, sc in ((LF, 1.0), (KK, -1.0)):
                            A(lambda e: e.activation(dst[:, h, 256:768], bk[:, 0:512], ACT.Sigmoid, scale=sc), tk)
                            t = A(lambda e: e.activation(dst[:, h, 0:256], bk[:, 512:768], ACT.Sigmoid, scale=sc))
                        banks.free(key, t)
                        yield
                    W.done()
                    ms = mod_products(mrow, mod_columns.read)
                    for h in range(2):
                        i = 4 * r + 2 * hp + h
                        V(lambda e: e.tensor_scalar(LF[:, h, :], LF[:, h, :], omlb[:, i:i + 1], lb[:, i:i + 1],
                                                    ALU.mult, ALU.add), t)
                        t_kk = V(lambda e: e.tensor_scalar(KK[:, h, :], KK[:, h, :], omlb[:, i:i + 1], None, ALU.mult))
                    t = A(lambda e: e.activation(LF[:, :, :], LF[:, :, :], ACT.Ln), t_kk)
                    yield
                    mod_columns(16 + 4 * (4 * hp + 3 * r), ms)
                    if r == 0:
                        w = W.get()
                        A.wait(V.last, PE.last)
                        for h in range(2):
                            bk, key = banks.take()
                            tk = proj(bk, [(w[:, k, 128 * h:128 * h + 128], hT[:, k, 256:768]) for k in range(8)])
                            t_q = A(lambda e: e.copy(qh[:, h, :], bk), tk)
                            banks.free(key, t_q)
                        W.done()
                        yield
                    for h in range(2):
                        t_scan = V(lambda e: e.tensor_tensor_scan(GG[:, h, :], reset[:, :], LF[:, h, :], 0.0,
                                                                  ALU.mult, ALU.add), t)
                    t_dec = V(lambda e: e.tensor_copy(
                        dec[:, :, :], GG[:, :, :].rearrange("p h (c t) -> p h c t", t=128)[:, :, :, 127]))
                    t_gg = t_dec
                    if r == 1:
                        t_gg = G(lambda e: e.tensor_tensor(GG[:, :, :], GG[:, :, :], LF[:, :, :], ALU.subtract), t_dec)
                    if r == 0:
                        w = W.get()
                        for i in range(6):
                            bk, key = banks.take()
                            tk = proj(bk[:, 0:256], [(hT[:, k, 128 * i:128 * i + 128], w[:, k, :]) for k in range(8)])
                            t_v = A(lambda e: e.copy(vh[:, i, :], bk[:, 0:256]), tk)
                            banks.free(key, t_v)
                            if i % 3 == 2:
                                yield
                        W.done()
                    else:
                        ms = mod_products(mrow, mod_columns.read)
                    V.wait(*t_pre, t_q)
                    A.wait(*t_pre)
                    G.wait(*t_pre)
                    T6 = dec[:, :, :].unsqueeze(3).broadcast_to([128, 2, 6, 128])
                    G6 = GG[:, :, :].rearrange("p h (c t) -> p h c t", t=128)
                    L6 = LF[:, :, :].rearrange("p h (c t) -> p h c t", t=128)
                    if r == 0:
                        t = A(lambda e: e.activation(X1[:, :, :], GG[:, :, 256:768], ACT.Exp), t_gg, V.last)
                        tl = G(lambda e: e.tensor_tensor(L6, T6, G6, ALU.subtract), t_dec)
                        tl = A(lambda e: e.activation(LF[:, :, :], LF[:, :, :], ACT.Exp), tl)
                    else:
                        t = G(lambda e: e.tensor_tensor(X1[:, :, :].rearrange("p h (c t) -> p h c t", t=128),
                                                        T6[:, :, 2:6, :], G6[:, :, 2:6, :], ALU.subtract), V.last)
                        tl = A(lambda e: e.activation(LF[:, :, :], GG[:, :, :], ACT.Exp), t_gg)
                        t = A(lambda e: e.activation(X1[:, :, :], X1[:, :, :], ACT.Exp), t)
                    V.wait(PE.last)
                    t_qe = V(lambda e: e.tensor_tensor(qe[:, :, :], X1[:, :, :], qh[:, :, :], ALU.mult), t)
                    t_ke = V(lambda e: e.tensor_tensor(LF[:, :, :], LF[:, :, :], KK[:, :, :], ALU.mult), tl)
                    t_dec = A(lambda e: e.activation(dec[:, :, :], dec[:, :, :], ACT.Exp), t_qe)
                    yield
                    if r:
                        mod_columns(20 + 16 * hp, ms)
                        ms = mod_products(mrow, mod_columns.read)
                    order = [0, 1, 2, 3, 4] if r == 0 else [1, 0, 5, 4, 3]
                    A.wait(V.last)
                    for n0 in range(0, 5, 2):
                        cs = order[n0:n0 + 2]
                        bk, key = banks.take()
                        PE.wait(t_ke)
                        for a, c in enumerate(cs):
                            for h in range(2):
                                o = 256 * a + 128 * h
                                mm = lambda e: transpose(bk[:, o:o + 128], LF[:, h, 128 * c:128 * c + 128])
                                tk = PE(mm) if h == 1 else mm(nc.tensor)
                        m = len(cs)
                        t_keT = A(lambda e: e.copy(keT[:, n0:n0 + m, :],
                                                   bk[:, 0:256 * m].rearrange("p (a x) -> p a x", a=m)), tk)
                        banks.free(key, t_keT)
                    if r:
                        t_mods.append(mod_columns(24 + 16 * hp, ms))
                    for c0 in range(0, 4, 2):
                        bk, key = banks.take()
                        PE.wait(t_q, t_kk)
                        for a in range(2):
                            for h in range(2):
                                c, o = c0 + a, 256 * a + 128 * h
                                mm = lambda e: e.matmul(bk[:, o:o + 128], KK[:, h, 256 + 128 * c:384 + 128 * c],
                                                        qh[:, h, 128 * c:128 * c + 128], start=True, stop=True)
                                tk = PE(mm) if a + h == 2 else mm(nc.tensor)
                        s4 = SS[:, c0:c0 + 2].rearrange("p c h t -> p (c h) t")
                        b4 = bk.rearrange("p (x t) -> p x t", x=4)
                        id4 = ident[:, :].unsqueeze(1).broadcast_to([128, 4, 128])
                        if r == 0:
                            V(lambda e: e.tensor_tensor(s4, b4, id4, ALU.mult), tk)
                            banks.free(key, V.last)
                        else:
                            y4 = Ys[0][:, :, :].rearrange("p h (x t) -> p (h x) t", t=128)[:, 4 * (c0 // 2):4 * (c0 // 2) + 4]
                            V(lambda e: e.tensor_tensor(y4, b4, id4, ALU.mult), tk)
                            banks.free(key, V.last)
                            V(lambda e: e.tensor_tensor(s4, s4, y4, ALU.add))
                    yield
                    PE.wait(t_keT, t_v)
                    V.wait(t_dec)
                    for n, c in enumerate(order):
                        bk, key = banks.take()
                        for h in range(2):
                            hs = slice(128 * h, 128 * h + 128)
                            mm = lambda e: e.matmul(bk[:, hs], keT[:, n, hs], vh[:, c, hs], start=True, stop=True)
                            tk = PE(mm) if h == 1 else mm(nc.tensor)
                        if n == 0:
                            t_st = V(lambda e: e.tensor_copy(St[:, 0, :], bk[:, 0:256]), tk)
                        else:
                            for h in range(2):
                                hs = slice(128 * h, 128 * h + 128)
                                t_st = V(lambda e: e.scalar_tensor_tensor(St[:, n, hs], St[:, n - 1, hs],
                                                                          dec[:, h, c:c + 1], bk[:, hs], ALU.mult,
                                                                          ALU.add), tk)
                        banks.free(key, t_st)
                        if n == 2:
                            yield
                    t_keT_read = tk
                    yield
                    t_x, t_mul, t_mm, got = {}, {-2: t_keT_read, -1: t_qe}, {}, {}

                    def views(l):
                        m = LEVELS[l]
                        v = lambda a: a.rearrange("p h (b u m) -> p h b u m", u=2, m=m)
                        return m, v(Xs[l % 2]), v(GG[:, :, 256:768]), v(KK[:, :, 256:768]), v(qh[:, :, :]), v(Ys[l % 2])

                    def exponents(l):
                        m, xv, gv, _, _, _ = views(l)
                        ref = gv[:, :, :, 0, m - 1:m] if r == 0 else gv[:, :, :, 1, 0:1]
                        ref = ref.broadcast_to([128, 2, 256 // m, m])
                        G(lambda e: e.tensor_tensor(xv[:, :, :, 0, :], ref, gv[:, :, :, 0, :], ALU.subtract),
                          t_mul[l - 2], t_gg)
                        t = G(lambda e: e.tensor_tensor(xv[:, :, :, 1, :], gv[:, :, :, 1, :], ref, ALU.subtract))
                        t_x[l] = A(lambda e: e.activation(Xs[l % 2], Xs[l % 2], ACT.Exp), t)

                    def select(l):
                        mk = masks[:, 7 * r + l, :].unsqueeze(1).broadcast_to([128, 4, 128])
                        for a in range(2):
                            bk, key, tk = got[l][a]
                            t = V(lambda e: e.copy_predicated(SS[:, 2 * a:2 * a + 2].rearrange("p c h t -> p (c h) t"),
                                                              mk, bk.rearrange("p (x t) -> p x t", x=4)), tk, t_masks)
                            banks.free(key, t)
                        return t

                    def scale(l):
                        _, xv, _, kv, qv, yv = views(l)
                        a, b = (kv, qv) if r == 0 else (qv, kv)
                        V.wait(t_x[l], t_y[l % 2])
                        V(lambda e: e.tensor_tensor(yv[:, :, :, 0, :], xv[:, :, :, 0, :], a[:, :, :, 0, :], ALU.mult))
                        t_mul[l] = V(lambda e: e.tensor_tensor(yv[:, :, :, 1, :], xv[:, :, :, 1, :], b[:, :, :, 1, :],
                                                               ALU.mult))

                    exponents(0)
                    exponents(1)
                    scale(0)
                    yield
                    for l in range(len(LEVELS)):
                        if l + 2 < len(LEVELS):
                            exponents(l + 2)
                        if l + 1 < len(LEVELS):
                            scale(l + 1)
                        PE.wait(t_mul[l])
                        got[l] = []
                        for a in range(2):
                            bk, key = level_banks.take()
                            for x in range(4):
                                c, h = 2 * a + x // 2, x % 2
                                yy = Ys[l % 2][:, h, 128 * c:128 * c + 128]
                                mm = lambda e: e.matmul(bk[:, 128 * x:128 * x + 128], yy, yy, start=True, stop=True)
                                tk = PE(mm) if x == 3 else mm(nc.tensor)
                            got[l].append((bk, key, tk))
                        t_y[l % 2] = tk
                        t_ss = select(l)
                        yield
                    PE.wait(t_st, t_qe, t_ss)
                    for c0 in range(0, 4, 2):
                        bk, key = banks.take()
                        for a in range(2):
                            for h in range(2):
                                c, o, hs = c0 + a, 256 * a + 128 * h, slice(128 * h, 128 * h + 128)
                                qc = qe[:, h, 128 * c:128 * c + 128]
                                if r == 0:
                                    tk = proj(bk[:, o:o + 128], [(St[:, 1 + c, hs], qc)])
                                else:
                                    tk = proj(bk[:, o:o + 128], [(vh[:, 2 + c, hs], SS[:, c, h, :]),
                                                                 (St[:, 4 - c, hs], qc)])
                        ov = oT[:, 2 * hp:2 * hp + 2, 128 * c0:128 * c0 + 256].rearrange("p h (a t) -> p a h t", a=2)
                        b4 = bk.rearrange("p (a h t) -> p a h t", a=2, h=2)
                        if r == 0:
                            t_of = A(lambda e: e.copy(ov, b4), tk)
                            banks.free(key, t_of)
                        else:
                            banks.free(key, V(lambda e: e.tensor_tensor(ov, b4, ov, ALU.add), tk, t_of))
                    yield

        two = scan()
        V.wait(t_gb, t_rope)
        k4 = akv[:, :, :].rearrange("p t (h e) -> p t h e", e=64)
        t_k = head_norm(k4, 6, 2, gb[:, 1, :], 1.0, t_ak)
        for t_k in rotate(k4[:, 2:6], 4, 2, lambda i, a, b: V(lambda e: e.tensor_tensor(a, a, b, ALU.add))):
            pass
        q4 = aq[:, :, :].rearrange("p t (h e) -> p t h e", e=64)
        head_norm(q4, 4, 8, gb[:, 0, :], 0.125, t_aq)
        next(two)
        next(two)
        for i in range(6):
            bk, key = banks.take()
            tk = PE(lambda e: transpose(bk[:, 0:128], akv[:, i, :]), t_k)
            for g in range(2):
                gs = slice(64 * g, 64 * g + 64)
                t = A(lambda e: e.copy(kz[gs, g, 128 * i:128 * i + 128], bk[gs, 0:128]), tk, t_kz)
            banks.free(key, t)
        next(two)
        rel_tC = [None, None]
        next(two)

        def put_q(i, a, b):
            o = tC[:, i % 2, :].rearrange("p (j g e) -> p g j e", g=2, e=64)
            t = V(lambda e: e.tensor_tensor(o, a.rearrange("p (g j) e -> p g j e", g=2),
                                            b.rearrange("p (g j) e -> p g j e", g=2), ALU.add), rel_tC[i % 2])
            bk, key = banks.take()
            PE.wait(t)
            for j in range(4):
                mm = lambda e: transpose(bk[:, 128 * j:128 * j + 128], tC[:, i % 2, 128 * j:128 * j + 128])
                tk = PE(mm) if j == 3 else mm(nc.tensor)
            rel_tC[i % 2] = tk
            t = A(lambda e: e.copy(qT[:, :, 128 * i:128 * i + 128], bk.rearrange("p (j q) -> p j q", j=4)), tk)
            banks.free(key, t)
            return t

        for n, t_qT in enumerate(rotate(q4, 4, 8, put_q)):
            if n == 1:
                next(two)
        t_pre = (V.last, A.last, PE.last)

        banks.hi, banks.at = 6, 0
        one = attention1()
        more = [one, two]
        while more:
            for g_ in list(more):
                if g_ in more and next(g_, "end") == "end":
                    more = [x for x in more if x is not g_]
        t_o = V.last
        t_hg_a = A.last
        banks.hi = 8

        def handover():
            last = (V.last, A.last, G.last, PE.last)
            for q in (V, A, G):
                q.wait(*last)

        def split(dst, src, *tokens):
            t = A(lambda e: e.copy(dst[0], src), *tokens)
            return V(lambda e: e.tensor_tensor(dst[1], src, dst[0].bitcast(F32), ALU.subtract), t)

        def split_scaled(dst, src, col, *tokens):
            t = A(lambda e: e.activation(dst[0], src, ACT.Copy, scale=col), *tokens)
            return V(lambda e: e.scalar_tensor_tensor(dst[1], src, col, dst[0].bitcast(F32), ALU.mult, ALU.subtract), t)

        class Parts:

            def __init__(self, tensor):
                self.t, self.n, self.free = tensor, 0, [None, None]

            def put(self, src):
                a, b = src.shape[1], src.shape[2]
                i = self.n % 2
                self.n += 1
                out = [self.t[:, i, x, 0:a * b].rearrange("p (a b) -> p a b", b=b) for x in range(2)]
                tok = split(out, src, self.free[i])
                return out, tok, i

        def run(parts, items, start=None):
            ahead = []
            for n in range(len(items) + 1):
                if n < len(items):
                    get, free, use = items[n]
                    out, tok, i = parts.put(get())
                    if free:
                        W.done(tok)
                    ahead.append((out, tok, i, use))
                    if n == 0 and start:
                        start()
                if n:
                    out, tok, i, use = ahead.pop(0)
                    PE.wait(tok)
                    use(out)
                    parts.free[i] = PE.last

        def products(dst, w, x, ks, first=True, last=True, ready=None):
            m = len(ks)
            for n, k in enumerate(ks):
                if ready:
                    PE.wait(ready[k])
                for j, (a, b) in enumerate(((0, 0), (0, 1), (1, 0))):
                    f = lambda e: e.matmul(dst, w(a, k), x(b, k), start=(first and n == 0 and j == 0),
                                           stop=(last and n == m - 1 and j == 2))
                    tk = PE(f) if n == m - 1 and j == 2 else f(nc.tensor)
            return tk

        def column_items(slab_cols, nk, xR, evac, ready=None):
            items = []
            state = {}
            total = sum(slab_cols)
            n = 0
            for ncol in slab_cols:
                for j in range(ncol):
                    def get(j=j):
                        if j == 0:
                            state["w"] = W.get(A)
                        return state["w"][:, :, 128 * j:128 * j + 128]

                    def use(out, n=n):
                        bk, key = banks.take()
                        tk = products(bk, lambda a, k: out[a][:, k, :], lambda b, k: xR[b][:, k, :], range(nk),
                                      ready=ready)
                        evac(n, bk, key, tk)
                    items.append((get, j == ncol - 1, use))
                    n += 1
            return items

        t_mod = V.last
        phase.close()
        handover()
        phase = ExitStack()
        hR = sb("hR1", [128, 2, 8, 512], F32R, at=phase)
        wR = sb("wR1", [128, 2, 2, 1024], F32R, at=phase)
        aR = sb("aR1", [128, 2, 4, 512], F32R, at=phase)
        small2 = sb("small2", [128, 2048], at=phase)
        r2 = Region(small2, 0, 2048)
        sg = sb("sg", [128, 2, 512], at=r2)
        rn = sb("rn", [128, 512], at=r2)
        tm = sb("tm", [128, 512], at=r2)
        sq1 = sb("sq1", [128, 2, 512], at=Region(keep, KEEP + 4096, TOP))
        parts = Parts(wR)
        h2 = (hR[:, 0], hR[:, 1])
        a2 = (aR[:, 0], aR[:, 1])
        PE.wait(t_o, t_hg_a)
        wr = hT[:, 0, 512:640].rearrange("p (k n) -> p k n", k=8)
        iot = hT[:, 1:3, 512:768]
        s_wr, s_iot = sem("s_wr"), sem("s_iot")
        def out_gate(h, bk, key, tk):
            s = h % 2
            t = A(lambda e: e.activation(sg[:, s, :], bk, ACT.Sigmoid), tk, t_og.get(h - 2))
            t = V(lambda e: e.tensor_tensor(sg[:, s, :], sg[:, s, :], bk, ALU.mult), t)
            banks.free(key, t)
            t = V(lambda e: e.tensor_tensor(tm[:, :], sg[:, s, :], oT[:, h, :], ALU.mult), t_og.get(h - 1))
            t_og[h] = split((aR[:, 0, h], aR[:, 1, h]), tm[:, :], t)

        t_og, t_so, t_sq, t_hR = {}, {}, {}, []

        def head_squares(h):
            t_sq[h] = A(lambda e: e.activation(sq1[:, h % 2, :], oT[:, h, :], ACT.Square), t_so.get(h - 2))

        def first_splits():
            head_squares(0)
            head_squares(1)
            t_hR.extend(split((hR[:, 0, k], hR[:, 1, k]), hT[:, k, 256:768]) for k in range(8))

        def head_norm1(h):
            bk, key = banks.take()
            t_so[h] = tk = PE(lambda e: e.matmul(bk, ones[:, :], sq1[:, h % 2, :], start=True, stop=True), t_sq[h])
            t = V(lambda e: e.tensor_scalar(rn[:, :], bk, 1.0 / 128, EPS, ALU.mult, ALU.add), tk)
            banks.free(key, t)
            t = A(lambda e: e.activation(rn[:, :], rn[:, :], ACT.Sqrt), t)
            if h < 2:
                head_squares(h + 2)
            V(lambda e: e.reciprocal(rn[:, :], rn[:, :]), t)
            V(lambda e: e.scalar_tensor_tensor(oT[:, h, :], rn[:, :], colA[:, 112 + h:113 + h], oT[:, h, :],
                                               ALU.mult, ALU.mult))

        def with_norm(h, item):
            get, free, use = item

            def both(out):
                head_norm1(h)
                use(out)
            return get, free, both

        gates = column_items([4], 8, h2, out_gate, t_hR)
        gates = [with_norm(h, item) for h, item in enumerate(gates)]
        uT = hT[:, :, 0:512]
        t_sg = {}

        def branch(br):
            items, state = [], {}
            for dt_ in range(8):
                def get_b(dt_=dt_):
                    return state["b"][:, :, 128 * dt_:128 * dt_ + 128]

                def get_g(dt_=dt_):
                    if dt_ == 0:
                        state["b"] = W.get(A)
                    if dt_ % 4 == 0:
                        state["g"] = W.get(A)
                    return state["g"][:, :, 128 * (dt_ % 4):128 * (dt_ % 4) + 128]

                def use_g(out, dt_=dt_):
                    bk, key = banks.take()
                    tk = products(bk, lambda a, k: out[a][:, k, :], lambda b, k: hR[:, b, k, :], range(8))
                    t_sg[dt_] = A(lambda e: e.activation(sg[:, dt_ % 2, :], bk, ACT.Sigmoid), tk,
                                  t_sg.get(("u", 8 * br + dt_ - 2)))
                    banks.free(key, t_sg[dt_])

                def use_b(out, dt_=dt_):
                    bk, key = banks.take()
                    if dt_ == 0:
                        PE.wait(t_a2[0] if br else t_og[3])
                    if br and dt_ == 7:
                        for k in range(7):
                            t_uR.append(split((hR[:, 0, k], hR[:, 1, k]), uT[:, k, :], V.last, PE.last))
                    tk = products(bk, lambda a, k: out[a][:, k, :], lambda b, k: aR[:, b, k, :], range(4))
                    s = dt_ % 2
                    if br == 0:
                        t = V(lambda e: e.tensor_tensor(uT[:, dt_, :], sg[:, s, :], bk, ALU.mult), tk, t_sg[dt_])
                        banks.free(key, t)
                    else:
                        t = V(lambda e: e.tensor_tensor(sg[:, s, :], sg[:, s, :], bk, ALU.mult), tk, t_sg[dt_])
                        banks.free(key, t)
                        t = V(lambda e: e.tensor_tensor(uT[:, dt_, :], uT[:, dt_, :], sg[:, s, :], ALU.add))
                        if 2 <= dt_ < 6:
                            turn_x(2 * dt_ - 4)
                            turn_x(2 * dt_ - 3)
                    t_sg[("u", 8 * br + dt_)] = t
                    if dt_ == 7 and br == 0:
                        turn_to_attention()
                    if dt_ == 7 and br == 1:
                        t_uR.append(split((hR[:, 0, 7], hR[:, 1, 7]), uT[:, 7, :], t))
                items += [(get_g, False, use_g), (get_b, dt_ == 7, use_b)]
            return items

        t_a2, t_uR, t_xs = [], [], {}
        top = Region(keep, KEEP, TOP)
        xT = sb("xT", [128, 8, 512], at=top)

        def turn_x(k):
            b1, k1 = banks.take()
            PE.wait((s_x2, 16))
            for i in range(4):
                mm = lambda e, i=i: transpose(b1[:, 128 * i:128 * i + 128], xk[:, i, 128 * k:128 * k + 128])
                tk = PE(mm) if i == 3 else mm(nc.tensor)
            t_xs[k] = A(lambda e: e.copy(xT[:, k, :], b1), tk)
            banks.free(k1, t_xs[k])

        xk = sb("xk", [128, 4, 1024], at=Region(keep, 0, KEEP))
        s_x2 = sem("s_x2")

        def turn_to_attention():
            A.wait(t_hR[-1])
            nc.scalar.dma_start(wr, d["w_router"].rearrange("(k p) n -> p k n", p=128)).then_inc(s_wr, 16)
            nc.scalar.dma_start(iot, d["k_iota"].rearrange("(a b) -> a b", a=2).partition_broadcast(128)).then_inc(s_iot, 16)
            for k in range(4):
                t = split((aR[:, 0, k], aR[:, 1, k]), oattT[:, k, :], PE.last)
            t_a2.append(t)
            A.wait(t)
            nc.scalar.dma_start(xk[:, :, :], d["x"].rearrange("(t p) n -> p t n", p=128)).then_inc(s_x2, 16)

        sq = sb("sq", [128, 2, 512], at=top)
        rinv = sb("rinv", [128, 512], at=top)

        class Squares:

            def __init__(self, nk, mats, pool):
                self.nk, self.mats = nk, mats
                self.banks = [pool.take() for _ in mats(0)]
                self.pending, self.rel = None, {}

            def add(self, k, src, tok):
                t = A(lambda e: e.activation(sq[:, k % 2, :], src, ACT.Square), tok, self.rel.get(k % 2))
                self.flush()
                self.pending = (k, t)

            def flush(self):
                if self.pending:
                    k, t = self.pending
                    for (bk, key), m in zip(self.banks, self.mats(k)):
                        self.rel[k % 2] = self.tok = PE(
                            lambda e: e.matmul(bk, m, sq[:, k % 2, :], start=(k == 0), stop=(k == self.nk - 1)), t)
                    self.pending = None

        def one_mat(k):
            return [ones[:, :]]

        def root(dst, total):
            total.flush()
            bk, key = total.banks[0]
            t = V(lambda e: e.tensor_scalar(dst, bk, 1.0 / 1024, EPS, ALU.mult, ALU.add), total.tok)
            banks.free(key, t)
            t = A(lambda e: e.activation(dst, dst, ACT.Sqrt), t)
            return V(lambda e: e.reciprocal(dst, dst), t)

        banks.hi, banks.at = 6, 0
        total = Squares(8, one_mat, Banks(6, 7))

        def add_y(n, bk, key, tk):
            t = V(lambda e: e.scalar_tensor_tensor(xT[:, n, :], bk, modc[:, 16 + n, 0:1], xT[:, n, :],
                                                   ALU.mult, ALU.add), tk, t_xs[n])
            banks.free(key, t)
            total.add(n, xT[:, n, :], t)

        run(parts, gates + branch(0) + branch(1) + column_items([4, 4], 8, h2, add_y, t_uR), first_splits)
        root(rinv[:, :], total)
        banks.hi = 8
        phase.close()
        handover()
        phase, rctx, mctx = ExitStack(), ExitStack(), ExitStack()
        held = sb("held", [128, 5216], at=phase)
        hR = sb("hR2", [128, 2, 8, 512], F32R, at=rctx)
        dyn = sb("dyn2", [128, ND - 5216 - 8192], at=mctx)

        def column_norm(srcT, nk, sq, rinv, tok):
            bk, key = banks.take()
            rel = [None, None]
            for k in range(nk):
                t = A(lambda e: e.activation(sq[:, k % 2, :], srcT[:, k, :], ACT.Square), tok, rel[k % 2])
                f = lambda e: e.matmul(bk, ones[:, :], sq[:, k % 2, :], start=(k == 0), stop=(k == nk - 1))
                rel[k % 2] = PE(f, t)
            t = V(lambda e: e.tensor_scalar(rinv, bk, 1.0 / (128 * nk), EPS, ALU.mult, ALU.add), PE.last)
            banks.free(key, t)
            t = A(lambda e: e.activation(rinv, rinv, ACT.Sqrt), t)
            return V(lambda e: e.reciprocal(rinv, rinv), t)

        moe, moe1, moe2 = Region(dyn, 0, ND - 5216 - 8192), Region(held, 0, 5216), Region(keep, 0, KEEP)
        h2T = hT[:, 0:8, 0:512]
        xeT = sb("xeT", [128, 8, 2, 128], at=moe1)
        h2k = sb("h2k", [128, 4, 1024], at=moe2)
        xe = sb("xe", [128, 1024], at=moe1)
        ye = sb("ye", [128, 2, 1024], at=moe1)
        PT = sb("PT", [128, 2, 512], at=moe)
        gmat = sb("gmat", [128, 8, 128], at=moe)
        hid = sb("hid", [128, 2, 512], at=moe)
        hidT = sb("hidT", [128, 8, 128], at=moe)
        lgt = sb("lgt", [128, 4, 16], at=moe1)
        lst = sb("lst", [128, 3, 4], at=moe1)
        aff = sb("aff", [16, 512], at=moe)
        gv = sb("gv", [16, 64], at=moe)
        iu = sb("iu", [16, 64], U32, at=moe)
        ifl = sb("ifl", [16, 64], at=moe)
        gi8 = sb("gi8", [8, 2, 128], at=moe)
        giT = sb("giT", [128, 2, 8], at=moe1)
        idx = sb("idx", [128, 8], U32, at=moe)
        s_h2, s_gi, s_ga = sem("s_h2"), sem("s_gi"), sem("s_ga")
        V(lambda e: e.scalar_tensor_tensor(AB[:, 0, :], modc[:, 32:40, 0], 1.0, colA[:, 24:32], ALU.add, ALU.mult))
        t_h2 = []
        for k in range(8):
            t = V(lambda e: e.scalar_tensor_tensor(h2T[:, k, :], xT[:, k, :], AB[:, 0, k:k + 1], rinv[:, :],
                                                   ALU.mult, ALU.mult))
            t_h2.append(A(lambda e: e.activation(h2T[:, k, :], h2T[:, k, :], ACT.Identity, bias=modc[:, 24 + k, 0:1]), t))
        bk, key = banks.take()
        PE.wait((s_wr, 16))
        for k in range(8):
            r = 32 * (k % 4)
            tk = PE(lambda e: e.matmul(bk[r:r + 16, :], wr[:, k, :], h2T[:, k, :], start=(k < 4), stop=(k >= 4)), t_h2[k])
        for c in range(4):
            t = V(lambda e: e.tensor_copy(mrow[32 * c:32 * c + 16, :], bk[32 * c:32 * c + 16, :]), tk)
        banks.free(key, t)
        bk, key = banks.take()
        PE.wait(t)
        for i in range(4):
            mm = lambda e: transpose(bk[:, 128 * i:128 * i + 128], mrow[:, 128 * i:128 * i + 128])
            tk = PE(mm) if i == 3 else mm(nc.tensor)
        t = V(lambda e: e.tensor_reduce(lgt[:, :, :], bk.rearrange("p (i c x) -> p i x c", i=4, c=4)[:, :, 0:16, :],
                                        AX, ALU.add), tk)
        banks.free(key, t)
        V(lambda e: e.tensor_reduce(lst[:, 0, :], lgt[:, :, :], AX, ALU.max))
        t = V(lambda e: e.tensor_tensor(lgt[:, :, :], lgt[:, :, :], lst[:, 0, :].unsqueeze(2).broadcast_to([128, 4, 16]),
                                        ALU.subtract))
        t = A(lambda e: e.activation(lgt[:, :, :], lgt[:, :, :], ACT.Exp), t)
        V(lambda e: e.tensor_reduce(lst[:, 1, :], lgt[:, :, :], AX, ALU.add), t)
        V(lambda e: e.reciprocal(lst[:, 2, :], lst[:, 1, :]))
        t = V(lambda e: e.tensor_tensor(lgt[:, :, :], lgt[:, :, :], lst[:, 2, :].unsqueeze(2).broadcast_to([128, 4, 16]),
                                        ALU.mult))
        bk, key = banks.take()
        PE.wait(t)
        for i in range(4):
            tk = PE(lambda e: transpose(bk[0:16, 128 * i:128 * i + 128], lgt[:, i, :]))
        t = V(lambda e: e.tensor_copy(aff[:, :], bk[0:16, :]), tk)
        banks.free(key, t)
        h2d = nc.dram_tensor("h2_scratch", (512, 1024), F32, kind="Internal").ap()
        for i in range(4):
            for q in range(2):
                bk, key = banks.take()
                for k in range(4):
                    mm = lambda e, k=k: transpose(bk[:, 128 * k:128 * k + 128],
                                                  h2T[:, 4 * q + k, 128 * i:128 * i + 128])
                    tk = PE(mm) if k == 3 else mm(nc.tensor)
                t_h2k = A(lambda e: e.copy(h2k[:, i, 512 * q:512 * q + 512], bk), tk)
                banks.free(key, t_h2k)
        A.wait(t_h2k)
        nc.scalar.dma_start(h2d.rearrange("(t p) n -> p t n", p=128), h2k[:, :, :]).then_inc(s_h2, 16)
        for r in range(8):
            rs = slice(8 * r, 8 * r + 8)
            V(lambda e: e.max(gv[:, rs], aff[:, :]))
            V(lambda e: e.max_index(iu[:, rs], gv[:, rs], aff[:, :]))
            if r < 7:
                V(lambda e: e.match_replace(aff[:, :], gv[:, rs], aff[:, :], -1.0))
        t = V(lambda e: e.tensor_copy(ifl[:, :], iu[:, :]))
        A.wait(t)
        for e2 in range(2):
            for n, src in enumerate((gv, ifl)):
                nc.scalar.dma_start(gi8[:, n, 64 * e2:64 * e2 + 64], src[e2:16:2, :]).then_inc(s_gi, 16)
        bk, key = banks.take()
        PE.wait((s_gi, 64))
        transpose(bk[:, 0:8], gi8[:, 0, :], 8)
        tk = PE(lambda e: transpose(bk[:, 8:16], gi8[:, 1, :], 8))
        V(lambda e: e.tensor_copy(giT[:, :, :], bk[:, 0:16].rearrange("p (a b) -> p a b", a=2)), tk)
        t_idx = V(lambda e: e.tensor_copy(idx[:, :], bk[:, 8:16]))
        banks.free(key, t_idx)

        def gather(p, tok):
            G.wait(t_idx, (s_h2, 16), tok)
            nc.gpsimd.indirect_dma_start(xe[:, :], None, h2d, bass.IndirectOffsetOnAxis(ap=idx[:, p:p + 1], axis=0))\
                .then_inc(s_ga, 16)
            return (s_ga, 16 * (p + 1))

        def expert_in(p, ta):
            for q in range(2):
                bk, key = banks.take()
                PE.wait(ta)
                for k in range(4):
                    mm = lambda e, k=k: transpose(bk[:, 128 * k:128 * k + 128],
                                                  xe[:, 512 * q + 128 * k:512 * q + 128 * k + 128])
                    tk = PE(mm) if k == 3 else mm(nc.tensor)
                t = A(lambda e: e.copy(xeT[:, 4 * q:4 * q + 4, p % 2, :], bk.rearrange("p (k s) -> p k s", k=4)), tk)
                banks.free(key, t)
            return tk, t

        tg_ = gather(0, None)
        t_free, t_xe = expert_in(0, tg_)
        rel_hid, rel_hidT = None, None

        def pair_product(stat):
            out = []
            for hf in range(2):
                bk, key = banks.take()
                for kh in range(2):
                    ww = [W.get(), W.get()]
                    for k in range(4):
                        for e2 in range(2):
                            es = slice(64 * e2, 64 * e2 + 64)
                            f = lambda e: e.matmul(bk[es, :], stat[:, 4 * kh + k, es], ww[e2][:, k, :],
                                                   start=(kh == 0 and k == 0), stop=(kh == 1 and k == 3))
                            tk = PE(f) if k == 3 else f(nc.tensor)
                    W.done()
                out.append((bk, key, tk))
            return out

        t_sc = {}

        def scatter(p, after=None):
            for k in range(8):
                bk, key = banks.take()
                tk = PE(lambda e: e.matmul(bk, ye[:, p % 2, 128 * k:128 * k + 128], PT[:, p % 2, :], start=True, stop=True),
                        t_sc[("ye", p)])
                t = V(lambda e: e.scalar_tensor_tensor(xT[:, k, :], bk, modc[:, 40 + k, 0:1], xT[:, k, :],
                                                       ALU.mult, ALU.add), tk)
                banks.free(key, t)
                if after:
                    after(k, t)
            t_sc[p] = tk

        for k in range(8):
            G(lambda e: e.tensor_scalar(gmat[:, k, :], ones[:, :], colA[:, 32 + k:33 + k], colA[:, 32 + k:33 + k],
                                        ALU.mult, ALU.mult))
        G(lambda e: e.tensor_tensor(AB[:, 1, :], colA[:, 32:40], colA[:, 40:48], ALU.mult))
        for p in range(8):
            if p < 7:
                tg_ = gather(p + 1, t_free)
            PE.wait(t_xe)
            bg = pair_product(xeT[:, :, p % 2, :])
            t = None
            for hf in range(2):
                bk, key, tk = bg[hf]
                t = A(lambda e: e.activation(hid[:, hf, :], bk, ACT.Sigmoid), tk, rel_hid)
                t = V(lambda e: e.tensor_tensor(hid[:, hf, :], hid[:, hf, :], bk, ALU.mult), t)
                banks.free(key, t)
            if p:
                scatter(p - 1)
            bu = pair_product(xeT[:, :, p % 2, :])
            if p < 7:
                t_free, t_xe = expert_in(p + 1, tg_)
            for hf in range(2):
                bk, key, tk = bu[hf]
                t = V(lambda e: e.tensor_tensor(hid[:, hf, :], hid[:, hf, :], bk, ALU.mult), tk)
                banks.free(key, t)
                bt, kt_ = banks.take()
                PE.wait(t)
                for k in range(4):
                    mm = lambda e: transpose(bt[:, 128 * k:128 * k + 128], hid[:, hf, 128 * k:128 * k + 128])
                    tk = PE(mm) if k == 3 else mm(nc.tensor)
                t_hT = A(lambda e: e.copy(hidT[:, 4 * hf:4 * hf + 4, :], bt.rearrange("p (k s) -> p k s", k=4)), tk,
                         rel_hidT)
                banks.free(kt_, t_hT)
            rel_hid = tk
            PE.wait(t_hT)
            for hf, (bk, key, tk) in enumerate(pair_product(hidT)):
                t_yek = V(lambda e: e.tensor_scalar(ye[:, p % 2, 512 * hf:512 * hf + 512], bk, giT[:, 0, p:p + 1], None,
                                                    ALU.mult), tk, t_sc.get(p - 2))
                banks.free(key, t_yek)
            t_sc[("ye", p)] = V(lambda e: e.tensor_scalar(PT[:, p % 2, :].rearrange("p (a b) -> p a b", a=2), iot,
                                                          giT[:, 1, p:p + 1], None, ALU.is_equal), (s_iot, 16))
            rel_hidT = PE.last
        banks.hi, banks.at = 6, 0
        total = Squares(8, lambda k: [ones[:, :], gmat[:, k, :]], Banks(6, 8))
        PE.wait(G.last)
        A.wait(G.last)
        t_h3 = []

        def last_add(k, t):
            total.add(k, xT[:, k, :], t)
            t_h3.append(split_scaled((hR[:, 0, k], hR[:, 1, k]), xT[:, k, :], AB[:, 1, k:k + 1], t))

        scatter(7, last_add)
        total.flush()
        t_moe = PE.last
        (b1_, key1), (b2_, key2) = total.banks
        cN, rm = sq[:, 0, :], sq[:, 1, :]
        banks.hi = 8
        mctx.close()
        wR = sb("wR2", [128, 2, 2, 1024], F32R, at=rctx)
        tA1 = sb("tA1", [128, 1024], at=rctx)
        A.wait(t_moe)
        parts = Parts(wR)
        t_cs = []

        def token_factors():
            V(lambda e: e.tensor_scalar(rinv[:, :], b1_, 1.0 / 1024, EPS, ALU.mult, ALU.add), t_moe)
            V(lambda e: e.tensor_scalar(rm, rinv[:, :], EPS, None, ALU.mult))
            t = V(lambda e: e.scalar_tensor_tensor(cN, b2_, 1.0 / 1024, rm, ALU.mult, ALU.add))
            banks.free(key1, t)
            banks.free(key2, t)
            A(lambda e: e.activation(rinv[:, :], rinv[:, :], ACT.Sqrt), t)
            t = A(lambda e: e.activation(cN, cN, ACT.Sqrt))
            V(lambda e: e.reciprocal(cN, cN), t)
            t_c = V(lambda e: e.reciprocal(rinv[:, :], rinv[:, :]))
            t_cs.append(t_c)

        h2 = (hR[:, 0], hR[:, 1])
        cT = ss[:, 0:4]

        def x3_and_columns():
            bk, key = banks.take()
            PE.wait(t_cs[0])
            for i in range(4):
                mm = lambda e: transpose(bk[:, 128 * i:128 * i + 128], cN[:, 128 * i:128 * i + 128])
                tk = PE(mm) if i == 3 else mm(nc.tensor)
            t = V(lambda e: e.tensor_copy(cT, bk.rearrange("p (i t) -> p i t", i=4)[:, :, 0]), tk)
            banks.free(key, t)
            A.wait(t)
            for k in range(8):
                V(lambda e: e.scalar_tensor_tensor(xT[:, k, :], xT[:, k, :], colA[:, 32 + k:33 + k], rinv[:, :],
                                                   ALU.mult, ALU.mult), t_h3[k])

        mixT = sb("mixT", [128, 8, 512], at=Region(keep, 0, KEEP))
        hl = Region(held, 0, 5216)
        kcv = sb("kcv", [128, 2, 512], at=hl)
        ksw = sb("ksw", [128, 4, 256], at=hl)
        kww = sb("kww", [128, 4, 256], at=hl)
        gat = sb("gat", [128, 4, 24], at=hl)
        q2 = sb("q2", [128, 4, 512], at=hl)
        hreg = hT[:, :, :].rearrange("p k t -> p (k t)")
        cv = Region(hreg, 0, 6144)
        uh = sb("uh", [128, 4, 514], at=cv)
        vc = sb("vc", [128, 4, 512], at=cv)
        dist = sb("dist", [128, 512], at=cv)
        cb = sb("cb", [128, 4, 8, 32], at=cv)
        wc2 = sb("wc2", [128, 2, 2, 64], at=cv)
        cmk = sb("cmk", [128, 4, 32], at=cv)
        rr = sb("rr2", [128, 32], at=cv)
        kz2 = sb("kz2", [128, 2, 2, 512], at=Region(hreg, 0, 2048))
        shA = sb("shA", [128, 4, 512], at=Region(keep, 0, 2048))
        s_k2, s_sh = sem("s_k2"), sem("s_sh")
        t_kz2 = {}

        def second_loads():
            A.wait(t_raw[1])
            for v in range(2):
                for g in range(2):
                    src = kcv[64 * g:64 * g + 64, v, :]
                    nc.scalar.dma_start(shA[0:64, 2 * v + g, :], src).then_inc(s_sh, 16)
                    nc.scalar.dma_start(shA[64:128, 2 * v + g, 0:511], src[:, 1:512]).then_inc(s_sh, 16)
            nc.scalar.dma_start(wc2[:, :, :, :], d["w_cmp2_2"].rearrange("v (k p) n -> p v k n", p=128)).then_inc(s_k2, 16)
            nc.scalar.dma_start(dist[:, :], d["k_dist"]).then_inc(s_k2, 16)
            nc.scalar.dma_start(cb[:, :, :, :], d["k_cb"]).then_inc(s_k2, 16)
            nc.scalar.dma_start(cmk[:, :, :], d["k_cm"]).then_inc(s_k2, 16)

        def head_norm2(src, nt, nh, gain, scale, tA, *tokens, P=128):
            n = nt * nh
            V(lambda e: e.tensor_tensor(tA[0:P, 0:64 * n].rearrange("p (t h e) -> p t h e", h=nh, e=64), src, src,
                                        ALU.mult), *tokens)
            V(lambda e: e.tensor_reduce(rr[0:P, 0:n], tA[0:P, 0:64 * n].rearrange("p (n e) -> p n e", e=64), AX, ALU.add))
            inv_root(rr[0:P, 0:n], rr[0:P, 0:n], 1.0 / 64)
            if scale != 1.0:
                V(lambda e: e.tensor_scalar(rr[0:P, 0:n], rr[0:P, 0:n], scale, None, ALU.mult))
            r4 = rr[0:P, 0:n].rearrange("p (t h) -> p t h", h=nh).unsqueeze(3).broadcast_to([P, nt, nh, 64])
            V(lambda e: e.tensor_tensor(src, src, r4, ALU.mult))
            g4 = gain.unsqueeze(1).unsqueeze(1).broadcast_to([P, nt, nh, 64])
            return V(lambda e: e.tensor_tensor(src, src, g4, ALU.mult))

        t_hn = {}

        def norm_keys(v):
            src = (ksw, kww)[v][:, :, 0:128].rearrange("p t (h e) -> p t h e", e=64)
            t_hn[v] = head_norm2(src, 4, 2, gb[:, 4 + v, :], 1.0, tA1, t_tok[v])

        def norm_queries(half):
            src = q2[:, 2 * half:2 * half + 2, :].rearrange("p t (h e) -> p t h e", e=64)
            t_hn[2 + half] = head_norm2(src, 2, 8, gb[:, 2, :], 0.125, tA1, t_tok[2])

        t_tok = {}

        def token_items(n_cols, c0, evac, first=True):
            items, state = [], {}
            step = 2
            for kk in range(0, 8, step):
                def get(kk=kk):
                    if first and kk == 0:
                        token_items.w = W.get(A)
                    return token_items.w[:, kk:kk + step, c0:c0 + n_cols]

                def use(out, kk=kk):
                    if kk == 0:
                        state["b"] = [banks.take() for _ in range(4)]
                    for i in range(4):
                        bk, key = state["b"][i]
                        for k in range(step):
                            for j, (a, b) in enumerate(((0, 0), (0, 1), (1, 0))):
                                f = lambda e: e.matmul(bk[:, 0:n_cols], hR[:, a, kk + k, 128 * i:128 * i + 128],
                                                       out[b][:, k, :], start=(kk + k + j == 0),
                                                       stop=(kk + k == 7 and j == 2))
                                tk = PE(f) if k == step - 1 and j == 2 else f(nc.tensor)
                        if kk + step == 8:
                            evac(i, bk, key, tk)
                items.append((get, kk + step == 8, use))
            return items

        t_raw = []

        def raw_items():
            items = []
            for v in range(2):
                def get(v=v):
                    if v == 0:
                        token_items.w = W.get(A)
                    return token_items.w[:, :, 128 * v:128 * v + 128]

                def use(out, v=v):
                    bk, key = banks.take()
                    tk = products(bk, lambda a, k: out[a][:, k, :], lambda b, k: hR[:, b, k, :], range(8),
                                  ready=t_h3)
                    t = V(lambda e: e.tensor_tensor(kcv[:, v, :], bk, cN, ALU.mult), tk)
                    banks.free(key, t)
                    t_raw.append(t)
                    if v == 0:
                        x3_and_columns()
                items.append((get, False, use))
            return items

        def to_ksw(i, bk, key, tk):
            t_tok[0] = A(lambda e: e.activation(ksw[:, i, :], bk[:, 0:256], ACT.Copy, scale=cT[:, i:i + 1]), tk)
            banks.free(key, t_tok[0])

        def to_q2(i, bk, key, tk):
            if i == 0:
                second_loads()
            t_tok[2] = A(lambda e: e.activation(q2[:, i, :].rearrange("p (j g e) -> p g j e", g=2, e=64),
                                                 bk.rearrange("p (g j e) -> p g j e", g=2, e=64), ACT.Copy,
                                                 scale=cT[:, i:i + 1]), tk)
            banks.free(key, t_tok[2])

        def to_kww(i, bk, key, tk):
            t_tok[1] = A(lambda e: e.activation(kww[:, i, :], bk[:, 0:256], ACT.Copy, scale=cT[:, i:i + 1]), tk)
            banks.free(key, A(lambda e: e.activation(gat[:, i, :], bk[:, 256:280], ACT.Sigmoid, scale=cT[:, i:i + 1])))

        def conv(c, bk, key, tk):
            V(lambda e: e.tensor_tensor(uh[:, c, 2:514], uh[:, c, 2:514], bk, ALU.mult), tk, t_uh[c])
            banks.free(key, V.last)
            V(lambda e: e.tensor_tensor(uh[:, c, 2:514], uh[:, c, 2:514], cN, ALU.mult))
            for tap in range(3):
                w1 = colB[:, 16 + 4 * tap + c:17 + 4 * tap + c]
                if tap == 0:
                    V(lambda e: e.tensor_scalar(vc[:, c, :], uh[:, c, 0:512], w1, None, ALU.mult))
                else:
                    V(lambda e: e.scalar_tensor_tensor(vc[:, c, :], uh[:, c, tap:tap + 512], w1, vc[:, c, :],
                                                       ALU.mult, ALU.add))

        t_uh = {}

        def conv_items(c, bk, key, tk):
            if c in (0, 1):
                norm_keys(c)
            if c in (8, 9):
                norm_queries(c - 8)
            if c == 8:
                t_kz2[0] = G(lambda e: e.memset(kz2[:, :, :, :], 0.0), V.last)
            if c < 4:
                t_uh[c] = V(lambda e: e.tensor_tensor(uh[:, c, 2:514], bk, cN, ALU.mult), tk)
                banks.free(key, t_uh[c])
            elif c < 8:
                conv(c - 4, bk, key, tk)
            else:
                banks.free(key, V(lambda e: e.tensor_tensor(vc[:, c - 8, :], vc[:, c - 8, :], bk, ALU.mult), tk))
                V(lambda e: e.tensor_tensor(vc[:, c - 8, :], vc[:, c - 8, :], cN, ALU.mult))

        V(lambda e: e.memset(uh[:, :, 0:2], 0.0), t_moe)
        run(parts, raw_items() + token_items(256, 256, to_ksw, False) + token_items(512, 0, to_q2)
            + token_items(280, 0, to_kww) + column_items([4, 4, 4], 8, h2, conv_items), token_factors)
        t_gat = t_ksw = A.last
        t_kcv = t_raw[1]
        t_vc = V.last
        rctx.close()
        handover()
        dyn = sb("dyn3", [128, ND - 5216], at=phase)
        b2 = Region(dyn, 0, ND - 5216)
        q2T = sb("q2T", [128, 4, 512], at=b2)
        hdn = sb("hdn", [128, 2, 256], at=b2)
        hdk = sb("hdk", [128, 256], at=b2)
        kcm = sb("kcm", [32, 2, 128], at=b2)
        kcz = sb("kcz", [128, 2, 32], at=b2)
        tA = sb("tA2", [128, 128], at=b2)
        p2 = sb("p2", [128, 4, 2, 512], at=b2)
        st2 = sb("st2", [128, 6, 3, 2], at=b2)
        cst = sb("cst", [128, 3, 8], at=b2)
        on = sb("on", [128, 1], at=b2)
        blkT = sb("blkT", [128, 16, 2, 2, 32], at=Region(dyn, b2.at, ND - 5216))
        p2T = sb("p2T", [128, 2, 2, 512], at=b2)
        cp = sb("cp", [128, 8, 32], at=b2)
        cpT = sb("cpT", [32, 8, 128], at=b2)
        o2 = sb("o2", [128, 2, 512], at=b2)
        o2n = sb("o2n", [128, 512], at=b2)
        t_kcz0 = G(lambda e: e.memset(kcz[:, :, :], 0.0))
        for v in range(2):
            for g in range(2):
                base_ap = shA[:, 2 * v + g, :].rearrange("p (i l) -> p i l", l=16)
                for half in range(2):
                    src = base_ap[:, half:half + 31, :].rearrange("p i (l u) -> p l u i", u=2)[:, :, 0, :]
                    dstv = blkT[:, 8 * half:8 * half + 8, v, g, 0:31]
                    pe = colB[:, 32 + 16 * v + 8 * half:40 + 16 * v + 8 * half].unsqueeze(2).broadcast_to([128, 8, 31])
                    V(lambda e: e.tensor_tensor(dstv, src, pe, ALU.add), (s_sh, 128))
        t_blk = V(lambda e: e.memset(blkT[:, :, :, :, 31:32], 0.0))
        PE.wait(t_hn[2], t_hn[3])
        for i in range(4):
            bk, key = banks.take()
            for j in range(4):
                mm = lambda e: transpose(bk[:, 128 * j:128 * j + 128], q2[:, i, 128 * j:128 * j + 128])
                tk = PE(mm) if j == 3 else mm(nc.tensor)
            t_q2T = A(lambda e: e.copy(q2T[:, :, 128 * i:128 * i + 128], bk.rearrange("p (j q) -> p j q", j=4)), tk)
            banks.free(key, t_q2T)
        for v, src_t in enumerate((ksw, kww)):
            bk, key = banks.take()
            PE.wait(t_hn[v])
            for i in range(4):
                mm = lambda e: transpose(bk[:, 128 * i:128 * i + 128], src_t[:, i, 0:128])
                tk = PE(mm) if i == 3 else mm(nc.tensor)
            for g in range(2):
                gs = slice(64 * g, 64 * g + 64)
                t_kz = A(lambda e: e.copy(kz2[gs, g, v, :], bk[gs, :]), tk, t_kz2[0])
            banks.free(key, t_kz)
        PE.wait(t_blk)
        wv = [W.get(), W.get()]
        bh, key_h = banks.take()
        for l in range(16):
            for v in range(2):
                vs = slice(64 * v, 64 * v + 64)
                f = lambda e: e.matmul(bh[vs, 0:256], blkT[:, l, v].rearrange("p g i -> p (g i)"), wv[v][:, l, :],
                                       start=(l == 0), stop=(l == 15))
                t_blk_read = PE(f) if l == 15 else f(nc.tensor)
        W.done()
        t_hdk = A(lambda e: e.copy(hdk[:, :], bh[:, 0:256]), t_blk_read)
        banks.free(key_h, t_hdk)
        A.wait(t_blk_read)

        def mix_conv():
            column_norm(vc, 4, sq, rinv[:, :], t_vc)
            for c in range(4):
                V(lambda e: e.scalar_tensor_tensor(mixT[:, 4 + c, :], vc[:, c, :], colA[:, 52 + c:53 + c],
                                                   rinv[:, :], ALU.mult, ALU.mult))

        def compress1():
            bk, key = banks.take()
            PE.wait(t_hdk)
            for hh in range(2):
                tk = PE(lambda e: transpose(bk[:, 128 * hh:128 * hh + 128], hdk[:, 128 * hh:128 * hh + 128]))
            for hh in range(2):
                for v in range(2):
                    o = 128 * hh + 64 * v
                    t = A(lambda e: e.activation(hdn[:, hh, 64 * v:64 * v + 64], bk[:, o:o + 64], ACT.Gelu_apprx_tanh,
                                                 bias=colB[:, 28 + 2 * v + hh:29 + 2 * v + hh]), tk)
            banks.free(key, t)
            return t

        def compress2(t_hd):
            PE.wait(t_hd, (s_k2, 64))
            for v in range(2):
                bk, key = banks.take()
                for g in range(2):
                    o = 64 * v + 32 * g
                    tk = proj(bk[0:32, 64 * g:64 * g + 64], [(hdn[:, hh, o:o + 32], wc2[:, v, hh, :]) for hh in range(2)])
                t = V(lambda e: e.tensor_tensor(kcm[:, v, :].rearrange("p (g e) -> p g e", g=2),
                                                bk[0:32, 0:128].rearrange("p (g e) -> p g e", g=2),
                                                gb[0:32, 6 + v, :].unsqueeze(1).broadcast_to([32, 2, 64]), ALU.add), tk)
                banks.free(key, t)
            return head_norm2(kcm[:, 0, :].rearrange("p (t h e) -> p t h e", t=1, e=64), 1, 2, gb[0:32, 3, :], 1.0, tA, P=32)

        def compress3(t_kcm):
            bk, key = banks.take()
            tk = PE(lambda e: transpose(bk[:, 0:32], kcm[:, 0, :], 32), t_kcm)
            for g in range(2):
                gs = slice(64 * g, 64 * g + 64)
                t = A(lambda e: e.copy(kcz[gs, g, :], bk[gs, 0:32]), tk, t_kcz0)
            banks.free(key, t)
            PE.wait(t)

        V.wait((s_k2, 64))
        PE.wait(t_q2T, t_kz)
        rel_p, rel_pT, e_done, t_pT = {}, {}, {}, {}
        its = [(i, h) for i in range(3, -1, -1) for h in range(8)]
        rel_cp, rel_cpT, rel_on, rel_o2 = None, None, None, {}

        def cmp_part(i):
            nonlocal rel_cp, rel_cpT
            bk, key = banks.take(2)
            for h in range(8):
                j, g = h % 4, h // 4
                tk = PE(lambda e: e.matmul(bk[:, 512 * g + 32 * j:512 * g + 32 * j + 32],
                                           q2T[:, j, 128 * i:128 * i + 128], kcz[:, g, :], start=True, stop=True))
            V.wait(rel_cp)
            V(lambda e: e.tensor_tensor(cp[:, :, :].rearrange("p (g j) s -> p g j s", g=2),
                                        bk.rearrange("p (g j s) -> p g j s", g=2, s=32)[:, :, 0:4, :],
                                        cb[:, i].rearrange("p (g j) s -> p g j s", g=2), ALU.add), tk)
            banks.free(key, V.last)
            V(lambda e: e.tensor_reduce(cst[:, 0, :], cp[:, :, 0:31], AX, ALU.max))
            t = V(lambda e: e.tensor_tensor(cp[:, :, :], cp[:, :, :], cst[:, 0, :].unsqueeze(2).broadcast_to([128, 8, 32]),
                                            ALU.subtract))
            t = A(lambda e: e.activation(cp[:, :, 0:31], cp[:, :, 0:31], ACT.Exp), t)
            V(lambda e: e.tensor_tensor(cp[:, :, :], cp[:, :, :], cmk[:, i, :].unsqueeze(1).broadcast_to([128, 8, 32]),
                                        ALU.mult), t)
            V(lambda e: e.tensor_reduce(cst[:, 1, :], cp[:, :, 0:31], AX, ALU.add))
            V(lambda e: e.tensor_scalar(cst[:, 1, :], cst[:, 1, :], 1e-30, None, ALU.max))
            V(lambda e: e.reciprocal(cst[:, 1, :], cst[:, 1, :]))
            V(lambda e: e.tensor_tensor(cst[:, 2, :], cst[:, 1, :], gat[:, i, 0:24:3], ALU.mult), t_gat)
            t = V(lambda e: e.tensor_tensor(cp[:, :, :], cp[:, :, :], cst[:, 2, :].unsqueeze(2).broadcast_to([128, 8, 32]),
                                            ALU.mult))
            yield
            bk, key = banks.take(2)
            PE.wait(t)
            for h in range(8):
                tk = PE(lambda e: transpose(bk[0:32, 128 * h:128 * h + 128], cp[:, h, :]))
            rel_cp = tk
            t = V(lambda e: e.tensor_copy(cpT[:, :, :], bk[0:32, :].rearrange("p (h q) -> p h q", h=8)), tk, rel_cpT)
            banks.free(key, t)
            yield
            bk, key = banks.take()
            PE.wait(t)
            for h in range(8):
                g = h // 4
                tk = PE(lambda e: e.matmul(bk[:, 64 * h:64 * h + 64], cpT[0:31, h, :], kcm[0:31, 1, 64 * g:64 * g + 64],
                                           start=True, stop=True))
            rel_cpT = tk
            t_o2[i] = A(lambda e: e.copy(o2[:, i % 2, :], bk), tk, rel_o2.get(i + 2))
            banks.free(key, t_o2[i])

        def scores2(n):
            i, h = its[n]
            s, nk = n % 4, 128 * (i + 1)
            slope = float(np.float32(2.0 ** -(h + 1)))
            for v in range(2):
                bk, key = banks.take()
                tk = PE(lambda e: e.matmul(bk[:, 0:nk], q2T[:, h % 4, 128 * i:128 * i + 128], kz2[:, h // 4, v, 0:nk],
                                           start=True, stop=True))
                t = V(lambda e: e.scalar_tensor_tensor(p2[:, s, v, 0:nk], dist[:, 512 - nk:512], slope, bk[:, 0:nk],
                                                       ALU.mult, ALU.add), tk, rel_p.get(n - 4))
                banks.free(key, t)
            t = V(lambda e: e.tensor_reduce(st2[:, n % 6, 0, :], p2[:, s, :, 0:nk], AX, ALU.max, negate=True))
            for v in range(2):
                e_done[n] = A(lambda e: e.activation(p2[:, s, v, 0:nk], p2[:, s, v, 0:nk], ACT.Exp,
                                                     bias=st2[:, n % 6, 0, v:v + 1],
                                                     accum_out=st2[:, n % 6, 1, v:v + 1]), t)

        def turn2(n):
            i, h = its[n]
            s, nk = n % 4, 128 * (i + 1)
            PE.wait(e_done[n])
            for v in range(2):
                bk, key = banks.take()
                for c in range(i + 1):
                    mm = lambda e: transpose(bk[:, 128 * c:128 * c + 128], p2[:, s, v, 128 * c:128 * c + 128])
                    tk = PE(mm) if c == i else mm(nc.tensor)
                t_pT[n] = A(lambda e: e.copy(p2T[:, n % 2, v, 0:nk], bk[:, 0:nk]), tk, rel_pT.get(n - 2))
                banks.free(key, t_pT[n])
            rel_p[n] = tk

        def values2(n, t_o2):
            nonlocal rel_on
            i, h = its[n]
            g, s = h // 4, n % 2
            bo, ko = banks.take()
            PE.wait(t_pT[n])
            for v, vt in enumerate((ksw, kww)):
                tk = proj(bo[:, 128 * v:128 * v + 128], [(p2T[:, n % 2, v, 128 * c:128 * c + 128], vt[:, c, 128:256])
                                                         for c in range(i + 1)])
            rel_pT[n] = tk
            r2 = st2[:, n % 6, 2, :]
            V(lambda e: e.reciprocal(r2, st2[:, n % 6, 1, :]), e_done[n])
            V(lambda e: e.tensor_tensor(r2, r2, gat[:, i, 3 * h + 1:3 * h + 3], ALU.mult))
            oh = o2[:, i % 2, 64 * h:64 * h + 64]
            for v in range(2):
                t = V(lambda e: e.scalar_tensor_tensor(oh, bo[:, 128 * v + 64 * g:128 * v + 64 * g + 64], r2[:, v:v + 1],
                                                       oh, ALU.mult, ALU.add), tk, t_o2)
            banks.free(ko, t)
            if h == 7:
                oi = o2[:, i % 2, :]
                V.wait(rel_on)
                V(lambda e: e.tensor_tensor(o2n[:, :], oi, oi, ALU.mult))
                V(lambda e: e.tensor_reduce(on[:, :], o2n[:, :], AX, ALU.add))
                inv_root(on[:, :], on[:, :], 1.0 / 512)
                t = V(lambda e: e.tensor_scalar(o2n[:, :], oi, on[:, :], None, ALU.mult))
                rel_o2[i] = t
                turned.append((i, t))

        def turn_out(i, t):
            nonlocal rel_on
            bt, kt_ = banks.take()
            PE.wait(t)
            for k in range(4):
                mm = lambda e: transpose(bt[:, 128 * k:128 * k + 128], o2n[:, 128 * k:128 * k + 128])
                rel_on = PE(mm) if k == 3 else mm(nc.tensor)
            t = V(lambda e: e.tensor_tensor(mixT[:, 0:4, 128 * i:128 * i + 128],
                                            bt.rearrange("p (k q) -> p k q", k=4),
                                            colA[:, 48:52].unsqueeze(2).broadcast_to([128, 4, 128]), ALU.mult), rel_on)
            banks.free(kt_, t)

        t_o2, turned, cmp_steps = {}, [], None
        t_hd = compress1()
        for n in range(36):
            if n < 32:
                scores2(n)
            if n == 0:
                t_kcm = compress2(t_hd)
            if n == 1:
                compress3(t_kcm)
                V.wait(t_blk_read)
            if n == 6:
                mix_conv()
            if turned:
                turn_out(*turned.pop(0))
            if n == 1 or n % 8 == 0 and 0 < n < 32:
                cmp_steps = cmp_part(its[n][0])
                next(cmp_steps)
            if n == 2 or n % 8 == 1 and 1 < n < 32:
                next(cmp_steps)
            if n % 8 == 2 and n < 32:
                next(cmp_steps, None)
            if 2 <= n < 34:
                turn2(n - 2)
            if 3 <= n < 35:
                values2(n - 3, t_o2[its[n - 3][0]])
        phase.close()
        hctx.close()
        handover()
        phase = ExitStack()
        hR = sb("hR3", [128, 2, 8, 512], F32R, at=phase)
        wR = sb("wR3", [128, 2, 2, 1024], F32R, at=phase)
        xR = sb("xR3", [128, 2, 8, 512], F32R, at=phase)
        tmp = sb("tmp3", [128, 4, 512], at=phase)
        parts = Parts(wR)
        h2 = (hR[:, 0], hR[:, 1])
        t_mR = []
        banks.hi, banks.at = 7, 0
        total = Squares(8, one_mat, Banks(7, 8))

        def add_o(n, bk, key, tk):
            t = V(lambda e: e.tensor_tensor(xT[:, n, :], xT[:, n, :], bk, ALU.add), tk)
            banks.free(key, t)
            total.add(n, xT[:, n, :], t)
            t_h4.append(split_scaled((xR[:, 0, n], xR[:, 1, n]), xT[:, n, :], colA[:, 56 + n:57 + n], t))

        t_h4 = []
        run(parts, column_items([4, 4], 8, h2, add_o, t_mR), lambda: t_mR.extend(
            split((hR[:, 0, k], hR[:, 1, k]), mixT[:, k, :]) for k in range(8)))
        t_x4 = V.last
        root(rinv[:, :], total)
        banks.hi = 8
        xo = mixT[:, :, :].rearrange("p (i q) n -> p i q n", q=2)
        for i in range(4):
            for q in range(2):
                bk, key = banks.take()
                PE.wait(t_x4)
                for k in range(4):
                    mm = lambda e: transpose(bk[:, 128 * k:128 * k + 128], xT[:, 4 * q + k, 128 * i:128 * i + 128])
                    tk = PE(mm) if k == 3 else mm(nc.tensor)
                t_xo = A(lambda e: e.copy(xo[:, i, q, :], bk), tk)
                banks.free(key, t_xo)
        rel_u = [PE.last, PE.last]
        uR = hR[:, :, :, :].rearrange("p x (s k) t -> p s x k t", s=2)
        h4 = (xR[:, 0], xR[:, 1])
        t_u = {}

        def up_items(r):
            def evac(j, bk, key, tk):
                m = tmp[:, j % 4, :]
                t = V(lambda e: e.scalar_tensor_tensor(m, bk, 0.0, rinv[:, :], ALU.max, ALU.mult), tk,
                      t_u.get(("tmp", j % 4)))
                banks.free(key, t)
                t = G(lambda e: e.tensor_tensor(m, m, m, ALU.mult), t)
                t_u[r] = t_u[("tmp", j % 4)] = split((uR[:, r % 2, 0, j], uR[:, r % 2, 1, j]), m, t, rel_u[r % 2])
            return column_items([4], 8, h4, evac, t_h4 if r == 0 else None)

        def down_items(r):
            items, state = [], {}
            for k in range(4):
                def get(k=k):
                    if k == 0:
                        state["w"] = W.get(A)
                    return state["w"][:, k:k + 1, :]

                def use(out, k=k):
                    if k == 0:
                        PE.wait(t_u[r])
                        state["b"] = [banks.take() for _ in range(8)]
                    for b in range(8):
                        i, q = b // 2, b % 2
                        bk, key = state["b"][b]
                        for n, (x, y) in enumerate(((0, 0), (0, 1), (1, 0))):
                            f = lambda e: e.matmul(bk, uR[:, r % 2, x, k, 128 * i:128 * i + 128],
                                                   out[y][:, 0, 512 * q:512 * q + 512],
                                                   start=(k == 0 and n == 0), stop=(k == 3 and n == 2))
                            tk = PE(f) if n == 2 else f(nc.tensor)
                        if k == 3:
                            rel_u[r % 2] = tk
                            state["t"] = V(lambda e: e.tensor_tensor(xo[:, i, q, :], xo[:, i, q, :], bk, ALU.add),
                                           tk, t_xo)
                            banks.free(key, state["t"])
                items.append((get, k == 3, use))
            return items

        items = up_items(0)
        for r in range(1, 8):
            items += up_items(r) + down_items(r - 1)
        run(parts, items + down_items(7))
        t = V.last
        s_out = sem("s_out")
        SP.wait(t)
        nc.sync.dma_start(out.rearrange("(i p) n -> p i n", p=128),
                          mixT[:, :, :].rearrange("p (i q) n -> p i (q n)", q=2)).then_inc(s_out, 16)
        SP.wait((s_out, 16))
        phase.close()


def constants():
    c = {}
    c["k_ident"] = np.eye(128, dtype=np.float32)
    s, t = np.meshgrid(np.arange(128), np.arange(128), indexing="ij")
    m = np.zeros((128, 14, 128), np.float32)
    for i, h in enumerate(LEVELS):
        same = (s // (2 * h)) == (t // (2 * h))
        m[:, i] = same & (s % (2 * h) < h) & (t % (2 * h) >= h)
        m[:, 7 + i] = same & (s % (2 * h) >= h) & (t % (2 * h) < h)
    c["k_masks"] = m
    inv = np.float32(10000.0) ** (-np.arange(0, 32, 2, dtype=np.float32) / np.float32(32))
    tt = np.arange(512)
    ang = np.stack([(tt // 64).astype(np.float32)[:, None] * inv, (tt % 64).astype(np.float32)[:, None] * inv], 1)
    co, si = np.cos(ang), np.sin(ang)
    cs = np.concatenate([co, co], -1).reshape(512, 64)
    sn = np.concatenate([-si, si], -1).reshape(512, 64)
    c["k_rope"] = np.ascontiguousarray(np.stack([cs, sn], 1).reshape(4, 128, 2, 64).transpose(1, 0, 2, 3)).astype(np.float32)
    c["k_iota"] = np.arange(512, dtype=np.float32)
    q, j = np.meshgrid(np.arange(128), np.arange(512), indexing="ij")
    dd = (q + 384 - j).astype(np.float32)
    c["k_dist"] = np.where(dd >= 0, -dd, np.float32(-1e33)).astype(np.float32)
    t4 = (np.arange(4)[None, :, None] * 128 + np.arange(128)[:, None, None]).astype(np.float32)
    dc = t4 - (16 * np.arange(32)[None, None, :] + 31).astype(np.float32)
    dc[:, :, 31] = -1
    slope = np.power(np.float32(2.0), -np.arange(1, 9, dtype=np.float32))
    cb = np.where(dc[:, :, None, :] >= 0, -slope[None, None, :, None] * dc[:, :, None, :], np.float32(-1e30))
    c["k_cb"] = np.ascontiguousarray(cb).astype(np.float32)
    c["k_cm"] = np.ascontiguousarray(dc >= 0).astype(np.float32)
    return c


_FLAT = ["c", "c_ctx", "b_mod", "norm1_g", "norm2_g", "hg_lb_logits", "hg_norm_g", "q_norm_g", "k_norm_g",
         "final_norm_g", "g_mix_norm_2", "g_q_2", "g_k_2", "pe_cmp_2", "b_cmp1_2", "b_cmp2_2", "conv_w_2", "g_out_2",
         "g_ffn_norm_2"]
_FIRST = ["x", "ctx", "w_mod", "w_in", "w_branch_a", "w_branch_b", "w_out", "w_router", "w_exp_gate", "w_exp_up",
          "w_exp_down", "w_in_2", "w_cmp1_2", "w_cmp2_2", "w_o_2", "w_up_2", "w_down_2"]


def kernel(**inputs):
    import concourse.bacc as _bacc
    from concourse.bass_utils import run_bass_kernel_spmd as _run

    nc = _bacc.Bacc("TRN2", target_bir_lowering=False, num_devices=1)
    arrays = {}
    for name in _FLAT:
        arrays[name] = np.ascontiguousarray(inputs[name]).reshape(-1)
    for name in _FIRST:
        a = np.ascontiguousarray(inputs[name])
        arrays[name] = a.reshape(a.shape[1:]) if a.shape[0] == 1 else a
    arrays.update(constants())
    d, sent = {}, {}
    for name, a in arrays.items():
        sent[f"in_{name}_dram"] = a
        d[name] = nc.dram_tensor(f"in_{name}_dram", a.shape, mybir.dt.from_np(a.dtype), kind="ExternalInput").ap()
    out = nc.dram_tensor("out_0_dram", (512, 1024), F32, kind="ExternalOutput").ap()
    program(nc, d, out)
    r = _run(nc, [sent], core_ids=[0])
    return np.asarray(r.results[0]["out_0_dram"]).reshape(1, 512, 1024)
```
